# Optimizing a Trainium2 kernel written in Bass

```python
import jax
import jax.numpy as jnp
from jax import lax
import numpy as np
import jax, jax.numpy as jnp

D_MODEL = 1024
BATCH = 1
SEQ = 512
DEPTH = 2

CTX_LEN = 256
GRID_W = 64
N_MOD = 6
RMS_EPS = 1e-6
NEG_INF = -1e30
D_POOL = D_MODEL // 2
POOL_WINDOWS = (2, 4, 8, 16)
D_POOL_GROUP = D_POOL // len(POOL_WINDOWS)
NA_HEAD_DIM = 64
D_NA = D_MODEL - D_POOL
NA_HEADS = D_NA // NA_HEAD_DIM
WIN_R = 8
WIN_C = 16
D_IN_EVEN = D_POOL + 3 * D_NA
RW_HEAD = 64
RW_HEADS = D_MODEL // RW_HEAD
DECAY_LORA = 64
AAA_LORA = 64
GATE_LORA = 128
GN_EPS = 64e-5
D_FF = 4 * D_MODEL


def rms_norm(x, g):
    xf = x.astype(jnp.float32)
    y = xf * lax.rsqrt(jnp.mean(xf * xf, axis=-1, keepdims=True) + RMS_EPS)
    return (y * g.astype(jnp.float32)).astype(x.dtype)

def modulate(h, shift, scale):
    return h * (1 + scale) + shift

def squared_relu_mlp(h, w1, w2):
    return jnp.square(jax.nn.relu(h @ w1)) @ w2

def split_heads(t, n_heads, head_dim):
    return t.reshape(t.shape[0], t.shape[1], n_heads, head_dim)

def pool_mixer(u, pool_w, pool_scale):
    L = u.shape[1]
    uf = u.astype(jnp.float32)
    cs = jnp.concatenate([jnp.zeros_like(uf[:, :1]), jnp.cumsum(uf, axis=1)], axis=1)
    t = jnp.arange(L)
    outs = []
    for gi, w in enumerate(POOL_WINDOWS):
        lo = jnp.clip(t - w // 2, 0, L)
        hi = jnp.clip(t + w // 2, 0, L)
        sl = slice(gi * D_POOL_GROUP, (gi + 1) * D_POOL_GROUP)
        csg = cs[..., sl]
        mean = (jnp.take(csg, hi, axis=1) - jnp.take(csg, lo, axis=1)) / (hi - lo).astype(jnp.float32)[None, :, None]
        outs.append((mean - uf[..., sl]).astype(u.dtype) @ pool_w[gi])
    return jnp.concatenate(outs, axis=-1) * pool_scale

def context_attention(q, k, v):
    B, L = q.shape[:2]
    s = jnp.einsum('bqhd,bkhd->bhqk', q, k).astype(jnp.float32) * (NA_HEAD_DIM ** -0.5)
    p = jax.nn.softmax(s, axis=-1).astype(v.dtype)
    return jnp.einsum('bhqk,bkhd->bqhd', p, v).reshape(B, L, D_NA)

def neighbourhood_attention(q, k, v, k_ctx, v_ctx, rpb):
    B, L = q.shape[:2]
    rows = L // GRID_W
    kr = min(WIN_R, rows)
    scale = NA_HEAD_DIM ** -0.5
    grid = lambda t: t.reshape(B, rows, GRID_W, NA_HEADS, NA_HEAD_DIM)
    qg, kg, vg = grid(q), grid(k), grid(v)
    col = jnp.arange(GRID_W)
    c_start = jnp.clip(col - WIN_C // 2, 0, GRID_W - WIN_C)
    col_ok = (col[None, :] >= c_start[:, None]) & (col[None, :] < c_start[:, None] + WIN_C)
    dc_idx = jnp.clip(col[None, :] - col[:, None], -(WIN_C - 1), WIN_C - 1) + WIN_C - 1
    rpb_c = rpb.astype(jnp.float32)[:, :, dc_idx]

    def row_block(args):
        q_row, r = args
        start = jnp.clip(r - kr // 2, 0, rows - kr)
        k_band = lax.dynamic_slice_in_dim(kg, start, kr, axis=1)
        v_band = lax.dynamic_slice_in_dim(vg, start, kr, axis=1)
        s_lat = jnp.einsum('bqhd,brkhd->bhqrk', q_row, k_band).astype(jnp.float32) * scale
        dr_idx = start + jnp.arange(kr) - r + WIN_R - 1
        bias = jnp.take(rpb_c, dr_idx, axis=1).transpose(0, 2, 1, 3)
        s_lat = jnp.where(col_ok[:, None, :], s_lat + bias, NEG_INF)
        s_ctx = jnp.einsum('bqhd,bchd->bhqc', q_row, k_ctx).astype(jnp.float32) * scale
        s = jnp.concatenate([s_lat.reshape(B, NA_HEADS, GRID_W, kr * GRID_W), s_ctx], axis=-1)
        p = jax.nn.softmax(s, axis=-1).astype(v.dtype)
        p_lat = p[..., :kr * GRID_W].reshape(B, NA_HEADS, GRID_W, kr, GRID_W)
        p_ctx = p[..., kr * GRID_W:]
        return (jnp.einsum('bhqrk,brkhd->bqhd', p_lat, v_band)
                + jnp.einsum('bhqc,bchd->bqhd', p_ctx, v_ctx))

    out = lax.map(row_block, (jnp.moveaxis(qg, 1, 0), jnp.arange(rows)))
    return jnp.moveaxis(out, 0, 1).reshape(B, L, D_NA)

def even_mixer(h, hc, w_in, w_out, pool_w, pool_scale, rpb, with_ctx):
    heads = lambda t: split_heads(t, NA_HEADS, NA_HEAD_DIM)
    u = h @ w_in
    q = heads(u[..., D_POOL:D_POOL + D_NA])
    k = heads(u[..., D_POOL + D_NA:D_POOL + 2 * D_NA])
    v = heads(u[..., D_POOL + 2 * D_NA:])
    if with_ctx:
        uc = hc @ w_in
        kv_c = uc[..., D_POOL + D_NA:]
    else:
        kv_c = hc @ w_in[:, D_POOL + D_NA:]
    k_c, v_c = heads(kv_c[..., :D_NA]), heads(kv_c[..., D_NA:])
    y = jnp.concatenate([pool_mixer(u[..., :D_POOL], pool_w, pool_scale),
                         neighbourhood_attention(q, k, v, k_c, v_c, rpb)], axis=-1) @ w_out
    if with_ctx:
        yc = jnp.concatenate([pool_mixer(uc[..., :D_POOL], pool_w, pool_scale),
                              context_attention(heads(uc[..., D_POOL:D_POOL + D_NA]), k_c, v_c)], axis=-1) @ w_out
    else:
        yc = None
    return y, yc

def centred_shift(x):
    prev = jnp.pad(x[:, :-1], ((0, 0), (1, 0), (0, 0)))
    nxt = jnp.pad(x[:, 1:], ((0, 0), (0, 1), (0, 0)))
    return 0.5 * (prev + nxt) - x

def rwkv_features(h, mu, wr, wk, wv, w0, w1, w2, a0, a1, a2, g1, g2, k_k, k_a, with_rg):
    B, L, _ = h.shape
    heads = lambda t: split_heads(t, RW_HEADS, RW_HEAD).astype(jnp.float32)
    xx = centred_shift(h)
    mix = lambda j: h + xx * mu[j]
    xw, xk, xv, xa = mix(1), mix(2), mix(3), mix(4)
    k = xk @ wk
    v = heads(xv @ wv)
    kk = heads(k * k_k)
    kk = kk * lax.rsqrt(jnp.maximum(jnp.sum(kk * kk, axis=-1, keepdims=True), 1e-24))
    kh = heads(k)
    k_a_h = k_a.reshape(RW_HEADS, RW_HEAD).astype(jnp.float32)
    dirs = []
    for d in range(2):
        w_raw = heads(w0[d] + jnp.tanh(xw @ w1[d]) @ w2[d])
        decay = jnp.exp(-jnp.exp(-jax.nn.softplus(-w_raw) - 0.5))
        a = jax.nn.sigmoid(heads(a0[d] + (xa @ a1[d]) @ a2[d]))
        k_d = kh * (1 + (a - 1) * k_a_h)
        dirs.append((decay, k_d, a))
    if with_rg:
        r = heads(mix(0) @ wr)
        g = jax.nn.sigmoid(mix(5) @ g1) @ g2
    else:
        r, g = None, None
    return v, kk, dirs, r, g

def wkv_scan(s0, decay, k, v, kk, a, r, reverse):
    tm = lambda t: jnp.moveaxis(t.astype(jnp.float32), 1, 0)
    emit = r is not None
    xs = (tm(decay), tm(k), tm(v), tm(kk), tm(kk * a)) + ((tm(r),) if emit else ())

    def step(S, inp):
        w_t, k_t, v_t, kk_t, kka_t = inp[:5]
        S = (S * w_t[:, :, None, :]
             - jnp.einsum('bhij,bhj->bhi', S, kk_t)[..., None] * kka_t[:, :, None, :]
             + v_t[..., None] * k_t[:, :, None, :])
        y = jnp.einsum('bhij,bhj->bhi', S, inp[5]) if emit else None
        return S, y

    S, ys = lax.scan(step, s0, xs, reverse=reverse)
    return S, (jnp.moveaxis(ys, 0, 1) if emit else None)

def rwkv_readout(y, r, k_sum, v, g, r_k, ln_g, ln_b, wo, dtype):
    B, L = y.shape[:2]
    mean = jnp.mean(y, axis=-1, keepdims=True)
    var = jnp.mean(jnp.square(y - mean), axis=-1, keepdims=True)
    yn = ((y - mean) * lax.rsqrt(var + GN_EPS)).reshape(B, L, D_MODEL) * ln_g + ln_b
    bonus = (jnp.sum(r * k_sum * r_k.astype(jnp.float32), axis=-1, keepdims=True) * v).reshape(B, L, D_MODEL)
    return ((yn + bonus) * g).astype(dtype) @ wo

def odd_mixer(h, hc, mu, wr, wk, wv, wo, w0, w1, w2, a0, a1, a2, g1, g2, k_k, k_a, r_k, ln_g, ln_b, with_ctx):
    feat = lambda t, rg: rwkv_features(t, mu, wr, wk, wv, w0, w1, w2, a0, a1, a2, g1, g2, k_k, k_a, rg)
    v, kk, dirs, r, g = feat(h, True)
    v_c, kk_c, dirs_c, r_c, g_c = feat(hc, with_ctx)
    s0 = jnp.zeros((h.shape[0], RW_HEADS, RW_HEAD, RW_HEAD), jnp.float32)
    ys, ys_c = [], []
    for d, reverse in enumerate((False, True)):
        decay_c, k_dc, a_c = dirs_c[d]
        s_ctx, y_c = wkv_scan(s0, decay_c, k_dc, v_c, kk_c, a_c, r_c, reverse)
        decay, k_d, a = dirs[d]
        _, y_d = wkv_scan(s_ctx, decay, k_d, v, kk, a, r, reverse)
        ys.append(y_d)
        ys_c.append(y_c)
    y = rwkv_readout(ys[0] + ys[1], r, dirs[0][1] + dirs[1][1], v, g, r_k, ln_g, ln_b, wo, h.dtype)
    if with_ctx:
        yc = rwkv_readout(ys_c[0] + ys_c[1], r_c, dirs_c[0][1] + dirs_c[1][1], v_c, g_c, r_k, ln_g, ln_b, wo, hc.dtype)
    else:
        yc = None
    return y, yc

def first_inputs(seed: int = 0) -> dict:
    key = jax.random.key(seed)
    ks = iter(jax.random.split(key, 40))
    n_even = (DEPTH + 1) // 2
    n_odd = DEPTH // 2
    D = D_MODEL
    nrm = lambda shape, s: jax.random.normal(next(ks), shape, jnp.float32) * s
    return {
        "x": nrm((BATCH, SEQ, D), 1.0),
        "c": nrm((BATCH, D), 1.0),
        "ctx": nrm((BATCH, CTX_LEN, D), 1.0),
        "c_ctx": nrm((D,), 1.0),
        "ada_w": nrm((DEPTH, D, N_MOD * D), 0.5 * D ** -0.5),
        "ada_b": nrm((DEPTH, N_MOD * D), 0.02),
        "norm_g": 1.0 + nrm((DEPTH, 4, D), 0.1),
        "mlp_w1": nrm((DEPTH, D, D_FF), D ** -0.5),
        "mlp_w2": nrm((DEPTH, D_FF, D), D_FF ** -0.5),
        "ev_w_in": nrm((n_even, D, D_IN_EVEN), D ** -0.5),
        "ev_w_out": nrm((n_even, D, D), D ** -0.5),
        "ev_pool_w": nrm((n_even, len(POOL_WINDOWS), D_POOL_GROUP, D_POOL_GROUP), D_POOL_GROUP ** -0.5),
        "ev_pool_scale": 1.0 + nrm((n_even, D_POOL), 0.1),
        "ev_rpb": nrm((n_even, NA_HEADS, 2 * WIN_R - 1, 2 * WIN_C - 1), 0.1),
        "rw_mu": jax.random.uniform(next(ks), (n_odd, 6, D), jnp.float32),
        "rw_wr": nrm((n_odd, D, D), D ** -0.5),
        "rw_wk": nrm((n_odd, D, D), D ** -0.5),
        "rw_wv": nrm((n_odd, D, D), D ** -0.5),
        "rw_wo": nrm((n_odd, D, D), D ** -0.5),
        "rw_w0": -2.0 + nrm((n_odd, 2, D), 0.5),
        "rw_w1": nrm((n_odd, 2, D, DECAY_LORA), D ** -0.5),
        "rw_w2": nrm((n_odd, 2, DECAY_LORA, D), 0.1 * DECAY_LORA ** -0.5),
        "rw_a0": nrm((n_odd, 2, D), 0.1),
        "rw_a1": nrm((n_odd, 2, D, AAA_LORA), D ** -0.5),
        "rw_a2": nrm((n_odd, 2, AAA_LORA, D), 0.1 * AAA_LORA ** -0.5),
        "rw_g1": nrm((n_odd, D, GATE_LORA), D ** -0.5),
        "rw_g2": nrm((n_odd, GATE_LORA, D), GATE_LORA ** -0.5),
        "rw_kk": 0.85 + nrm((n_odd, D), 0.05),
        "rw_ka": 1.0 + nrm((n_odd, D), 0.05),
        "rw_rk": nrm((n_odd, RW_HEADS, RW_HEAD), 0.1),
        "rw_lng": 1.0 + nrm((n_odd, D), 0.1),
        "rw_lnb": nrm((n_odd, D), 0.01),
    }

def first_block(x, c, ctx, c_ctx, ada_w, ada_b, norm_g, mlp_w1, mlp_w2,
              ev_w_in, ev_w_out, ev_pool_w, ev_pool_scale, ev_rpb,
              rw_mu, rw_wr, rw_wk, rw_wv, rw_wo, rw_w0, rw_w1, rw_w2,
              rw_a0, rw_a1, rw_a2, rw_g1, rw_g2, rw_kk, rw_ka, rw_rk, rw_lng, rw_lnb):
    silu_c = jax.nn.silu(c)
    silu_cc = jax.nn.silu(c_ctx)
    for i in range(DEPTH):
        j = i // 2
        with_ctx = i < DEPTH - 1
        mod = (silu_c @ ada_w[i] + ada_b[i])[:, None, :]
        mod_c = silu_cc @ ada_w[i] + ada_b[i]
        sh1, sc1, gt1, sh2, sc2, gt2 = jnp.split(mod, N_MOD, axis=-1)
        sh1c, sc1c, gt1c, sh2c, sc2c, gt2c = jnp.split(mod_c, N_MOD, axis=-1)
        h = modulate(rms_norm(x, norm_g[i, 0]), sh1, sc1)
        hc = modulate(rms_norm(ctx, norm_g[i, 0]), sh1c, sc1c)
        if i % 2 == 0:
            y, yc = even_mixer(h, hc, ev_w_in[j], ev_w_out[j], ev_pool_w[j], ev_pool_scale[j], ev_rpb[j], with_ctx)
        else:
            y, yc = odd_mixer(h, hc, rw_mu[j], rw_wr[j], rw_wk[j], rw_wv[j], rw_wo[j],
                              rw_w0[j], rw_w1[j], rw_w2[j], rw_a0[j], rw_a1[j], rw_a2[j],
                              rw_g1[j], rw_g2[j], rw_kk[j], rw_ka[j], rw_rk[j], rw_lng[j], rw_lnb[j], with_ctx)
        x = x + gt1 * rms_norm(y, norm_g[i, 1])
        h = modulate(rms_norm(x, norm_g[i, 2]), sh2, sc2)
        x = x + gt2 * rms_norm(squared_relu_mlp(h, mlp_w1[i], mlp_w2[i]), norm_g[i, 3])
        if with_ctx:
            ctx = ctx + gt1c * rms_norm(yc, norm_g[i, 1])
            hc = modulate(rms_norm(ctx, norm_g[i, 2]), sh2c, sc2c)
            ctx = ctx + gt2c * rms_norm(squared_relu_mlp(hc, mlp_w1[i], mlp_w2[i]), norm_g[i, 3])
    return x


MEM_LEN = 256
HEAD_DIM = 64
N_CONV_GROUPS = 6
CONV_CH = N_CONV_GROUPS * HEAD_DIM
CONV_WIDTH = 31
N_Q_HEADS = 6
N_KV_HEADS = 2
SWA_Q = N_Q_HEADS * HEAD_DIM
SWA_KV = N_KV_HEADS * HEAD_DIM
WINDOW = 128
BLOCK = 128
N_MEM_HEADS = 4
MEM_W = N_MEM_HEADS * HEAD_DIM
D_MIX = CONV_CH + SWA_Q + MEM_W
D_IN = 2 * CONV_CH + SWA_Q + 2 * SWA_KV + MEM_W
D_FF_2 = 2816
ROPE_THETA = 10000.0
EPS = 1e-6


def rms_norm_2(x, g):
    xf = x.astype(jnp.float32)
    y = xf * lax.rsqrt(jnp.mean(xf * xf, axis=-1, keepdims=True) + EPS)
    return (y * g.astype(jnp.float32)).astype(x.dtype)

def layer_norm(x, g, b):
    xf = x.astype(jnp.float32)
    mu = jnp.mean(xf, axis=-1, keepdims=True)
    var = jnp.mean(jnp.square(xf - mu), axis=-1, keepdims=True)
    y = (xf - mu) * lax.rsqrt(var + EPS)
    return (y * g.astype(jnp.float32) + b.astype(jnp.float32)).astype(x.dtype)

def swiglu(x, w1, w3, w2):
    return (jax.nn.silu(x @ w1) * (x @ w3)) @ w2

def rope_tables(positions):
    inv_freq = ROPE_THETA ** (-jnp.arange(0, HEAD_DIM, 2, dtype=jnp.float32) / HEAD_DIM)
    ang = positions.astype(jnp.float32)[..., None] * inv_freq
    return jnp.cos(ang)[:, :, None, :], jnp.sin(ang)[:, :, None, :]

def apply_rope(x, cos, sin):
    xf = x.astype(jnp.float32)
    x1, x2 = jnp.split(xf, 2, axis=-1)
    out = jnp.concatenate([x1 * cos - x2 * sin, x2 * cos + x1 * sin], axis=-1)
    return out.astype(x.dtype)

def conv_module(u, w_dw, b_dw, ln_g, ln_b):
    a, gate = jnp.split(u, 2, axis=-1)
    y = a * jax.nn.sigmoid(gate)
    y = lax.conv_general_dilated(
        y, w_dw[:, None, :], window_strides=(1,),
        padding=[(CONV_WIDTH - 1, 0)],
        dimension_numbers=('NWC', 'WIO', 'NWC'),
        feature_group_count=CONV_CH) + b_dw
    y = layer_norm(y, ln_g, ln_b)
    return jax.nn.silu(y)

def sliding_window_attention(q, k, v, sinks):
    B, S, _, Dh = q.shape
    nb = S // BLOCK
    g = N_Q_HEADS // N_KV_HEADS
    qb = q.reshape(B, nb, BLOCK, N_KV_HEADS, g, Dh)
    kb = k.reshape(B, nb, BLOCK, N_KV_HEADS, Dh)
    vb = v.reshape(B, nb, BLOCK, N_KV_HEADS, Dh)

    def with_prev(t):
        prev = jnp.concatenate([jnp.zeros_like(t[:, :1]), t[:, :-1]], axis=1)
        return jnp.concatenate([prev, t], axis=2)

    kw, vw = with_prev(kb), with_prev(vb)
    scores = jnp.einsum('bnqhgd,bnkhd->bnhgqk', qb, kw).astype(jnp.float32) * (Dh ** -0.5)
    qi = jnp.arange(BLOCK)[:, None] + BLOCK
    kj = jnp.arange(2 * BLOCK)[None, :]
    rel = qi - kj
    band = (rel >= 0) & (rel < WINDOW)
    first_ok = (jnp.arange(nb)[:, None, None] > 0) | (kj[None] >= BLOCK)
    mask = band[None] & first_ok
    scores = jnp.where(mask[None, :, None, None], scores, -jnp.inf)
    sink = jnp.broadcast_to(
        sinks.astype(jnp.float32).reshape(N_KV_HEADS, g)[None, None, :, :, None, None],
        scores.shape[:-1] + (1,))
    probs = jax.nn.softmax(jnp.concatenate([scores, sink], axis=-1), axis=-1)[..., :-1]
    out = jnp.einsum('bnhgqk,bnkhd->bnqhgd', probs.astype(v.dtype), vw)
    return out.reshape(B, S, N_Q_HEADS * Dh)

def memory_attention(q, mk, mv):
    B, S, _, Dh = q.shape
    scores = jnp.einsum('bshd,bmhd->bhsm', q, mk).astype(jnp.float32) * (Dh ** -0.5)
    probs = jax.nn.softmax(scores, axis=-1)
    out = jnp.einsum('bhsm,bmhd->bshd', probs.astype(mv.dtype), mv)
    return out.reshape(B, S, N_MEM_HEADS * Dh)

def second_inputs(seed: int = 0) -> dict:
    key = jax.random.key(seed)
    ks = iter(jax.random.split(key, 32))
    f32 = jnp.float32

    def w(shape, fan_in):
        return jax.random.normal(next(ks), shape, f32) * (fan_in ** -0.5)

    def gain(shape):
        return 1.0 + 0.02 * jax.random.normal(next(ks), shape, f32)

    def bias(shape):
        return 0.02 * jax.random.normal(next(ks), shape, f32)

    L = DEPTH
    x = jax.random.normal(next(ks), (BATCH, SEQ, D_MODEL), f32)
    mem = jax.random.normal(next(ks), (BATCH, MEM_LEN, D_MODEL), f32)
    positions = jnp.broadcast_to(jnp.arange(SEQ, dtype=jnp.int32)[None, :], (BATCH, SEQ))
    return {
        "x": x,
        "mem": mem,
        "positions": positions,
        "ffn1_norm": gain((L, D_MODEL)),
        "ffn1_w1": w((L, D_MODEL, D_FF_2), D_MODEL),
        "ffn1_w3": w((L, D_MODEL, D_FF_2), D_MODEL),
        "ffn1_w2": w((L, D_FF_2, D_MODEL), D_FF_2),
        "mix_norm": gain((L, D_MODEL)),
        "w_in": w((L, D_MODEL, D_IN), D_MODEL),
        "conv_w": w((L, CONV_WIDTH, CONV_CH), CONV_WIDTH),
        "conv_b": bias((L, CONV_CH)),
        "conv_ln_g": gain((L, CONV_CH)),
        "conv_ln_b": bias((L, CONV_CH)),
        "swa_q_norm": gain((L, HEAD_DIM)),
        "swa_k_norm": gain((L, HEAD_DIM)),
        "swa_sinks": jax.random.normal(next(ks), (L, N_Q_HEADS), f32),
        "mem_norm": gain((L, D_MODEL)),
        "w_mem_kv": w((L, D_MODEL, 2 * MEM_W), D_MODEL),
        "mem_q_norm": gain((L, HEAD_DIM)),
        "mem_k_norm": gain((L, HEAD_DIM)),
        "w_out": w((L, D_MIX, D_MODEL), D_MIX),
        "ffn2_norm": gain((L, D_MODEL)),
        "ffn2_w1": w((L, D_MODEL, D_FF_2), D_MODEL),
        "ffn2_w3": w((L, D_MODEL, D_FF_2), D_MODEL),
        "ffn2_w2": w((L, D_FF_2, D_MODEL), D_FF_2),
        "final_norm": gain((L, D_MODEL)),
    }

def second_block(x, mem, positions, ffn1_norm, ffn1_w1, ffn1_w3, ffn1_w2, mix_norm, w_in,
              conv_w, conv_b, conv_ln_g, conv_ln_b, swa_q_norm, swa_k_norm, swa_sinks,
              mem_norm, w_mem_kv, mem_q_norm, mem_k_norm, w_out,
              ffn2_norm, ffn2_w1, ffn2_w3, ffn2_w2, final_norm):
    B, S, _ = x.shape
    cos, sin = rope_tables(positions)
    splits = [2 * CONV_CH, 2 * CONV_CH + SWA_Q, 2 * CONV_CH + SWA_Q + SWA_KV,
              2 * CONV_CH + SWA_Q + 2 * SWA_KV]
    for l in range(DEPTH):
        h = x + 0.5 * swiglu(rms_norm_2(x, ffn1_norm[l]), ffn1_w1[l], ffn1_w3[l], ffn1_w2[l])

        n = rms_norm_2(h, mix_norm[l])
        p = n @ w_in[l]
        u_conv, q, k, v, q_mem = jnp.split(p, splits, axis=-1)

        y_conv = conv_module(u_conv, conv_w[l], conv_b[l], conv_ln_g[l], conv_ln_b[l])

        q = apply_rope(rms_norm_2(q.reshape(B, S, N_Q_HEADS, HEAD_DIM), swa_q_norm[l]), cos, sin)
        k = apply_rope(rms_norm_2(k.reshape(B, S, N_KV_HEADS, HEAD_DIM), swa_k_norm[l]), cos, sin)
        v = v.reshape(B, S, N_KV_HEADS, HEAD_DIM)
        y_swa = sliding_window_attention(q, k, v, swa_sinks[l])

        mkv = rms_norm_2(mem, mem_norm[l]) @ w_mem_kv[l]
        mk, mv = jnp.split(mkv, 2, axis=-1)
        mk = rms_norm_2(mk.reshape(B, MEM_LEN, N_MEM_HEADS, HEAD_DIM), mem_k_norm[l])
        mv = mv.reshape(B, MEM_LEN, N_MEM_HEADS, HEAD_DIM)
        qm = rms_norm_2(q_mem.reshape(B, S, N_MEM_HEADS, HEAD_DIM), mem_q_norm[l])
        y_mem = memory_attention(qm, mk, mv)

        y = jnp.concatenate([y_conv, y_swa, y_mem], axis=-1)
        h = h + y @ w_out[l]

        h = h + 0.5 * swiglu(rms_norm_2(h, ffn2_norm[l]), ffn2_w1[l], ffn2_w3[l], ffn2_w2[l])

        x = rms_norm_2(h, final_norm[l])
    return x


def setup_inputs(seed=0):
    out = dict(first_inputs(seed))
    for name, value in second_inputs(seed + 1).items():
        if name != "x":
            out[name + "_2"] = value
    return out


def reference(
    x, c, ctx, c_ctx, ada_w, ada_b, norm_g, mlp_w1, mlp_w2, ev_w_in, ev_w_out, ev_pool_w,
    ev_pool_scale, ev_rpb, rw_mu, rw_wr, rw_wk, rw_wv, rw_wo, rw_w0, rw_w1, rw_w2, rw_a0, rw_a1,
    rw_a2, rw_g1, rw_g2, rw_kk, rw_ka, rw_rk, rw_lng, rw_lnb, mem_2, positions_2, ffn1_norm_2,
    ffn1_w1_2, ffn1_w3_2, ffn1_w2_2, mix_norm_2, w_in_2, conv_w_2, conv_b_2, conv_ln_g_2,
    conv_ln_b_2, swa_q_norm_2, swa_k_norm_2, swa_sinks_2, mem_norm_2, w_mem_kv_2, mem_q_norm_2,
    mem_k_norm_2, w_out_2, ffn2_norm_2, ffn2_w1_2, ffn2_w3_2, ffn2_w2_2, final_norm_2,
):
    x = first_block(
        x, c, ctx, c_ctx, ada_w, ada_b, norm_g, mlp_w1, mlp_w2, ev_w_in, ev_w_out, ev_pool_w,
        ev_pool_scale, ev_rpb, rw_mu, rw_wr, rw_wk, rw_wv, rw_wo, rw_w0, rw_w1, rw_w2, rw_a0,
        rw_a1, rw_a2, rw_g1, rw_g2, rw_kk, rw_ka, rw_rk, rw_lng, rw_lnb,
    )
    return second_block(
        x, mem_2, positions_2, ffn1_norm_2, ffn1_w1_2, ffn1_w3_2, ffn1_w2_2, mix_norm_2, w_in_2,
        conv_w_2, conv_b_2, conv_ln_g_2, conv_ln_b_2, swa_q_norm_2, swa_k_norm_2, swa_sinks_2,
        mem_norm_2, w_mem_kv_2, mem_q_norm_2, mem_k_norm_2, w_out_2, ffn2_norm_2, ffn2_w1_2,
        ffn2_w3_2, ffn2_w2_2, final_norm_2,
    )


_drawn_inputs = setup_inputs


def setup_inputs(seed=0):
    import zlib

    import numpy as np

    out = dict(_drawn_inputs(seed))
    spreads = {}
    factors = {'ev_rpb': 8.0,
     'rw_w1': 8.0,
     'rw_w2': 8.0,
     'rw_a0': 3.79,
     'rw_a1': 4.809,
     'rw_a2': 4.802,
     'rw_kk': 3.08,
     'rw_lnb': 8.0,
     'ffn1_norm_2': 4.893,
     'mix_norm_2': 4.823,
     'conv_b_2': 2.883,
     'conv_ln_g_2': 4.988,
     'conv_ln_b_2': 5.543,
     'swa_q_norm_2': 8.0,
     'swa_k_norm_2': 8.0,
     'swa_sinks_2': 50.472,
     'mem_norm_2': 8.0,
     'mem_q_norm_2': 8.0,
     'mem_k_norm_2': 8.0,
     'ffn2_norm_2': 5.398}
    for name, (base, spread) in spreads.items():
        noise = np.random.default_rng([zlib.crc32(name.encode()), seed]).standard_normal(out[name].shape)
        drawn = base * np.exp(spread * noise) if base else spread * noise
        out[name] = jnp.asarray(drawn.astype(out[name].dtype))
    for name, factor in factors.items():
        out[name] = (out[name] * factor).astype(out[name].dtype)
    return out
```

```python
from collections import defaultdict
from contextlib import ExitStack

import numpy as np

import concourse.bass as bass
from concourse import mybir

P = 128
D = 1024
KD = D // P
LAT = 512
CTX = 256
TOK = LAT + CTX
FF1 = 4096
FF2 = 2816
COLS = 512
RING = 4
C = 64
CHUNKS = TOK // C
CTX_CHUNKS = CTX // C
PAIRS = KD
NEG = -1e30
UNIT = KD * TOK
PANEL = KD * COLS
POOL_WINDOWS = (2, 4, 8, 16)
TAPS = 31
Q_ORDER = (0, 3, 1, 4, 2, 5)
LEVELS = 6

F32 = mybir.dt.float32
I32 = mybir.dt.int32
ALU = mybir.AluOpType
ACT = mybir.ActivationFunctionType
AX = mybir.AxisListType



def mlp_steps(groups):
    steps = [("up", 0)]
    for g in range(groups):
        if g + 1 < groups:
            steps.append(("up", g + 1))
        steps.append(("down", g))
    return steps


MOD_STEPS = range(1, 7)
FF1_GROUPS = [8] * (FF1 // D)
FF2_GROUPS = [8, 8, 6]


def pack_panels(a):
    panels = []

    def add(w):
        rows, cols = w.shape
        full = np.zeros((KD * P, COLS), np.float32)
        full[:rows, :cols] = w
        panels.append(full.reshape(KD, P, COLS).transpose(1, 0, 2))

    def add_cols(w, lo=0, hi=None):
        for c in range(lo, w.shape[1] if hi is None else hi, COLS):
            add(w[:, c:c + COLS])

    def add_mlp(w1, w2, beside=None):
        for step, (kind, g) in enumerate(mlp_steps(len(FF1_GROUPS))):
            if beside is not None and step in MOD_STEPS:
                lo = 2 * (step - MOD_STEPS[0])
                add_cols(beside, lo * COLS, (lo + 2) * COLS)
            if kind == "up":
                add_cols(w1, g * D, (g + 1) * D)
            else:
                add_cols(w2[g * D:(g + 1) * D])

    def add_swiglu(w1, w3, w2):
        for kind, g in mlp_steps(len(FF2_GROUPS)):
            if kind == "up":
                for j in range(FF2_GROUPS[g] // 2):
                    c = g * D + 2 * j * P
                    add(np.concatenate([w1[:, c:c + P], w3[:, c:c + P], w1[:, c + P:c + 2 * P], w3[:, c + P:c + 2 * P]], 1))
            else:
                add_cols(w2[g * D:g * D + FF2_GROUPS[g] * P])

    add_cols(a["ada_w"][0], 0, 2 * D)
    for j in range(4):
        add_cols(a["ev_w_in"][0], j * COLS, (j + 1) * COLS)
        add_cols(a["ada_w"][0], 2 * D + 2 * j * COLS, 2 * D + 2 * (j + 1) * COLS)
    add_cols(a["ev_w_out"][0])
    add_mlp(a["mlp_w1"][0], a["mlp_w2"][0], a["ada_w"][1])
    add(np.concatenate([a["rw_w1"][0, 0], a["rw_w1"][0, 1], a["rw_a1"][0, 0], a["rw_a1"][0, 1], a["rw_g1"][0]], 1))
    add_cols(a["rw_wk"][0])
    heads = a["rw_wv"][0].reshape(D, PAIRS, 2, C)
    add(heads[:, :, 0].reshape(D, COLS))
    add(heads[:, :, 1].reshape(D, COLS))
    second = np.concatenate([a["rw_w2"][0].reshape(P, D), a["rw_a2"][0].reshape(P, D), a["rw_g2"][0]], 1)
    panels.append(np.concatenate([second, np.zeros((P, PANEL - 3 * D), np.float32)], 1).reshape(P, KD, COLS))
    add_cols(a["rw_wr"][0])
    add_cols(a["rw_wo"][0])
    add_mlp(a["mlp_w1"][1], a["mlp_w2"][1])
    for l in range(2):
        add_swiglu(a["ffn1_w1_2"][l], a["ffn1_w3_2"][l], a["ffn1_w2_2"][l])
        add(a["w_mem_kv_2"][l])
        w = a["w_in_2"][l]
        conv, gate = w[:, 0:384].reshape(D, 3, P), w[:, 384:768].reshape(D, 3, P)
        q = w[:, 768:1152].reshape(D, 6, C)[:, Q_ORDER, :].reshape(D, 3, P)
        add(np.concatenate([conv[:, 0], gate[:, 0], conv[:, 1], gate[:, 1]], 1))
        add(np.concatenate([conv[:, 2], gate[:, 2], q[:, 0], q[:, 1]], 1))
        add(np.concatenate([q[:, 2], w[:, 1152:1280], w[:, 1408:1664]], 1))
        add(w[:, 1280:1408])
        wo = a["w_out_2"][l]
        wo = np.concatenate([wo[0:384], wo[384:768].reshape(6, C, D)[Q_ORDER, :, :].reshape(384, D), wo[768:]], 0)
        add_cols(wo)
        add_swiglu(a["ffn2_w1_2"][l], a["ffn2_w3_2"][l], a["ffn2_w2_2"][l])
    return np.ascontiguousarray(np.stack(panels).reshape(len(panels), P, PANEL))


VEC_AT = {}


def vector_parts():
    for i in range(2):
        for j in range(4):
            yield f"norm_g{i}{j}", KD
        yield f"ada_b{i}", 6 * KD
    yield "pool_scale", 4
    for j in range(6):
        yield f"mu{j}", KD
    for d in range(2):
        yield f"w0{d}", KD
        yield f"a0{d}", KD
    for name in ("kk", "ka", "rk", "lng", "lnb"):
        yield name, KD
    for l in range(2):
        for name in ("ffn1_norm", "mix_norm", "mem_norm", "ffn2_norm", "final_norm"):
            yield f"{name}{l}", KD
        for name in ("conv_b", "conv_ln_g", "conv_ln_b"):
            yield f"{name}{l}", 3
        yield f"conv_w{l}", 3 * TAPS
        for name in ("swa_q_norm", "swa_k_norm", "mem_q_norm", "mem_k_norm"):
            yield f"{name}{l}", 1
        yield f"sinks{l}", 6


NVEC = 0
for _name, _cols in vector_parts():
    VEC_AT[_name] = NVEC
    NVEC += _cols


def pack_vectors(a):
    v = np.zeros((P, NVEC), np.float32)

    def put(name, x):
        x = np.asarray(x).reshape(-1, P).T
        v[:, VEC_AT[name]:VEC_AT[name] + x.shape[1]] = x

    for i in range(2):
        for j in range(4):
            put(f"norm_g{i}{j}", a["norm_g"][i, j])
        put(f"ada_b{i}", a["ada_b"][i])
    put("pool_scale", a["ev_pool_scale"][0])
    for j in range(6):
        put(f"mu{j}", a["rw_mu"][0, j])
    for d in range(2):
        put(f"w0{d}", a["rw_w0"][0, d])
        put(f"a0{d}", a["rw_a0"][0, d])
    for name in ("kk", "ka", "rk", "lng", "lnb"):
        put(name, a[f"rw_{name}"][0])
    for l in range(2):
        for name in ("ffn1_norm", "mix_norm", "mem_norm", "ffn2_norm", "final_norm", "conv_b", "conv_ln_g", "conv_ln_b"):
            put(f"{name}{l}", a[f"{name}_2"][l])
        put(f"conv_w{l}", a["conv_w_2"][l].reshape(TAPS, 3, P).transpose(1, 0, 2))
        for name in ("swa_q_norm", "swa_k_norm", "mem_q_norm", "mem_k_norm"):
            put(f"{name}{l}", np.concatenate([a[f"{name}_2"][l]] * 2))
        put(f"sinks{l}", np.repeat(np.asarray(a["swa_sinks_2"][l])[:, None], P, 1))
    return v


CONST_PARTS = (("ident", P), ("head_ones", P), ("rotate", P), ("gram_mask", 2 * 2 * C),
               ("level", LEVELS * C), ("level_t", LEVELS * C), ("ident2", C), ("pool_edge", 2 * 15), ("inv_freq", 1))
CONST_AT = {}
NCONST = 0
for _name, _cols in CONST_PARTS:
    CONST_AT[_name] = NCONST
    NCONST += _cols


def pack_constants():
    v = np.zeros((P, NCONST), np.float32)

    def put(name, x):
        x = np.asarray(x, np.float32).reshape(x.shape[0], -1)
        v[:, CONST_AT[name]:CONST_AT[name] + x.shape[1]] = x

    p = np.arange(P)
    put("ident", np.eye(P))
    put("head_ones", p[:, None] // C == p[None, :] // C)
    same = p[:, None] // C == p[None, :] // C
    half = C // 2
    first = p[None, :] % C < half
    put("rotate", np.where(same & first & (p[:, None] == p[None, :] + half), -1.0, 0.0)
        + np.where(same & ~first & (p[:, None] == p[None, :] - half), 1.0, 0.0))
    s, t = (p % C)[:, None], np.arange(C)[None, :]
    put("gram_mask", np.concatenate([s < t, s <= t, s > t, s >= t], 1))
    levels = []
    for j in range(LEVELS):
        m = 1 << j
        levels.append((s // m % 2 == 1) & (t // m == s // m - 1))
    put("level", np.concatenate(levels, 1))
    put("level_t", np.concatenate([(t // (1 << j) % 2 == 1) & (s // (1 << j) == t // (1 << j) - 1) for j in range(LEVELS)], 1))
    put("ident2", s == t)
    edge = []
    for w in POOL_WINDOWS:
        edge.append([w / (i + w // 2) for i in range(w // 2)] + [w / (w - i) for i in range(w // 2)])
    put("pool_edge", np.repeat(np.concatenate(edge)[None, :], P, 0))
    put("inv_freq", (10000.0 ** (-(2 * (p % half)).astype(np.float32) / C)).astype(np.float32)[:, None])
    return v


def pack_window():
    rel = (np.arange(P)[:, None] + P) - np.arange(2 * P)[None, :]
    return np.where((rel >= 0) & (rel < P), np.float32(0.0), np.float32(NEG)).astype(np.float32)


def pack_bias(rpb):
    heads = rpb.shape[0]
    col = np.arange(64)
    start = np.clip(col - 8, 0, 48)
    ok = (col[None, :] >= start[:, None]) & (col[None, :] < start[:, None] + 16)
    dc = np.clip(col[None, :] - col[:, None], -15, 15) + 15
    t = np.where(ok[None, None], rpb[:, :, dc], np.float32(NEG)).transpose(0, 2, 1, 3)
    out = np.full((heads, 2, 64, 16, 64), np.float32(NEG), np.float32)
    out[:, 0, :, 0:15] = t
    out[:, 1, :, 1:16] = t
    return out.reshape(heads, P, 16 * 64)



def build_program(nc, panels, vecs, consts, x_in, c_in, mem_in, pool_w, bias, pos, window_in, out, x_save):
    npanels = panels.shape[0]
    with ExitStack() as ctx:
        def sb(name, shape, dt=F32):
            return ctx.enter_context(nc.sbuf_tensor(name, shape, dt))

        sems = {}

        def sem(name):
            if name not in sems:
                sems[name] = ctx.enter_context(nc.semaphore(name))
            return sems[name]

        arena = sb("arena", [P, 5 * UNIT + RING * PANEL])
        vec = sb("vec", [P, NVEC])
        const = sb("const", [P, NCONST])
        ones = sb("ones", [P, P])
        square = sb("square", [P, 2, TOK])
        rstd = sb("rstd", [P, TOK])
        mod_sb = sb("mod", [P, 2, 2, 6 * KD])
        gain = sb("gain", [P, 2, 4, 2, KD])
        silu_c = sb("silu_c", [P, KD, 2])
        raw_c = sb("raw_c", [P, KD, 2])
        stat = sb("stat", [P, 16])
        reset = sb("reset", [P, TOK])
        ps = ctx.enter_context(nc.psum_tensor("ps", [P, 8, 512], F32))

        def area(at, *shape):
            n = int(np.prod(shape))
            flat = arena[:, at:at + n]
            if len(shape) == 1:
                return flat
            names = " ".join("abcd"[:len(shape)])
            return flat.rearrange(f"p ({names}) -> p {names}", **{"abcd"[i]: s for i, s in enumerate(shape)})

        X0, H0, Y0, W0 = 0, UNIT, 2 * UNIT, 3 * UNIT
        RING0 = 5 * UNIT
        X, H, Y = (area(o, KD, TOK) for o in (X0, H0, Y0))
        ring = [area(RING0 + s * PANEL, KD, COLS) for s in range(RING)]
        hidden1 = [area(W0 + s * UNIT, KD, TOK) for s in range(2)]
        hidden2 = [area(W0 + s * KD * LAT, KD, LAT) for s in range(2)]
        Z = area(W0, KD, TOK)
        qT = area(W0, 4, TOK)
        kT = area(W0 + 4 * TOK, 4, TOK)
        vN = area(W0 + 8 * TOK, TOK // P, 512)
        pool_buf = [area(W0 + 12 * TOK + i * 792, 792) for i in range(3)]
        pool_wb = area(W0 + 12 * TOK + 3 * 792, 4, P)
        probs = area(H0, 3, TOK)
        probsT = area(H0 + 3 * TOK, 2, TOK)
        bias_sb = area(H0 + 5 * TOK, 2, 1024)
        B0 = W0
        q2 = area(B0, 6, LAT)
        mk2 = area(B0 + 6 * LAT, 2, CTX)
        v2 = area(B0 + 7 * LAT, 4, P)
        mv2 = area(B0 + 8 * LAT, 2, 256)
        conv_in = area(B0 + 9 * LAT, 3, TAPS - 1 + LAT)
        conv_y = area(B0 + 9 * LAT + 3 * (TAPS - 1 + LAT), 3, LAT)
        rope = area(W0 + 2 * KD * LAT, 2, LAT)
        rope_tmp = area(W0 + 2 * KD * LAT + 2 * LAT, 2, LAT)
        pos_i = area(W0 + 2 * KD * LAT + 4 * LAT, LAT)
        window = area(W0 + 2 * KD * LAT + 5 * LAT, 2 * P)
        sig = square[:, :, 0:LAT]

        def vcol(name, c=0, n=1):
            return vec[:, VEC_AT[name] + c:VEC_AT[name] + c + n]

        def ccol(name, c=0, n=1):
            return const[:, CONST_AT[name] + c:CONST_AT[name] + c + n]

        ident = ccol("ident", 0, P)
        head_ones = ccol("head_ones", 0, P)
        rotate = ccol("rotate", 0, P)

        SEG2 = ((0, 384), (384, TOK))
        SEG1 = ((0, LAT),)
        SEGM = ((LAT, TOK),)

        def norm_banks(lo, hi):
            return [(a, b, bank) for a, b, bank in ((lo, min(hi, LAT), 4), (max(lo, LAT), hi, 5)) if b > a]

        def norm_psum(lo, hi):
            flat = ps[:, 4:6, :].rearrange("p a b -> p (a b)")
            return flat[:, lo:hi]

        def even_units():
            units = []
            for h in range(8):
                base, ch = C * (h % 2), h // 2
                for qt in range(TOK // P):
                    lat = qt < LAT // P
                    lo = 0 if lat else LAT
                    units.append(dict(
                        q=qT[base:base + C, ch, qt * P:(qt + 1) * P],
                        keys=[kT[base:base + C, ch, a:b] for a, b in ([(0, LAT)] if lat else []) + [(LAT, TOK)]],
                        bias=bias_sb[:, h % 2, (7 - 2 * qt) * 64:(7 - 2 * qt) * 64 + LAT] if lat else None,
                        bias_head=h, width=TOK - lo, sink=None,
                        values=[vN[:, t, h * C:(h + 1) * C] for t in range(lo // P, TOK // P)],
                        base=base, dest=Y[base:base + C, 4 + ch, qt * P:(qt + 1) * P]))
            return units

        def conformer_units(l):
            units = []
            for i in range(6):
                base, ch = C * (i % 2), i // 2
                for qb in range(LAT // P):
                    lo = max(0, qb - 1)
                    n = (qb + 1 - lo) * P
                    units.append(dict(
                        q=q2[base:base + C, ch, qb * P:(qb + 1) * P],
                        keys=[q2[base:base + C, 3, lo * P:(qb + 1) * P]],
                        bias=window[:, 2 * P - n:2 * P], bias_head=None, width=n,
                        sink=vcol(f"sinks{l}", Q_ORDER[i]),
                        values=[v2[:, t, (i % 2) * C:(i % 2 + 1) * C] for t in range(lo, qb + 1)],
                        base=base, dest=Y[base:base + C, 3 + ch, qb * P:(qb + 1) * P]))
            for h in range(4):
                base, ch = C * (h % 2), h // 2
                for qb in range(LAT // P):
                    units.append(dict(
                        q=q2[base:base + C, 4 + ch, qb * P:(qb + 1) * P],
                        keys=[mk2[base:base + C, ch, :]], bias=None, bias_head=None, width=CTX, sink=None,
                        values=[mv2[:, t, h * C:(h + 1) * C] for t in range(2)],
                        base=base, dest=Y[base:base + C, 6 + ch, qb * P:(qb + 1) * P]))
            return units

        def scores_ps(u, width):
            return ps[:, 2 * (u % 2):2 * (u % 2) + 2, :].rearrange("p a b -> p (a b)")[:, 0:width]

        def turned_ps(width):
            return ps[:, 4:6, :].rearrange("p a b -> p (a b)")[:, 0:width]

        XX, MIX = Y, area(W0, KD, TOK)
        K = area(W0 + UNIT, KD, TOK)
        V = area(X0, CHUNKS, PAIRS, C)
        R = area(H0, KD, LAT)
        decay_in, a_in = area(H0 + KD * LAT, TOK), area(H0 + KD * LAT + TOK, TOK)
        gate_in = area(H0 + KD * LAT + 2 * TOK, LAT)
        LORA_SLOT = 3
        lora2 = area(RING0 + LORA_SLOT * PANEL, 3, D)
        k_sum = area(RING0 + LORA_SLOT * PANEL + 3 * D, LAT)
        y_pair = area(RING0 + LORA_SLOT * PANEL + 3 * D + LAT, LAT)
        state = sb("state", [P, 2, C])
        omka = sb("omka", [P, KD])
        w0_neg = sb("w0_neg", [P, 2, C])
        state_dec = sb("state_dec", [P, 2, C])
        chunk_decay = sb("chunk_decay", [P, 2, CHUNKS])
        SET = 4 * CHUNKS * 2 * C + CHUNKS * 2 * 2 * C + CHUNKS * C
        SET0 = (Y0, RING0)
        sets = []
        for o in SET0:
            W = CHUNKS * 2 * C
            sets.append(dict(
                kr=area(o, CHUNKS, 2, C), bk=area(o + W, CHUNKS, 2, C), bkn=area(o + 2 * W, CHUNKS, 2 * C),
                uv=area(o + 3 * W, CHUNKS, 2, C), gram=area(o + 4 * W, CHUNKS, 2, 2 * C), xt=area(o + 6 * W, CHUNKS, C)))
        spare = [area(o + SET + i * TOK, TOK) for o in SET0 for i in range(3)]
        f_kk, f_a, f_inc, f_inv, f_b, f_kd = spare
        f_cs = square[:, 1, :]
        v_turned = f_kd[:, 0:LAT]
        chunked = lambda f: f.rearrange("p (c t) -> p c t", t=C)
        f_x, f_at, f_am, f_y1 = (chunked(f) for f in (f_inv, f_b, f_kd, f_inc))
        E_HALF = float(np.exp(-0.5))
        JOBS = 2 * PAIRS
        GRAMS = CHUNKS // 2

        def chunk_order(d):
            ctx_first = list(range(LAT // C, CHUNKS))
            lat = list(range(LAT // C))
            return ctx_first + lat if d == 0 else ctx_first[::-1] + lat[::-1]

        def two_banks(b, n=TOK):
            return ps[:, b:b + 2, :].rearrange("p a b -> p (a b)")[:, 0:n]

        def job_steps(e):
            for j in range(JOBS + 1):
                for s in range(CHUNKS):
                    for part, name in enumerate(("state_in", "solve", "state_out")):
                        if j > 0:
                            e[name](j - 1, s)
                        if j < JOBS:
                            e["prepare"](j, 3 * s + part)
                if j > 0 and j % 2 == 0:
                    e["readout"](j // 2 - 1)

        def model(e):
            e["load"]()
            e["mod"](0, 0, 4)
            e["gains"](0, 0)
            e["norm_mod"](0, 0)
            e["even_in"]()
            e["gains"](0, 1)
            e["attention"](even_units(), None)
            e["project"](2, SEG2, Y, Z, "attn")
            e["post"](Z, 0, 1)
            e["norm_mod"](0, 2)
            e["mlp"](SEG2, True)
            e["post"](Y, 0, 3)
            e["gains"](1, 0)
            e["gains"](1, 1)
            e["norm_mod"](1, 0)
            e["odd_in"]()
            job_steps(e)
            e["odd_out"]()
            e["project"](2, SEG1, R, Z, "odd")
            e["post"](Z, 1, 1)
            e["norm_mod"](1, 2)
            e["mlp"](SEG1, False)
            e["post"](Y, 1, 3)
            e["tables"]()
            for l in range(2):
                e["norm_vec"](0, LAT, "ffn1_norm", l, X)
                e["swiglu"]()
                e["half_step"]()
                e["norm_vec"](LAT, TOK, "mem_norm", l, X)
                e["norm_vec"](0, LAT, "mix_norm", l, X)
                e["mix_in"](l)
                e["attention"](conformer_units(l), l)
                e["conv"](l)
                e["project"](2, SEG1, Y, None, "attn")
                e["norm_vec"](0, LAT, "ffn2_norm", l, X)
                e["swiglu"]()
                e["half_step"]()
                e["norm_vec"](0, LAT, "final_norm", l, X)
            e["store"]()

        block = ctx.enter_context(nc.Block())

        def counting():
            n = defaultdict(int)

            def more(name, k=1):
                n[name] += k
                return n[name]

            def one(name):
                n[name] += 1
                return 1

            return n, more, one

        @block.sync
        def _(sp):
            n, more, one = counting()
            ends = []

            def load_panel(tiles, width=PANEL):
                p = len(ends)
                if p >= RING:
                    if ends[p - RING] > 0:
                        sp.wait_ge(sem("tile_done"), ends[p - RING])
                sp.dma_start(arena[:, RING0 + (p % RING) * PANEL:RING0 + (p % RING) * PANEL + width],
                             panels[p, :, 0:width]).then_inc(sem(f"panel{p % RING}"), 16)
                n["tile"] += tiles
                ends.append(n["tile"])

            def load():
                sp.dma_start(raw_c[:, :, :], c_in).then_inc(sem("small_in"), 16)
                sp.dma_start(vec[:, :], vecs).then_inc(sem("small_in"), 16)
                load_panel(1)
                load_panel(1)
                sp.dma_start(const[:, :], consts).then_inc(sem("small_in"), 16)
                sp.dma_start(X, x_in).then_inc(sem("x_in"), 16)
                n["mod_skip"] = 2

            def mod(i, lo, hi):
                for _ in range(lo + n["mod_skip"], hi):
                    load_panel(1)
                n["mod_skip"] = 0

            def even_in():
                for j, tiles in enumerate((8, 8, 8, TOK // P)):
                    load_panel(tiles)
                    mod(0, 4 + 2 * j, 6 + 2 * j)
                n["tile"] += 8

            def project(count, segs, src, dest, ready):
                for _ in range(count):
                    load_panel(4 * len(segs))

            def mlp(segs, beside):
                for step, _ in enumerate(mlp_steps(len(FF1_GROUPS))):
                    if beside and step in MOD_STEPS:
                        mod(1, 2 * (step - MOD_STEPS[0]), 2 * (step - MOD_STEPS[0]) + 2)
                    for _ in range(2):
                        load_panel(4 * len(segs))

            def swiglu():
                for kind, g in mlp_steps(len(FF2_GROUPS)):
                    if kind == "up":
                        for _ in range(FF2_GROUPS[g] // 2):
                            load_panel(4)
                    else:
                        for _ in range(2):
                            load_panel(4, FF2_GROUPS[g] * COLS)

            def odd_in():
                load_panel(5)
                for _ in range(2):
                    load_panel(8)
                for _ in range(2):
                    load_panel(CHUNKS)
                load_panel(0, 3 * D)
                for _ in range(2):
                    load_panel(4)

            def odd_out():
                if PAIRS > 0:
                    sp.wait_ge(sem("r_out"), PAIRS)

            def mix_in(l):
                for tiles in (4, 4, 4, 4, LAT // P):
                    load_panel(tiles)

            def store():
                if 10 * KD > 0:
                    sp.wait_ge(sem("x_chunk"), 10 * KD)
                sp.dma_start(out, X[:, :, 0:LAT]).then_inc(sem("stored"), 16)
                sp.wait_ge(sem("stored"), 16)

            skip = lambda *a: None
            model(dict(load=load, mod=mod, gains=skip, norm_mod=skip, even_in=even_in, attention=skip, project=project,
                       post=skip, mlp=mlp, odd_in=odd_in, prepare=skip, state_in=skip, solve=skip, state_out=skip,
                       readout=skip, odd_out=odd_out, tables=skip, norm_vec=skip, swiglu=swiglu, half_step=skip,
                       mix_in=mix_in, conv=skip, store=store))
            assert len(ends) == npanels

        @block.gpsimd
        def _(pool):
            n, more, one = counting()

            def load():
                pool.dma_start(pool_wb, pool_w).then_inc(sem("pool_w"), 16)
                pool.memset(ones[:, :], 1.0).then_inc(sem("ones"), one("ones"))

            def attention(units, l):
                heads = []
                for u, unit in enumerate(units):
                    h = unit["bias_head"]
                    if h is not None and h not in heads:
                        heads.append(h)
                        if len(heads) == 1:
                            if n["tile"] > 0:
                                pool.wait_ge(sem("tile_free"), n["tile"])
                        if len(heads) > 2:
                            if u - TOK // P > 0:
                                pool.wait_ge(sem("scored"), u - TOK // P)
                        pool.dma_start(bias_sb[:, h % 2, :], bias[h]).then_inc(sem(f"bias{h % 2}"), 16)

            def even_in():
                n["tile"] += 24 + TOK // P + 8 + 8

            def mod(i, lo, hi):
                n["tile"] += hi - lo

            def odd_in():
                if 2 * KD > 0:
                    pool.wait_ge(sem("x_chunk"), 2 * KD)
                pool.dma_start(x_save, X[:, :, 0:LAT]).then_inc(sem("x_saved"), 16)

            def prepare(j, i):
                p, d = divmod(j, 2)
                if i == 8:
                    uv = sets[d]["uv"]
                    pool.wait_ge(sem("keys"), more("keys"))
                    for h, lo in ((0, C), (1, 0)):
                        ins = pool.tensor_copy(uv[lo:lo + C, :, h, :], V[lo:lo + C, :, p, :])
                    ins.then_inc(sem("values"), one("values"))

            def odd_out():
                if PAIRS > 0:
                    pool.wait_ge(sem("r_out"), PAIRS)
                pool.dma_start(X[:, :, 0:LAT], x_save).then_inc(sem("x_back"), 16)
                pool.dma_start(X[:, :, LAT:TOK], mem_in).then_inc(sem("mem_in"), 16)

            def tables():
                if 4 * KD > 0:
                    pool.wait_ge(sem("x_chunk"), 4 * KD)
                pool.dma_start(pos_i.bitcast(I32), pos).then_inc(sem("pos"), 16)
                pool.dma_start(window, window_in).then_inc(sem("pos"), 16)

            skip = lambda *a: None
            model(dict(load=load, mod=mod, gains=skip, norm_mod=skip, even_in=even_in, attention=attention, project=skip,
                       post=skip, mlp=skip, odd_in=odd_in, prepare=prepare, state_in=skip, solve=skip, state_out=skip,
                       readout=skip, odd_out=odd_out, tables=tables, norm_vec=skip, swiglu=skip, half_step=skip,
                       mix_in=skip, conv=skip, store=skip))

        @block.tensor
        def _(pe):
            n, more, one = counting()

            def panel():
                p = n["panel"]
                n["panel"] += 1
                pe.wait_ge(sem(f"panel{p % RING}"), 16 * (p // RING + 1))
                return ring[p % RING]

            def tile():
                if n["tile"] - 3 > 0:
                    pe.wait_ge(sem("tile_free"), n["tile"] - 3)
                n["tile"] += 1
                return ps[:, (n["tile"] - 1) % 4, :]

            def accumulate(dest, left, right, nk=KD, ready=None):
                for k in range(nk):
                    if ready:
                        pe.wait_ge(sem(ready), more(ready))
                    ins = pe.matmul(dest, left(k), right(k), start=(k == 0), stop=(k == nk - 1))
                ins.then_inc(sem("tile_done"), one("tile_done"))

            def columns(w, ms, src, segs, nk=KD, ready=None):
                for m in ms:
                    for a, b in segs:
                        accumulate(tile()[:, 0:b - a], lambda k: w[:, k, m * P:(m + 1) * P],
                                   lambda k: src[:, k, a:b], nk, ready)
                        ready = None

            def rows(w, lo, width, src, tok, cols, ready=None):
                for t in tok:
                    accumulate(tile()[:, 0:width], lambda k: src[:, k, t * P:(t + 1) * P],
                               lambda k: w[:, k, cols:cols + width], KD, ready)
                    ready = None

            def sums(lhs, count, lo, hi, src="square"):
                if n["norm"] > 0:
                    pe.wait_ge(sem("var"), n["norm"])
                n["norm"] += 1
                for c in range(count):
                    if src == "square":
                        pe.wait_ge(sem("square"), more("square"))
                    for a, b, bank in norm_banks(lo, hi):
                        right = square[:, n["sq"] % 2, a - lo:b - lo] if src == "square" else conv_y[:, c, :]
                        ins = pe.matmul(ps[:, bank, 0:b - a], lhs, right, start=(c == 0), stop=(c == count - 1))
                    n["sq"] += src == "square"
                    ins.then_inc(sem("summed"), one("summed"))

            def load():
                pe.wait_ge(sem("small_in"), 48)
                pe.wait_ge(sem("ones"), more("ones"))
                pe.wait_ge(sem("silu"), more("silu"))

            def mod(i, lo, hi):
                for _ in range(lo, hi):
                    w = panel()
                    bank = tile()
                    for m in range(4):
                        for k in range(KD):
                            ins = pe.matmul(bank[:, 2 * m:2 * m + 2], w[:, k, m * P:(m + 1) * P], silu_c[:, k, :],
                                            start=(k == 0), stop=(k == KD - 1))
                    ins.then_inc(sem("tile_done"), one("tile_done"))

            def norm_mod(i, which):
                sums(ones[:, :], KD, 0, TOK if (i, which) != (1, 2) else LAT)
                n["source"] = "h_act"

            def norm_vec(lo, hi, name, l, src):
                sums(ones[:, :], KD, lo, hi)
                n["source"] = "h_dve"

            def post(src, i, which):
                sums(ones[:, :], KD, 0, TOK if i == 0 else LAT)

            def even_in():
                columns(panel(), range(4), H, ((0, LAT), (LAT, TOK)), ready="h_act")
                mod(0, 4, 6)
                columns(panel(), range(4), H, SEG2)
                mod(0, 6, 8)
                columns(panel(), range(4), H, SEG2)
                mod(0, 8, 10)
                rows(panel(), 0, 512, H, range(TOK // P), 0)
                mod(0, 10, 12)
                pe.wait_ge(sem("pool_w"), 16)
                for g in range(4):
                    pe.wait_ge(sem("pooled"), more("pooled"))
                    for a, b in SEG2:
                        accumulate(tile()[:, 0:b - a], lambda k: pool_wb[:, g, :], lambda k: Y[:, 4 + g, a:b], 1)

            def attention(units, l):
                if n["tile"] > 0:
                    pe.wait_ge(sem("tile_free"), n["tile"])
                if n["norm"] > 0:
                    pe.wait_ge(sem("var"), n["norm"])
                if n["unit"] > 0:
                    pe.wait_ge(sem("roped"), more("roped"))
                base = n["unit"]
                for i in range(len(units) + 3):
                    if i < len(units):
                        unit, u = units[i], base + i
                        if u - 1 > 0:
                            pe.wait_ge(sem("scored"), u - 1)
                        col = 0
                        for key in unit["keys"]:
                            w = key.shape[1]
                            ins = pe.matmul(scores_ps(u, TOK)[:, col:col + w], unit["q"], key, start=True, stop=True)
                            col += w
                        ins.then_inc(sem("scores"), one("scores"))
                    if 2 <= i <= len(units) + 1:
                        unit, u = units[i - 2], base + i - 2
                        pe.wait_ge(sem("probs"), more("probs"))
                        if u > 0:
                            pe.wait_ge(sem("turned_copy"), u)
                        for t in range(unit["width"] // P):
                            ins = pe.transpose(turned_ps(TOK)[:, t * P:(t + 1) * P], probs[:, u % 3, t * P:(t + 1) * P],
                                               ident)
                        ins.then_inc(sem("turned"), one("turned"))
                    if i >= 3:
                        unit, u = units[i - 3], base + i - 3
                        if u + 1 > 0:
                            pe.wait_ge(sem("turned_copy"), u + 1)
                        if u - 1 > 0:
                            pe.wait_ge(sem("attended"), u - 1)
                        nt = unit["width"] // P
                        for t in range(nt):
                            ins = pe.matmul(ps[unit["base"]:unit["base"] + C, 6 + u % 2, 0:P], unit["values"][t],
                                            probsT[:, u % 2, t * P:(t + 1) * P], start=(t == 0), stop=(t == nt - 1))
                        ins.then_inc(sem("output"), one("output"))
                n["unit"] += len(units)

            def project(count, segs, src, dest, ready):
                if ready == "attn":
                    if n["unit"] > 0:
                        pe.wait_ge(sem("attended"), n["unit"])
                    if dest is None:
                        pe.wait_ge(sem("convolved"), more("convolved"))
                for _ in range(count):
                    columns(panel(), range(4), src, segs)

            def mlp(segs, beside):
                ready = "h_act"
                ends = {}
                for step, (kind, g) in enumerate(mlp_steps(len(FF1_GROUPS))):
                    if beside and step in MOD_STEPS:
                        mod(1, 2 * (step - MOD_STEPS[0]), 2 * (step - MOD_STEPS[0]) + 2)
                    if kind == "down":
                        if ends[g] > 0:
                            pe.wait_ge(sem("tile_free"), ends[g])
                    for _ in range(2):
                        columns(panel(), range(4), H if kind == "up" else hidden1[g % 2], segs, KD, ready)
                        ready = None
                    ends[g] = n["tile"]

            def swiglu():
                ready = "h_dve"
                ends = {}
                for kind, g in mlp_steps(len(FF2_GROUPS)):
                    if kind == "up":
                        for _ in range(FF2_GROUPS[g] // 2):
                            columns(panel(), range(4), H, SEG1, KD, ready)
                            ready = None
                        ends[g] = n["tile"]
                    else:
                        if ends[g] > 0:
                            pe.wait_ge(sem("tile_free"), ends[g])
                        for _ in range(2):
                            columns(panel(), range(4), hidden2[g % 2], SEG1, FF2_GROUPS[g])

            def odd_in():
                n["h_act"] += KD
                w = panel()
                columns(w, [0], K, SEG2, ready="mix")
                columns(w, [1], MIX, SEG2, ready="mix")
                columns(w, [2], K, SEG1, ready="mix")
                ready = "mix"
                for _ in range(2):
                    columns(panel(), range(4), MIX, SEG2, ready=ready)
                    ready = None
                ready = "mix"
                for h in range(2):
                    w = panel()
                    lo = C if h == 0 else 0
                    for c in range(CHUNKS):
                        accumulate(tile()[lo:lo + C, :], lambda k: MIX[:, k, c * C:(c + 1) * C], lambda k: w[:, k, :],
                                   KD, ready)
                        ready = None
                panel()
                ready = "mix"
                for _ in range(2):
                    columns(panel(), range(4), XX, SEG1, ready=ready)
                    ready = None
                if n["tile"] > 0:
                    pe.wait_ge(sem("tile_free"), n["tile"])
                pe.wait_ge(sem("lora"), more("lora", 3))
                if n["norm"] > 0:
                    pe.wait_ge(sem("var"), n["norm"])

            def half(h):
                return slice(C * h, C * h + C)

            def wide(bank, lhs, rhs):
                pe.matmul(ps[:, bank, :], lhs, rhs[:, 0:LAT], start=True, stop=True)
                return pe.matmul(ps[:, bank + 1, 0:CTX], lhs, rhs[:, LAT:TOK], start=True, stop=True)

            def prepare(j, i):
                p, d = divmod(j, 2)
                S = sets[d]
                if i == 0 and d == 0:
                    pe.wait_ge(sem("feature_act"), more("feature_act"))
                    wide(0, head_ones, square[:, 0, :]).then_inc(sem("feature_pe"), one("feature_pe"))
                elif i == 2:
                    if d == 0:
                        pe.wait_ge(sem("feature_act"), more("feature_act"))
                    wide(0, lora2[half(d), 0, p * P:(p + 1) * P], decay_in[half(d), :]).then_inc(sem("feature_pe"), one("feature_pe"))
                elif i == 3:
                    pe.wait_ge(sem("feature_act"), more("feature_act"))
                    wide(0, lora2[half(d), 1, p * P:(p + 1) * P], a_in[half(d), :]).then_inc(sem("feature_pe"), one("feature_pe"))
                    n["feature_act"] += 3
                elif 9 <= i < 9 + GRAMS:
                    g = i - 9
                    if g == 0:
                        pe.wait_ge(sem("keys"), more("keys"))
                    if GRAMS * j + g - 1 > 0:
                        pe.wait_ge(sem("gram_read"), GRAMS * j + g - 1)
                    if GRAMS * j + g - 1 > 0:
                        pe.wait_ge(sem("gram_copied"), GRAMS * j + g - 1)
                    bank = 2 * (g % 2)
                    for c in (2 * g, 2 * g + 1):
                        at_c = c % 2
                        for h in range(2):
                            right = S["kr"][half(h), c, :, :] if c < LAT // C else S["kr"][half(h), c, 0:1, :]
                            wd = 2 * C if c < LAT // C else C
                            o = at_c * 2 * C
                            pe.matmul(ps[:, bank + h, o:o + wd], S["bk"][half(h), c, :, :].rearrange("p a b -> p (a b)"),
                                      right.rearrange("p a b -> p (a b)"), start=True, stop=True)
                        for h in range(2):
                            o = at_c * C
                            pe.matmul(ps[half(h), 4 + g % 2, o:o + C], S["kr"][half(h), c, 0, :], S["bk"][half(h), c, h, :],
                                      start=True, stop=True)
                    for c in (2 * g, 2 * g + 1):
                        o = (1 + c % 2) * P
                        ins = pe.transpose(ps[:, 4 + g % 2, o:o + P], S["bk"][:, c, :, :].rearrange("p a b -> p (a b)"), ident)
                    ins.then_inc(sem("gram"), one("gram"))
                elif i == 15:
                    pe.wait_ge(sem("values"), more("values"))
                    if GRAMS * (j + 1) > 0:
                        pe.wait_ge(sem("gram_read"), GRAMS * (j + 1))
                    if GRAMS * (j + 1) > 0:
                        pe.wait_ge(sem("gram_copied"), GRAMS * (j + 1))
                    batch(0, lambda c, h: S["gram"][half(1 - h), c, h, 0:C],
                              lambda c, h: S["uv"][half(1 - h), c, h, :]).then_inc(sem("inverse_pe"), one("inverse_pe"))
                elif 16 <= i < 16 + 3 * (LEVELS - 1):
                    level, q = divmod(i - 16, 3)
                    if q == 0:
                        pe.wait_ge(sem("inverse_dve"), more("inverse_dve"))
                        batch(2, lambda c, h: f_am[half(h), c, :], lambda c, h: f_x[half(h), c, :]).then_inc(sem("inverse_pe"), one("inverse_pe"))
                    elif q == 1:
                        pe.wait_ge(sem("inverse_act"), more("inverse_act"))
                        if level < LEVELS - 2:
                            batch(4, lambda c, h: S["xt"][half(h), c, :], lambda c, h: f_y1[half(h), c, :]).then_inc(sem("inverse_pe"), one("inverse_pe"))
                    else:
                        batch(2, lambda c, h: f_y1[half(h), c, :], lambda c, h: S["xt"][half(h), c, :]).then_inc(sem("inverse_pe"), one("inverse_pe"))

            def batch(bank, left, right):
                both = two_banks(bank)
                for c in range(CHUNKS):
                    for h in range(2):
                        ins = pe.matmul(both[half(h), c * C:(c + 1) * C], left(c, h), right(c, h), start=True, stop=True)
                return ins

            def state_in(j, s):
                d = j % 2
                S, c = sets[d], chunk_order(d)[s]
                if s == 0:
                    pe.wait_ge(sem("inverted"), more("inverted"))
                pe.wait_ge(sem("state"), more("state"))
                for h in range(2):
                    ins = pe.matmul(ps[half(h), 6, 0:C], S["kr"][half(h), c, 0, :], state[half(h), d, :],
                                    start=True, stop=True)
                ins.then_inc(sem("from_state"), one("from_state"))

            def solve(j, s):
                d = j % 2
                S, c = sets[d], chunk_order(d)[s]
                pe.wait_ge(sem("residual"), more("residual"))
                for h in range(2):
                    ins = pe.matmul(ps[half(h), 6, C:2 * C], S["xt"][half(h), c, :], w0_neg[half(h), d, :],
                                    start=True, stop=True)
                ins.then_inc(sem("solved"), one("solved"))
                if c < LAT // C:
                    if n["y"] > 0:
                        pe.wait_ge(sem("y_read"), n["y"])
                    for h in range(2):
                        pe.matmul(ps[half(h), 7, 0:C], state[half(h), d, :], S["kr"][half(h), c, 1, :],
                                  start=True, stop=False)

            def state_out(j, s):
                d = j % 2
                S, c = sets[d], chunk_order(d)[s]
                pe.wait_ge(sem("update"), more("update"))
                if s < CHUNKS - 1:
                    for h in range(2):
                        ins = pe.matmul(ps[half(h), 6, 2 * C:3 * C], S["bkn"][:, c, half(h)], S["uv"][:, c, h, :],
                                        start=True, stop=True)
                    ins.then_inc(sem("to_state"), one("to_state"))
                if c < LAT // C:
                    for h in range(2):
                        ins = pe.matmul(ps[half(h), 7, 0:C], S["uv"][:, c, h, :], S["gram"][:, c, h, C:2 * C],
                                        start=False, stop=True)
                    ins.then_inc(sem("y"), one("y"))

            def readout(p):
                pe.wait_ge(sem("read_dve"), more("read_dve"))
                n["read_dve"] += 2
                pe.matmul(ps[:, 0, :], head_ones, y_pair, start=True, stop=True).then_inc(sem("read_pe"), one("read_pe"))
                pe.matmul(ps[:, 1, :], head_ones, R[:, p, :], start=True, stop=True)
                for c in range(LAT // C):
                    for h in range(2):
                        pe.matmul(ps[half(h), 2, c * C:(c + 1) * C], V[half(1 - h), c, p, :],
                                  ccol("ident2", 0, C)[half(1 - h), :], start=True, stop=True)
                pe.matmul(ps[:, 3, :], lora2[:, 2, p * P:(p + 1) * P], gate_in, start=True, stop=True).then_inc(sem("read_pe"), one("read_pe"))
                pe.wait_ge(sem("read_act"), more("read_act"))
                pe.matmul(ps[:, 4, :], head_ones, square[:, 0, 0:LAT], start=True, stop=True).then_inc(sem("read_pe"), one("read_pe"))
                pe.wait_ge(sem("r_out"), more("r_out"))

            def mix_in(l):
                w = panel()
                columns(w, range(2), H, SEGM, ready="h_dve")
                for t in range(2):
                    accumulate(tile()[:, 0:CTX], lambda k: H[:, k, LAT + t * P:LAT + (t + 1) * P],
                               lambda k: w[:, k, CTX:2 * CTX])
                ready = "h_dve"
                for _ in range(3):
                    columns(panel(), range(4), H, SEG1, ready=ready)
                    ready = None
                rows(panel(), 0, P, H, range(LAT // P), 0)
                for i in range(8):
                    sums(head_ones, 1, 0, LAT if i < 6 else CTX)
                    if i < 4:
                        pe.wait_ge(sem("normed"), more("normed"))
                        pe.matmul(ps[:, 5, :], rotate, q2[:, i, :], start=True, stop=True).then_inc(sem("rotated"), one("rotated"))

            def conv(l):
                pe.wait_ge(sem("tapped"), more("tapped"))
                sums(ones[:, :], 3, 0, LAT, "conv")
                sums(ones[:, :], 3, 0, LAT)

            skip = lambda *a: None
            model(dict(load=load, mod=mod, gains=skip, norm_mod=norm_mod, even_in=even_in, attention=attention,
                       project=project, post=post, mlp=mlp, odd_in=odd_in, prepare=prepare, state_in=state_in,
                       solve=solve, state_out=state_out, readout=readout, odd_out=skip, tables=skip,
                       norm_vec=norm_vec, swiglu=swiglu, half_step=skip, mix_in=mix_in, conv=conv, store=skip))

        @block.scalar
        def _(act):
            n, more, one = counting()
            sigmoid_used = [0, 0]

            def load():
                act.wait_ge(sem("small_in"), 48)
                act.activation(silu_c[:, :, :], raw_c[:, :, :], ACT.Sigmoid).then_inc(sem("sigmoid_c"), one("sigmoid_c"))
                n["source"] = "load"

            def squares(src, count, lo, hi, ready):
                if sigmoid_used[-1] > 0:
                    act.wait_ge(sem("tile_free"), sigmoid_used[-1])
                for c in range(count):
                    ready(c)
                    if n["sq"] - 1 + n["plain_sums"] > 0:
                        act.wait_ge(sem("summed"), n["sq"] - 1 + n["plain_sums"])
                    act.activation(square[:, n["sq"] % 2, 0:hi - lo], src(c), ACT.Square).then_inc(sem("square"), one("square"))
                    n["sq"] += 1
                act.wait_ge(sem("var"), more("var"))
                act.activation(rstd[:, 0:hi - lo], rstd[:, 0:hi - lo], ACT.Sqrt).then_inc(sem("std"), one("std"))

            def source():
                kind = n["source"]
                if kind == "load":
                    act.wait_ge(sem("x_in"), 16)
                    return lambda c: None
                if kind == "x_chunk":
                    base = n["x_chunk"] - KD
                    return lambda c: act.wait_ge(sem("x_chunk"), base + c + 1)
                base = n["tile"] - KD
                return lambda c: act.wait_ge(sem("tile_free"), base + c + 1)

            def mod(i, lo, hi):
                n["tile"] += hi - lo

            def norm_mod(i, which):
                hi = TOK if (i, which) != (1, 2) else LAT
                squares(lambda c: X[:, c, 0:hi], KD, 0, hi, source())
                act.wait_ge(sem("gains"), more("gains")) if which == 0 and i == 0 else None
                if (i, which) != (0, 0):
                    if 1 + 1 if i == 0 else 4 > 0:
                        act.wait_ge(sem("gains"), 1 + 1 if i == 0 else 4)
                for c in range(KD):
                    act.wait_ge(sem("scaled"), more("scaled"))
                    for v, (a, b) in enumerate(((0, LAT), (LAT, TOK))):
                        if b <= hi:
                            ins = act.activation(H[:, c, a:b], H[:, c, a:b], ACT.Identity,
                                                 bias=mod_col(i, 3 * (which // 2), v, c), scale=gain[:, i, which, v, c:c + 1])
                    ins.then_inc(sem("h_act"), one("h_act"))

            def mod_col(i, part, v, c):
                return mod_sb[:, i, v, part * KD + c:part * KD + c + 1]

            def norm_vec(lo, hi, name, l, src):
                if lo == LAT:
                    act.wait_ge(sem("mem_in"), 16)
                    ready = lambda c: None
                else:
                    ready = source()
                squares(lambda c: X[:, c, lo:hi], KD, lo, hi, ready)
                if name == "final_norm":
                    n["x_chunk"] += KD
                    n["source"] = "x_chunk"

            def even_in():
                n["tile"] += 24 + TOK // P + 8 + 8

            def attention(units, l):
                base = n["unit"]
                for i in range(len(units) + 2):
                    if i < len(units):
                        unit, u = units[i], base + i
                        w = unit["width"]
                        act.wait_ge(sem("row_max"), more("row_max"))
                        act.activation(probs[:, u % 3, 0:w], probs[:, u % 3, 0:w], ACT.Exp,
                                           bias=stat[:, 4 * (u % 3) + 1:4 * (u % 3) + 2],
                                           accum_out=stat[:, 4 * (u % 3) + 2:4 * (u % 3) + 3]).then_inc(sem("exped"), one("exped"))
                        if unit["sink"] is not None:
                            act.activation(stat[:, 4 * (u % 3) + 3:4 * (u % 3) + 4], unit["sink"], ACT.Exp,
                                               bias=stat[:, 4 * (u % 3) + 1:4 * (u % 3) + 2]).then_inc(sem("exped_sink"), one("exped_sink"))
                    if i >= 2:
                        unit, u = units[i - 2], base + i - 2
                        w = unit["width"]
                        act.wait_ge(sem("turned"), more("turned"))
                        if u - 1 > 0:
                            act.wait_ge(sem("output"), u - 1)
                        act.copy(probsT[:, u % 2, 0:w], turned_ps(w)).then_inc(sem("turned_copy"), one("turned_copy"))
                n["unit"] += len(units)

            def project(count, segs, src, dest, ready):
                n["tile"] += 4 * count * len(segs)
                n["source"] = "tile"
                n["last"] = len(segs)

            def post(src, i, which):
                hi = TOK if i == 0 else LAT
                nseg = n["last"]
                base = n["tile"] - KD * nseg
                squares(lambda c: src[:, c, 0:hi], KD, 0, hi, lambda c: act.wait_ge(sem("tile_free"), base + nseg * (c + 1)))
                n["x_chunk"] += KD
                n["source"] = "x_chunk"

            def mlp(segs, beside):
                for step, (kind, g) in enumerate(mlp_steps(len(FF1_GROUPS))):
                    if beside and step in MOD_STEPS:
                        mod(1, 2 * (step - MOD_STEPS[0]), 2 * (step - MOD_STEPS[0]) + 2)
                    for c in range(8):
                        for a, b in segs:
                            if kind == "up":
                                if n["tile"] + 1 > 0:
                                    act.wait_ge(sem("tile_done"), n["tile"] + 1)
                                act.activation(hidden1[g % 2][:, c, a:b], ps[:, n["tile"] % 4, 0:b - a], ACT.Relu).then_inc(sem("relu"), one("relu"))
                            n["tile"] += 1
                n["last"] = len(segs)

            def swiglu():
                for kind, g in mlp_steps(len(FF2_GROUPS)):
                    if kind == "down":
                        n["tile"] += 8
                        continue
                    for c in range(FF2_GROUPS[g]):
                        if sigmoid_used[-2] > 0:
                            act.wait_ge(sem("tile_free"), sigmoid_used[-2])
                        if n["tile"] + 1 > 0:
                            act.wait_ge(sem("tile_done"), n["tile"] + 1)
                        sigmoid_used.append(n["tile"] + 1)
                        act.activation(sig[:, n["sig"] % 2, :], ps[:, n["tile"] % 4, :], ACT.Sigmoid).then_inc(sem("sigmoid"), one("sigmoid"))
                        n["sig"] += 1
                        n["tile"] += 2

            def half_step():
                n["x_chunk"] += KD
                n["source"] = "x_chunk"

            def odd_in():
                base = n["tile"]
                n["tile"] += 5 + 16 + 2 * CHUNKS + 8
                if 6 * KD > 0:
                    act.wait_ge(sem("mix"), 6 * KD)
                if base + 5 > 0:
                    act.wait_ge(sem("tile_free"), base + 5)
                act.activation(decay_in, square[:, 0, :], ACT.Tanh).then_inc(sem("lora"), one("lora"))
                act.copy(a_in, square[:, 1, :]).then_inc(sem("lora"), one("lora"))
                act.activation(gate_in, rstd[:, 0:LAT], ACT.Sigmoid).then_inc(sem("lora"), one("lora"))
                if 3 > 0:
                    act.wait_ge(sem("lora"), 3)

            def half(h):
                return slice(C * h, C * h + C)

            def prepare(j, i):
                p, d = divmod(j, 2)
                S = sets[d]
                if i == 0 and d == 0:
                    act.wait_ge(sem("feature_dve"), more("feature_dve"))
                    act.activation(square[:, 0, :], f_kk, ACT.Square).then_inc(sem("feature_act"), one("feature_act"))
                    n["feature_pe"] += 1
                elif i == 1 and d == 0:
                    act.wait_ge(sem("feature_dve"), more("feature_dve"))
                    act.activation(rstd[:, :], rstd[:, :], ACT.Sqrt).then_inc(sem("feature_act"), one("feature_act"))
                elif i == 2:
                    act.wait_ge(sem("feature_pe"), more("feature_pe"))
                    if j > 0:
                        act.wait_ge(sem("inverted"), j)
                    act.activation(f_cs, two_banks(0), ACT.Sigmoid, bias=vcol(f"w0{d}", p)).then_inc(sem("feature_act"), one("feature_act"))
                elif i == 3:
                    act.wait_ge(sem("feature_pe"), more("feature_pe"))
                    act.activation(f_a, two_banks(0), ACT.Sigmoid, bias=vcol(f"a0{d}", p)).then_inc(sem("feature_act"), one("feature_act"))
                elif i == 4:
                    act.wait_ge(sem("feature_dve"), more("feature_dve"))
                    act.activation(f_inc, f_cs, ACT.Exp, scale=-E_HALF).then_inc(sem("feature_act"), one("feature_act"))
                    act.activation(f_inv, f_cs, ACT.Exp, scale=E_HALF).then_inc(sem("feature_act"), one("feature_act"))
                elif 9 <= i < 9 + GRAMS:
                    g = i - 9
                    c = 2 * g
                    act.wait_ge(sem("gram"), more("gram"))
                    bank = ps[:, 4 + g % 2, :]
                    act.copy(S["bkn"][:, c:c + 2, :], bank[:, P:3 * P].rearrange("p (a b) -> p a b", a=2))
                    act.copy(f_x[:, c:c + 2, :], bank[:, 0:P].rearrange("p (a b) -> p a b", a=2)).then_inc(sem("gram_copied"), one("gram_copied"))
                    act.wait_ge(sem("gram_read"), more("gram_read"))
                    for h in range(2):
                        ins = act.copy(f_at[half(h), c:c + 2, :], S["gram"][half(h), c:c + 2, h, 0:C])
                    ins.then_inc(sem("coupling"), one("coupling"))
                elif i == 15:
                    n["inverse_pe"] += 1
                elif 16 <= i < 16 + 3 * (LEVELS - 1):
                    level, q = divmod(i - 16, 3)
                    if q == 0:
                        act.wait_ge(sem("inverse_pe"), more("inverse_pe"))
                        act.copy(f_y1.rearrange("p c t -> p (c t)"), two_banks(2)).then_inc(sem("inverse_act"), one("inverse_act"))
                    elif q == 2 or level < LEVELS - 2:
                        n["inverse_pe"] += 1

            def solve(j, s):
                d = j % 2
                S, c = sets[d], chunk_order(d)[s]
                act.wait_ge(sem("solved"), more("solved"))
                for h in range(2):
                    ins = act.copy(S["uv"][half(h), c, h, :], ps[half(h), 6, C:2 * C])
                ins.then_inc(sem("update"), one("update"))

            def readout(p):
                act.wait_ge(sem("read_pe"), more("read_pe", 2))
                act.copy(v_turned, ps[:, 2, :]).then_inc(sem("read_act_v"), one("read_act_v"))
                act.wait_ge(sem("read_dve"), more("read_dve", 2))
                act.activation(square[:, 0, 0:LAT], y_pair, ACT.Square).then_inc(sem("read_act"), one("read_act"))
                n["read_pe"] += 1
                act.wait_ge(sem("read_dve"), more("read_dve"))
                act.activation(rstd[:, 0:LAT], rstd[:, 0:LAT], ACT.Sqrt).then_inc(sem("read_act_root"), one("read_act_root"))

            def tables():
                act.wait_ge(sem("angle"), more("angle"))
                act.activation(rope[:, 1, :], rope_tmp[:, 0, :], ACT.Sin).then_inc(sem("sine"), one("sine"))
                act.activation(rope[:, 0, :], rope_tmp[:, 0, :], ACT.Sin, scale=0.5).then_inc(sem("sine"), one("sine"))

            def mix_in(l):
                n["tile"] += 4
                base = n["tile"]
                for m in (1, 3, 5):
                    if sigmoid_used[-2] > 0:
                        act.wait_ge(sem("tile_free"), sigmoid_used[-2])
                    if base + m + 1 > 0:
                        act.wait_ge(sem("tile_done"), base + m + 1)
                    sigmoid_used.append(base + m + 1)
                    act.activation(sig[:, n["sig"] % 2, :], ps[:, (base + m) % 4, :], ACT.Sigmoid).then_inc(sem("sigmoid"), one("sigmoid"))
                    n["sig"] += 1
                n["tile"] += 12 + LAT // P
                for i in range(8):
                    src = q2[:, i, :] if i < 6 else mk2[:, i - 6, :]
                    squares(lambda c: src, 1, 0, LAT if i < 6 else CTX, lambda c: act.wait_ge(sem("tile_free"), n["tile"]))

            def conv(l):
                act.wait_ge(sem("tapped"), more("tapped"))
                n["plain_sums"] += 3
                n["var"] += 1
                squares(lambda c: conv_y[:, c, :], 3, 0, LAT, lambda c: act.wait_ge(sem("centred"), more("centred")))
                for c in range(3):
                    act.wait_ge(sem("conv_z"), more("conv_z"))
                    act.activation(sig[:, c % 2, :] if c < 2 else rstd[:, 0:LAT], conv_y[:, c, :], ACT.Sigmoid).then_inc(sem("conv_sigmoid"), one("conv_sigmoid"))

            skip = lambda *a: None
            model(dict(load=load, mod=mod, gains=skip, norm_mod=norm_mod, even_in=even_in, attention=attention,
                       project=project, post=post, mlp=mlp, odd_in=odd_in, prepare=prepare, state_in=skip, solve=solve,
                       state_out=skip, readout=readout, odd_out=skip, tables=tables, norm_vec=norm_vec, swiglu=swiglu,
                       half_step=half_step, mix_in=mix_in, conv=conv, store=skip))

        @block.vector
        def _(dve):
            n, more, one = counting()

            def settle(ins):
                ins.then_inc(sem("own"), one("own"))
                dve.wait_ge(sem("own"), n["own"])

            def tile():
                dve.wait_ge(sem("tile_done"), more("tile_done"))
                n["tile"] += 1
                return ps[:, (n["tile"] - 1) % 4, :]

            def load():
                dve.wait_ge(sem("small_in"), 48)
                settle(dve.tensor_scalar(omka[:, :], vcol("ka", 0, KD), -1.0, 1.0, ALU.mult, ALU.add))
                dve.wait_ge(sem("sigmoid_c"), more("sigmoid_c"))
                dve.tensor_tensor(silu_c[:, :, :], silu_c[:, :, :], raw_c[:, :, :], ALU.mult).then_inc(sem("silu"), one("silu"))

            def mod(i, lo, hi):
                for j in range(lo, hi):
                    bank = tile()
                    b = vcol(f"ada_b{i}", 4 * j, 4)
                    for v in range(2):
                        ins = dve.tensor_tensor(mod_sb[:, i, v, 4 * j:4 * j + 4], bank[:, v:8:2], b, ALU.add)
                    ins.then_inc(sem("tile_free"), one("tile_free"))

            def gains(i, part):
                if n["tile"] > 0:
                    dve.wait_ge(sem("tile_free"), n["tile"])
                for which in ((0,), (1, 2, 3))[part]:
                    for v in range(2):
                        g = vcol(f"norm_g{i}{which}", 0, KD)
                        chunk = (1, 2, 4, 5)[which]
                        m = mod_sb[:, i, v, chunk * KD:(chunk + 1) * KD]
                        ins = dve.scalar_tensor_tensor(gain[:, i, which, v, :], m, 0.0 if which % 2 else 1.0, g, ALU.add,
                                                       ALU.mult)
                ins.then_inc(sem("gains"), one("gains"))
                dve.wait_ge(sem("gains"), n["gains"])

            def inverse_root(count, lo, hi, mean, eps, op=ALU.add):
                dve.wait_ge(sem("summed"), more("summed", count))
                r = rstd[:, 0:hi - lo]
                dve.tensor_scalar(r, norm_psum(lo, hi), mean, eps, ALU.mult, op).then_inc(sem("var"), one("var"))
                dve.wait_ge(sem("std"), more("std"))
                settle(dve.reciprocal(r, r))
                return r

            def norm_mod(i, which):
                hi = TOK if (i, which) != (1, 2) else LAT
                r = inverse_root(KD, 0, hi, 1.0 / D, 1e-6)
                for c in range(KD):
                    dve.tensor_tensor(H[:, c, 0:hi], X[:, c, 0:hi], r, ALU.mult).then_inc(sem("scaled"), one("scaled"))
                n["h_act"] += KD

            def norm_vec(lo, hi, name, l, src):
                r = inverse_root(KD, lo, hi, 1.0 / D, 1e-6)
                dest, signal = (X, "x_chunk") if name == "final_norm" else (H, "h_dve")
                for c in range(KD):
                    dve.scalar_tensor_tensor(dest[:, c, lo:hi], X[:, c, lo:hi], vcol(f"{name}{l}", c), r, ALU.mult,
                                                 ALU.mult).then_inc(sem(signal), one(signal))
                dve.wait_ge(sem(signal), n[signal])

            def copies(dest, ms, segs):
                for m in ms:
                    for a, b in segs:
                        dve.tensor_copy(dest[:, m, a:b], tile()[:, 0:b - a]).then_inc(sem("tile_free"), one("tile_free"))

            def even_in():
                u, s0, s1 = pool_buf
                GAP = 8
                parts = ((0, LAT, GAP), (LAT, TOK, GAP + LAT + GAP))
                settle(dve.memset(u, 0.0))
                for g, w in enumerate(POOL_WINDOWS):
                    for a, b, o in parts:
                        dve.tensor_copy(u[:, o:o + b - a], tile()[:, 0:b - a]).then_inc(sem("tile_free"), one("tile_free"))
                    dve.wait_ge(sem("tile_free"), n["tile_free"])
                    src, width = u, 1
                    while width < w:
                        dest = s0 if src is not s0 else s1
                        m = 792 - 2 * width + 1
                        settle(dve.tensor_tensor(dest[:, 0:m], src[:, 0:m], src[:, width:width + m], ALU.add))
                        src, width = dest, 2 * width
                    edge = ccol("pool_edge", 2 * (w // 2 - 1), w)
                    diff = Y[:, 4 + g, :]
                    for a, b, o in parts:
                        ins = dve.tensor_scalar(diff[:, a:b], src[:, o - w // 2:o - w // 2 + b - a], 1.0 / w, None, ALU.mult)
                    settle(ins)
                    for a, b, o in parts:
                        dve.tensor_tensor(diff[:, a:a + w // 2], diff[:, a:a + w // 2], edge[:, 0:w // 2], ALU.mult)
                        ins = dve.tensor_tensor(diff[:, b - w // 2:b], diff[:, b - w // 2:b], edge[:, w // 2:w], ALU.mult)
                    settle(ins)
                    for a, b, o in parts:
                        ins = dve.tensor_tensor(diff[:, a:b], diff[:, a:b], u[:, o:o + b - a], ALU.subtract)
                    ins.then_inc(sem("pooled"), one("pooled"))
                    dve.wait_ge(sem("pooled"), n["pooled"])
                mod(0, 4, 6)
                copies(qT, range(4), SEG2)
                mod(0, 6, 8)
                copies(kT, range(4), SEG2)
                mod(0, 8, 10)
                for t in range(TOK // P):
                    dve.tensor_copy(vN[:, t, :], tile()).then_inc(sem("tile_free"), one("tile_free"))
                mod(0, 10, 12)
                for g in range(4):
                    for a, b in SEG2:
                        dve.tensor_scalar(Y[:, g, a:b], tile()[:, 0:b - a], vcol("pool_scale", g), None, ALU.mult).then_inc(sem("tile_free"), one("tile_free"))

            def conv_tap(l, tap):
                for c in range(3):
                    w, src = vcol(f"conv_w{l}", c * TAPS + tap), conv_in[:, c, tap:tap + LAT]
                    if tap == 0:
                        ins = dve.tensor_scalar(conv_y[:, c, :], src, w, vcol(f"conv_b{l}", c), ALU.mult, ALU.add)
                    else:
                        dve.wait_ge(sem("tap"), n["tap"] - 2)
                        ins = dve.scalar_tensor_tensor(conv_y[:, c, :], src, w, conv_y[:, c, :], ALU.mult, ALU.add)
                    ins.then_inc(sem("tap"), one("tap"))

            def attention(units, l):
                base = n["unit"]
                scale = C ** -0.5
                for i in range(len(units) + 4):
                    if i < len(units):
                        unit, u = units[i], base + i
                        w, o = unit["width"], 4 * (u % 3)
                        dve.wait_ge(sem("scores"), more("scores"))
                        if u - 2 > 0:
                            dve.wait_ge(sem("turned"), u - 2)
                        S, raw = probs[:, u % 3, :], scores_ps(u, w)
                        wb = 0
                        if unit["bias"] is not None:
                            wb = min(w, LAT)
                            if unit["bias_head"] is not None:
                                h = unit["bias_head"]
                                dve.wait_ge(sem(f"bias{h % 2}"), 16 * (h // 2 + 1))
                            ins = dve.scalar_tensor_tensor(S[:, 0:wb], raw[:, 0:wb], scale, unit["bias"], ALU.mult, ALU.add)
                        if wb < w:
                            ins = dve.tensor_scalar(S[:, wb:w], raw[:, wb:w], scale, None, ALU.mult)
                        ins.then_inc(sem("scored"), one("scored"))
                        dve.wait_ge(sem("scored"), n["scored"])
                        settle(dve.tensor_reduce(stat[:, o:o + 1], S[:, 0:w], AX.X, ALU.max))
                        if unit["sink"] is not None:
                            settle(dve.tensor_tensor(stat[:, o:o + 1], stat[:, o:o + 1], unit["sink"], ALU.max))
                        dve.tensor_scalar(stat[:, o + 1:o + 2], stat[:, o:o + 1], -1.0, None, ALU.mult).then_inc(sem("row_max"), one("row_max"))
                    if 1 <= i <= len(units):
                        unit, u = units[i - 1], base + i - 1
                        w, o = unit["width"], 4 * (u % 3)
                        dve.wait_ge(sem("exped"), more("exped"))
                        if unit["sink"] is not None:
                            dve.wait_ge(sem("exped_sink"), more("exped_sink"))
                            settle(dve.tensor_tensor(stat[:, o + 2:o + 3], stat[:, o + 2:o + 3], stat[:, o + 3:o + 4], ALU.add))
                        settle(dve.reciprocal(stat[:, o + 2:o + 3], stat[:, o + 2:o + 3]))
                        dve.tensor_scalar(probs[:, u % 3, 0:w], probs[:, u % 3, 0:w], stat[:, o + 2:o + 3], None,
                                              ALU.mult).then_inc(sem("probs"), one("probs"))
                    if l is not None and i < TAPS:
                        conv_tap(l, i)
                    if i >= 4:
                        unit, u = units[i - 4], base + i - 4
                        b = unit["base"]
                        dve.wait_ge(sem("output"), more("output"))
                        dve.tensor_copy(unit["dest"], ps[b:b + C, 6 + u % 2, 0:P]).then_inc(sem("attended"), one("attended"))
                n["unit"] += len(units)

            def project(count, segs, src, dest, ready):
                for c in range(4 * count):
                    for a, b in segs:
                        bank = tile()[:, 0:b - a]
                        if dest is None:
                            ins = dve.tensor_tensor(X[:, c, a:b], bank, X[:, c, a:b], ALU.add)
                        else:
                            ins = dve.tensor_copy(dest[:, c, a:b], bank)
                        ins.then_inc(sem("tile_free"), one("tile_free"))

            def post(src, i, which):
                streams = ((0, LAT), (LAT, TOK)) if i == 0 else ((0, LAT),)
                hi = streams[-1][1]
                r = inverse_root(KD, 0, hi, 1.0 / D, 1e-6)
                if (i, which) == (1, 1):
                    dve.wait_ge(sem("x_back"), 16)
                for c in range(KD):
                    for v, (a, b) in enumerate(streams):
                        ins = dve.scalar_tensor_tensor(src[:, c, a:b], src[:, c, a:b], gain[:, i, which, v, c:c + 1],
                                                       r[:, a:b], ALU.mult, ALU.mult)
                    ins.then_inc(sem("gated"), one("gated"))
                for c in range(KD):
                    dve.wait_ge(sem("gated"), n["gated"] - KD + c + 1)
                    dve.tensor_tensor(X[:, c, 0:hi], X[:, c, 0:hi], src[:, c, 0:hi], ALU.add).then_inc(sem("x_chunk"), one("x_chunk"))

            def add_up(c, a, b, first):
                bank = tile()[:, 0:b - a]
                if first:
                    dve.tensor_copy(Y[:, c, a:b], bank).then_inc(sem("tile_free"), one("tile_free"))
                else:
                    dve.tensor_tensor(Y[:, c, a:b], bank, Y[:, c, a:b], ALU.add).then_inc(sem("tile_free"), one("tile_free"))

            def mlp(segs, beside):
                for step, (kind, g) in enumerate(mlp_steps(len(FF1_GROUPS))):
                    if beside and step in MOD_STEPS:
                        mod(1, 2 * (step - MOD_STEPS[0]), 2 * (step - MOD_STEPS[0]) + 2)
                    for c in range(8):
                        for a, b in segs:
                            if kind == "up":
                                bank = tile()[:, 0:b - a]
                                dve.wait_ge(sem("relu"), more("relu"))
                                hid = hidden1[g % 2][:, c, a:b]
                                dve.tensor_tensor(hid, hid, bank, ALU.mult).then_inc(sem("tile_free"), one("tile_free"))
                            else:
                                add_up(c, a, b, g == 0)

            def swiglu():
                for kind, g in mlp_steps(len(FF2_GROUPS)):
                    for c in range(8 if kind == "down" else FF2_GROUPS[g]):
                        if kind == "up":
                            bank = tile()
                            dve.wait_ge(sem("sigmoid"), more("sigmoid"))
                            hid = hidden2[g % 2][:, c, :]
                            dve.tensor_tensor(hid, bank, sig[:, n["sig"] % 2, :], ALU.mult).then_inc(sem("tile_free"), one("tile_free"))
                            n["sig"] += 1
                            gate = tile()
                            dve.wait_ge(sem("tile_free"), n["tile_free"])
                            dve.tensor_tensor(hid, gate, hid, ALU.mult).then_inc(sem("tile_free"), one("tile_free"))
                        else:
                            add_up(c, 0, LAT, g == 0)

            def half_step():
                if n["tile_free"] > 0:
                    dve.wait_ge(sem("tile_free"), n["tile_free"])
                for c in range(KD):
                    dve.scalar_tensor_tensor(X[:, c, 0:LAT], Y[:, c, 0:LAT], 0.5, X[:, c, 0:LAT], ALU.mult, ALU.add).then_inc(sem("x_chunk"), one("x_chunk"))

            def odd_in():
                if n["h_act"] > 0:
                    dve.wait_ge(sem("h_act"), n["h_act"])
                for a, b in ((0, LAT), (LAT, TOK)):
                    dve.tensor_tensor(XX[:, :, a + 1:b - 1], H[:, :, a:b - 2], H[:, :, a + 2:b], ALU.add)
                    dve.tensor_copy(XX[:, :, a:a + 1], H[:, :, a + 1:a + 2])
                    ins = dve.tensor_copy(XX[:, :, b - 1:b], H[:, :, b - 2:b - 1])
                settle(ins)
                settle(dve.scalar_tensor_tensor(XX, XX, 0.5, H, ALU.mult, ALU.subtract))

                def mix(mu, dest, hi):
                    for c in range(KD):
                        dve.scalar_tensor_tensor(dest[:, c, 0:hi], XX[:, c, 0:hi], vcol(f"mu{mu}", c), H[:, c, 0:hi],
                                                     ALU.mult, ALU.add).then_inc(sem("mix"), one("mix"))

                def raw(dest, segs):
                    for a, b in segs:
                        dve.tensor_copy(dest[:, a:b], tile()[:, 0:b - a]).then_inc(sem("tile_free"), one("tile_free"))

                mix(1, K, TOK)
                mix(4, MIX, TOK)
                raw(square[:, 0, :], SEG2)
                mix(5, K, LAT)
                raw(square[:, 1, :], SEG2)
                mix(2, MIX, TOK)
                raw(rstd[:, :], SEG1)
                copies(K, range(8), SEG2)
                mix(3, MIX, TOK)
                dve.wait_ge(sem("mix"), n["mix"])
                mix(0, XX, LAT)
                dve.wait_ge(sem("x_saved"), 16)
                for lo in (C, 0):
                    for c in range(CHUNKS):
                        dve.tensor_copy(V[lo:lo + C, c, :, :].rearrange("p a b -> p (a b)"), tile()[lo:lo + C, :]).then_inc(sem("tile_free"), one("tile_free"))
                dve.wait_ge(sem("mix"), n["mix"])
                copies(R, range(8), SEG1)
                dve.wait_ge(sem("tile_free"), n["tile_free"])
                settle(dve.memset(reset[:, :], 1.0))
                settle(dve.memset(chunked(reset[:, :])[:, :, 0:1], 0.0))

            def half(h):
                return slice(C * h, C * h + C)

            def each_chunk(m, count):
                return m.unsqueeze(1).broadcast_to([m.shape[0], count, m.shape[1]])

            def prepare(j, i):
                p, d = divmod(j, 2)
                S = sets[d]
                lat = LAT // C
                inc, inv = chunked(f_inc), chunked(f_inv)
                kk, b, kd = chunked(f_kk), chunked(f_b), chunked(f_kd)
                lower, upper = ("level", "level_t") if d == 0 else ("level_t", "level")
                if i == 0 and d == 0:
                    dve.tensor_scalar(f_kk, K[:, p, :], vcol("kk", p), None, ALU.mult).then_inc(sem("feature_dve"), one("feature_dve"))
                elif i == 1 and d == 0:
                    dve.wait_ge(sem("feature_pe"), more("feature_pe"))
                    dve.tensor_scalar(rstd[:, :], two_banks(0), 1e-24, None, ALU.max).then_inc(sem("feature_dve"), one("feature_dve"))
                elif i == 2 and d == 0:
                    dve.wait_ge(sem("feature_act"), more("feature_act", 2))
                    settle(dve.reciprocal(rstd[:, :], rstd[:, :]))
                    settle(dve.tensor_tensor(f_kk, f_kk, rstd[:, :], ALU.mult))
                elif i == 3:
                    dve.wait_ge(sem("feature_act"), more("feature_act"))
                    line = f_cs if d == 0 else f_cs[:, ::-1]
                    dve.tensor_tensor_scan(line, reset[:, :], line, 0.0, ALU.mult, ALU.add).then_inc(sem("feature_dve"), one("feature_dve"))
                    n["feature_pe"] += 2
                elif i == 4:
                    dve.wait_ge(sem("feature_act"), more("feature_act"))
                    settle(dve.tensor_tensor(f_b, f_kk, f_a, ALU.mult))
                elif i == 5:
                    dve.wait_ge(sem("feature_act"), more("feature_act"))
                    to, of = (slice(1, C), slice(0, C - 1)) if d == 0 else (slice(0, C - 1), slice(1, C))
                    e = slice(0, 1) if d == 0 else slice(C - 1, C)
                    last = slice(C - 1, C) if d == 0 else slice(0, 1)
                    dve.tensor_tensor(S["kr"][:, :, 0, to], kk[:, :, to], inc[:, :, of], ALU.mult)
                    dve.tensor_copy(S["kr"][:, :, 0, e], kk[:, :, e])
                    dve.tensor_tensor(S["kr"][:, 0:lat, 1, :], chunked(R[:, p, :]), inc[:, 0:lat, :], ALU.mult)
                    settle(dve.tensor_copy(chunk_decay[:, d, :].unsqueeze(2), inc[:, :, last]))
                elif i == 6:
                    settle(dve.tensor_scalar(f_kd, f_a, vcol("ka", p), omka[:, p:p + 1], ALU.mult, ALU.add))
                    settle(dve.tensor_tensor(f_kd, f_kd, K[:, p, :], ALU.mult))
                    if d == 0:
                        settle(dve.tensor_copy(k_sum, f_kd[:, 0:LAT]))
                    else:
                        settle(dve.tensor_tensor(k_sum, k_sum, f_kd[:, 0:LAT], ALU.add))
                        settle(dve.scalar_tensor_tensor(R[:, p, :], k_sum, vcol("rk", p), R[:, p, :], ALU.mult, ALU.mult))
                elif i == 7:
                    dve.wait_ge(sem("feature_act"), more("feature_act"))
                    for h in range(2):
                        dve.tensor_tensor(S["bk"][half(h), :, h, :], b[half(h)], inv[half(h)], ALU.mult)
                elif i == 8:
                    for h in range(2):
                        ins = dve.tensor_tensor(S["bk"][half(h), :, 1 - h, :], kd[half(h)], inv[half(h)], ALU.mult)
                    ins.then_inc(sem("keys"), one("keys"))
                elif 9 <= i < 9 + GRAMS:
                    g = i - 9
                    c = 2 * g
                    dve.wait_ge(sem("gram"), more("gram"))
                    wd = 2 * C if c < lat else C
                    for h in range(2):
                        raw = ps[:, 2 * (g % 2) + h, 0:4 * C].rearrange("p (a b) -> p a b", a=2)[:, :, 0:wd]
                        ins = dve.tensor_tensor(S["gram"][:, c:c + 2, h, 0:wd], raw,
                                                each_chunk(ccol("gram_mask", 2 * C * d, wd), 2), ALU.mult)
                    ins.then_inc(sem("gram_read"), one("gram_read"))
                elif i == 15:
                    dve.wait_ge(sem("coupling"), more("coupling", GRAMS))
                    dve.wait_ge(sem("inverse_pe"), more("inverse_pe"))
                    dve.tensor_scalar(S["gram"][:, :, 0, 0:C], chunked(two_banks(0)), -1.0, None, ALU.mult)
                    dve.wait_ge(sem("gram_copied"), more("gram_copied", GRAMS))
                    settle(dve.scalar_tensor_tensor(f_x, f_x, -1.0, each_chunk(ccol(lower, 0, C), CHUNKS), ALU.mult, ALU.mult))
                    dve.tensor_tensor(f_x, f_x, each_chunk(ccol("ident2", 0, C), CHUNKS), ALU.add)
                    settle(dve.tensor_tensor(f_am, f_at, each_chunk(ccol(upper, 0, C), CHUNKS), ALU.mult))
                    settle(dve.tensor_tensor(S["xt"], each_chunk(ccol("ident2", 0, C), CHUNKS), f_am, ALU.subtract))
                elif 16 <= i < 16 + 3 * (LEVELS - 1):
                    level, q = divmod(i - 16, 3)
                    if q == 0:
                        dve.tensor_tensor(f_am, f_at, each_chunk(ccol(upper, C * (level + 1), C), CHUNKS), ALU.mult).then_inc(sem("inverse_dve"), one("inverse_dve"))
                        n["inverse_pe"] += 1
                    elif q == 1:
                        if level < LEVELS - 2:
                            dve.wait_ge(sem("inverse_pe"), more("inverse_pe"))
                            settle(dve.tensor_tensor(f_x, f_x, chunked(two_banks(4)), ALU.subtract))
                    else:
                        dve.wait_ge(sem("inverse_pe"), more("inverse_pe"))
                        ins = dve.tensor_tensor(S["xt"], S["xt"], chunked(two_banks(2)), ALU.subtract)
                        if level == LEVELS - 2:
                            ins.then_inc(sem("inverted"), one("inverted"))
                        else:
                            settle(ins)

            def state_in(j, s):
                d = j % 2
                S, c = sets[d], chunk_order(d)[s]
                if s == 0:
                    dve.memset(state[:, d, :], 0.0).then_inc(sem("state"), one("state"))
                dve.wait_ge(sem("state"), n["state"])
                dve.tensor_scalar(state_dec[:, d, :], state[:, d, :], chunk_decay[:, d, c:c + 1], None, ALU.mult)
                dve.wait_ge(sem("from_state"), more("from_state"))
                dve.scalar_tensor_tensor(w0_neg[:, d, :], ps[:, 6, 0:C], -1.0, S["gram"][:, c, 0, 0:C], ALU.mult,
                                             ALU.add).then_inc(sem("residual"), one("residual"))

            def state_out(j, s):
                d = j % 2
                S, c = sets[d], chunk_order(d)[s]
                if s < CHUNKS - 1:
                    dve.wait_ge(sem("to_state"), more("to_state"))
                    dve.wait_ge(sem("residual"), n["residual"])
                    dve.scalar_tensor_tensor(state[:, d, :], ps[:, 6, 2 * C:3 * C], chunk_decay[:, d, c:c + 1],
                                                 state_dec[:, d, :], ALU.mult, ALU.add).then_inc(sem("state"), one("state"))
                if c < LAT // C:
                    dve.wait_ge(sem("y"), more("y"))
                    y, raw = y_pair[:, c * C:(c + 1) * C], ps[:, 7, 0:C]
                    if d == 0:
                        dve.tensor_copy(y, raw).then_inc(sem("y_read"), one("y_read"))
                    else:
                        dve.wait_ge(sem("y_read"), n["y_read"])
                        dve.tensor_tensor(y, y, raw, ALU.add).then_inc(sem("y_read"), one("y_read"))

            def readout(p):
                dve.wait_ge(sem("y_read"), n["y_read"])
                dve.tensor_copy(stat[:, 15:16], y_pair[:, 0:1]).then_inc(sem("read_dve"), one("read_dve"))
                dve.wait_ge(sem("read_pe"), more("read_pe"))
                dve.scalar_tensor_tensor(y_pair, ps[:, 0, :], -1.0 / C, y_pair, ALU.mult, ALU.add).then_inc(sem("read_dve"), one("read_dve"))
                dve.wait_ge(sem("read_pe"), more("read_pe", 2))
                dve.tensor_scalar(rstd[:, 0:LAT], ps[:, 4, :], 1.0 / C, 64e-5, ALU.mult, ALU.add).then_inc(sem("read_dve"), one("read_dve"))
                dve.wait_ge(sem("read_act_v"), more("read_act_v"))
                settle(dve.tensor_tensor(v_turned, v_turned, ps[:, 1, :], ALU.mult))
                dve.wait_ge(sem("read_act_root"), more("read_act_root"))
                settle(dve.reciprocal(rstd[:, 0:LAT], rstd[:, 0:LAT]))
                settle(dve.scalar_tensor_tensor(y_pair, y_pair, vcol("lng", p), rstd[:, 0:LAT], ALU.mult, ALU.mult))
                settle(dve.scalar_tensor_tensor(y_pair, y_pair, vcol("lnb", p), v_turned, ALU.add, ALU.add))
                dve.tensor_tensor(R[:, p, :], y_pair, ps[:, 3, :], ALU.mult).then_inc(sem("r_out"), one("r_out"))

            def tables():
                dve.wait_ge(sem("pos"), 32)
                ang, turns = rope_tmp[:, 0, :], rope_tmp[:, 1, :]
                two_pi = 2 * np.pi
                first = 6.28125
                second = float(np.float32(np.round((two_pi - first) * 2 ** 19) / 2 ** 19))
                third = two_pi - first - second
                magic = 1.5 * 2 ** 23
                settle(dve.tensor_copy(ang, pos_i.bitcast(I32)))
                settle(dve.tensor_scalar(ang, ang, ccol("inv_freq"), None, ALU.mult))
                settle(dve.tensor_scalar(turns, ang, 1.0 / two_pi, magic, ALU.mult, ALU.add))
                settle(dve.tensor_scalar(turns, turns, magic, None, ALU.subtract))
                for part in (first, second, third):
                    settle(dve.scalar_tensor_tensor(ang, turns, -part, ang, ALU.mult, ALU.add))
                dve.tensor_scalar(ang, ang, 3.1415925, -3.1415925, ALU.min, ALU.max).then_inc(sem("angle"), one("angle"))
                dve.wait_ge(sem("sine"), more("sine", 2))
                cos = rope[:, 0, :]
                settle(dve.tensor_tensor(cos, cos, cos, ALU.mult))
                settle(dve.tensor_scalar(cos, cos, -2.0, 1.0, ALU.mult, ALU.add))

            def mix_in(l):
                settle(dve.memset(conv_in[:, :, 0:TAPS - 1], 0.0))
                for c in range(2):
                    dve.tensor_copy(mk2[:, c, :], tile()[:, 0:CTX]).then_inc(sem("tile_free"), one("tile_free"))
                for t in range(2):
                    dve.tensor_copy(mv2[:, t, :], tile()[:, 0:CTX]).then_inc(sem("tile_free"), one("tile_free"))
                for c in range(3):
                    a = conv_in[:, c, TAPS - 1:]
                    dve.tensor_copy(a, tile()).then_inc(sem("tile_free"), one("tile_free"))
                    gate = tile()
                    dve.wait_ge(sem("sigmoid"), more("sigmoid"))
                    dve.wait_ge(sem("tile_free"), n["tile_free"])
                    dve.tensor_tensor(a, a, sig[:, n["sig"] % 2, :], ALU.mult).then_inc(sem("tile_free"), one("tile_free"))
                    n["sig"] += 1
                for c in range(6):
                    dve.tensor_copy(q2[:, c, :], tile()).then_inc(sem("tile_free"), one("tile_free"))
                for t in range(LAT // P):
                    dve.tensor_copy(v2[:, t, :], tile()[:, 0:P]).then_inc(sem("tile_free"), one("tile_free"))
                gains = ["swa_q_norm"] * 3 + ["swa_k_norm"] + ["mem_q_norm"] * 2 + ["mem_k_norm"] * 2
                for i in range(8):
                    hi = LAT if i < 6 else CTX
                    t = q2[:, i, :] if i < 6 else mk2[:, i - 6, :]
                    r = inverse_root(1, 0, hi, 1.0 / C, 1e-6)
                    ins = dve.scalar_tensor_tensor(t, t, vcol(f"{gains[i]}{l}"), r, ALU.mult, ALU.mult)
                    if i >= 4:
                        settle(ins)
                        continue
                    ins.then_inc(sem("normed"), one("normed"))
                    dve.wait_ge(sem("normed"), n["normed"])
                    dve.wait_ge(sem("rotated"), more("rotated"))
                    dve.tensor_tensor(rope_tmp[:, 0, :], ps[:, 5, :], rope[:, 1, :], ALU.mult)
                    settle(dve.tensor_tensor(t, t, rope[:, 0, :], ALU.mult))
                    settle(dve.tensor_tensor(t, t, rope_tmp[:, 0, :], ALU.add))
                dve.tensor_copy(stat[:, 15:16], q2[:, 0, 0:1]).then_inc(sem("roped"), one("roped"))

            def conv(l):
                dve.wait_ge(sem("tap"), n["tap"])
                dve.tensor_copy(stat[:, 15:16], conv_y[:, 0, 0:1]).then_inc(sem("tapped"), one("tapped"))
                dve.wait_ge(sem("summed"), more("summed", 3))
                for c in range(3):
                    dve.scalar_tensor_tensor(conv_y[:, c, :], ps[:, 4, :], -1.0 / 384, conv_y[:, c, :], ALU.mult, ALU.add).then_inc(sem("centred"), one("centred"))
                dve.wait_ge(sem("centred"), n["centred"])
                dve.tensor_copy(stat[:, 14:15], conv_y[:, 0, 0:1]).then_inc(sem("var"), one("var"))
                r = inverse_root(3, 0, LAT, 1.0 / 384, 1e-6)
                for c in range(3):
                    settle(dve.scalar_tensor_tensor(conv_y[:, c, :], conv_y[:, c, :], vcol(f"conv_ln_g{l}", c), r, ALU.mult,
                                                    ALU.mult))
                for c in range(3):
                    dve.tensor_scalar(conv_y[:, c, :], conv_y[:, c, :], vcol(f"conv_ln_b{l}", c), None, ALU.add).then_inc(sem("conv_z"), one("conv_z"))
                for c in range(3):
                    dve.wait_ge(sem("conv_sigmoid"), more("conv_sigmoid"))
                    s = sig[:, c, :] if c < 2 else rstd[:, 0:LAT]
                    ins = dve.tensor_tensor(Y[:, c, 0:LAT], conv_y[:, c, :], s, ALU.mult)
                ins.then_inc(sem("convolved"), one("convolved"))

            skip = lambda *a: None
            model(dict(load=load, mod=mod, gains=gains, norm_mod=norm_mod, even_in=even_in, attention=attention,
                       project=project, post=post, mlp=mlp, odd_in=odd_in, prepare=prepare, state_in=state_in, solve=skip,
                       state_out=state_out, readout=readout, odd_out=skip, tables=tables, norm_vec=norm_vec,
                       swiglu=swiglu, half_step=half_step, mix_in=mix_in, conv=conv, store=skip))


def kernel(**inputs):
    import numpy as _np
    import concourse.bacc as _bacc
    from concourse import mybir as _mybir
    from concourse.bass_utils import run_bass_kernel_spmd as _run

    a = {k: _np.asarray(v) for k, v in inputs.items()}

    def features(x):
        return x.reshape(-1, KD, P).transpose(2, 1, 0)

    arrays = dict(
        panels=pack_panels(a), vecs=pack_vectors(a), consts=pack_constants(),
        x_in=features(_np.concatenate([a["x"][0], a["ctx"][0]], 0)),
        c_in=features(_np.stack([a["c"][0], a["c_ctx"]], 0)),
        mem_in=features(a["mem_2"][0]),
        pool_w=a["ev_pool_w"][0].transpose(1, 0, 2),
        bias=pack_bias(a["ev_rpb"][0]),
        pos=_np.repeat(a["positions_2"].astype(_np.int32).reshape(1, LAT), P, 0),
        window=pack_window(),
    )
    arrays = {f"in_{k}": _np.ascontiguousarray(v) for k, v in arrays.items()}
    nc = _bacc.Bacc("TRN2", target_bir_lowering=False, num_devices=1)
    args = [nc.dram_tensor(k, v.shape, _mybir.dt.from_np(v.dtype), kind="ExternalInput").ap() for k, v in arrays.items()]
    out = nc.dram_tensor("out_x", (P, KD, LAT), F32, kind="ExternalOutput").ap()
    x_save = nc.dram_tensor("x_save", (P, KD, LAT), F32, kind="Internal").ap()
    build_program(nc, *args, out, x_save)
    r = _run(nc, [arrays], core_ids=[0])
    return _np.ascontiguousarray(r.results[0]["out_x"].transpose(2, 1, 0)).reshape(1, LAT, D)
```

```python
from collections import defaultdict
from contextlib import ExitStack

import numpy as np

import concourse.bass as bass
from concourse import mybir

P = 128
D = 1024
KD = D // P
LAT = 512
CTX = 256
TOK = LAT + CTX
FF1 = 4096
FF2 = 2816
COLS = 512
RING = 4
C = 64
CHUNKS = TOK // C
CTX_CHUNKS = CTX // C
PAIRS = KD
NEG = -1e30
UNIT = KD * TOK
PANEL = KD * COLS
POOL_WINDOWS = (2, 4, 8, 16)
TAPS = 31
Q_ORDER = (0, 3, 1, 4, 2, 5)
LEVELS = 6

F32 = mybir.dt.float32
I32 = mybir.dt.int32
ALU = mybir.AluOpType
ACT = mybir.ActivationFunctionType
AX = mybir.AxisListType



def mlp_steps(groups):
    steps = [("up", 0)]
    for g in range(groups):
        if g + 1 < groups:
            steps.append(("up", g + 1))
        steps.append(("down", g))
    return steps


MOD_STEPS = range(1, 7)
FF1_GROUPS = [8] * (FF1 // D)
FF2_GROUPS = [8, 8, 6]


def pack_panels(a):
    panels = []

    def add(w):
        rows, cols = w.shape
        full = np.zeros((KD * P, COLS), np.float32)
        full[:rows, :cols] = w
        panels.append(full.reshape(KD, P, COLS).transpose(1, 0, 2))

    def add_cols(w, lo=0, hi=None):
        for c in range(lo, w.shape[1] if hi is None else hi, COLS):
            add(w[:, c:c + COLS])

    def add_mlp(w1, w2, beside=None):
        for step, (kind, g) in enumerate(mlp_steps(len(FF1_GROUPS))):
            if beside is not None and step in MOD_STEPS:
                lo = 2 * (step - MOD_STEPS[0])
                add_cols(beside, lo * COLS, (lo + 2) * COLS)
            if kind == "up":
                add_cols(w1, g * D, (g + 1) * D)
            else:
                add_cols(w2[g * D:(g + 1) * D])

    def add_swiglu(w1, w3, w2):
        for kind, g in mlp_steps(len(FF2_GROUPS)):
            if kind == "up":
                for j in range(FF2_GROUPS[g] // 2):
                    c = g * D + 2 * j * P
                    add(np.concatenate([w1[:, c:c + P], w3[:, c:c + P], w1[:, c + P:c + 2 * P], w3[:, c + P:c + 2 * P]], 1))
            else:
                add_cols(w2[g * D:g * D + FF2_GROUPS[g] * P])

    add_cols(a["ada_w"][0], 0, 2 * D)
    for j in range(4):
        add_cols(a["ev_w_in"][0], j * COLS, (j + 1) * COLS)
        add_cols(a["ada_w"][0], 2 * D + 2 * j * COLS, 2 * D + 2 * (j + 1) * COLS)
    add_cols(a["ev_w_out"][0])
    add_mlp(a["mlp_w1"][0], a["mlp_w2"][0], a["ada_w"][1])
    add(np.concatenate([a["rw_w1"][0, 0], a["rw_w1"][0, 1], a["rw_a1"][0, 0], a["rw_a1"][0, 1], a["rw_g1"][0]], 1))
    add_cols(a["rw_wk"][0])
    heads = a["rw_wv"][0].reshape(D, PAIRS, 2, C)
    add(heads[:, :, 0].reshape(D, COLS))
    add(heads[:, :, 1].reshape(D, COLS))
    second = np.concatenate([a["rw_w2"][0].reshape(P, D), a["rw_a2"][0].reshape(P, D), a["rw_g2"][0]], 1)
    panels.append(np.concatenate([second, np.zeros((P, PANEL - 3 * D), np.float32)], 1).reshape(P, KD, COLS))
    add_cols(a["rw_wr"][0])
    add_cols(a["rw_wo"][0])
    add_mlp(a["mlp_w1"][1], a["mlp_w2"][1])
    for l in range(2):
        add_swiglu(a["ffn1_w1_2"][l], a["ffn1_w3_2"][l], a["ffn1_w2_2"][l])
        add(a["w_mem_kv_2"][l])
        w = a["w_in_2"][l]
        conv, gate = w[:, 0:384].reshape(D, 3, P), w[:, 384:768].reshape(D, 3, P)
        q = w[:, 768:1152].reshape(D, 6, C)[:, Q_ORDER, :].reshape(D, 3, P)
        add(np.concatenate([conv[:, 0], gate[:, 0], conv[:, 1], gate[:, 1]], 1))
        add(np.concatenate([conv[:, 2], gate[:, 2], q[:, 0], q[:, 1]], 1))
        add(np.concatenate([q[:, 2], w[:, 1152:1280], w[:, 1408:1664]], 1))
        add(w[:, 1280:1408])
        wo = a["w_out_2"][l]
        wo = np.concatenate([wo[0:384], wo[384:768].reshape(6, C, D)[Q_ORDER, :, :].reshape(384, D), wo[768:]], 0)
        add_cols(wo)
        add_swiglu(a["ffn2_w1_2"][l], a["ffn2_w3_2"][l], a["ffn2_w2_2"][l])
    return np.ascontiguousarray(np.stack(panels).reshape(len(panels), P, PANEL))


VEC_AT = {}


def vector_parts():
    for i in range(2):
        for j in range(4):
            yield f"norm_g{i}{j}", KD
        yield f"ada_b{i}", 6 * KD
    yield "pool_scale", 4
    for j in range(6):
        yield f"mu{j}", KD
    for d in range(2):
        yield f"w0{d}", KD
        yield f"a0{d}", KD
    for name in ("kk", "ka", "rk", "lng", "lnb"):
        yield name, KD
    for l in range(2):
        for name in ("ffn1_norm", "mix_norm", "mem_norm", "ffn2_norm", "final_norm"):
            yield f"{name}{l}", KD
        for name in ("conv_b", "conv_ln_g", "conv_ln_b"):
            yield f"{name}{l}", 3
        yield f"conv_w{l}", 3 * TAPS
        for name in ("swa_q_norm", "swa_k_norm", "mem_q_norm", "mem_k_norm"):
            yield f"{name}{l}", 1
        yield f"sinks{l}", 6


NVEC = 0
for _name, _cols in vector_parts():
    VEC_AT[_name] = NVEC
    NVEC += _cols


def pack_vectors(a):
    v = np.zeros((P, NVEC), np.float32)

    def put(name, x):
        x = np.asarray(x).reshape(-1, P).T
        v[:, VEC_AT[name]:VEC_AT[name] + x.shape[1]] = x

    for i in range(2):
        for j in range(4):
            put(f"norm_g{i}{j}", a["norm_g"][i, j])
        put(f"ada_b{i}", a["ada_b"][i])
    put("pool_scale", a["ev_pool_scale"][0])
    for j in range(6):
        put(f"mu{j}", a["rw_mu"][0, j])
    for d in range(2):
        put(f"w0{d}", a["rw_w0"][0, d])
        put(f"a0{d}", a["rw_a0"][0, d])
    for name in ("kk", "ka", "rk", "lng", "lnb"):
        put(name, a[f"rw_{name}"][0])
    for l in range(2):
        for name in ("ffn1_norm", "mix_norm", "mem_norm", "ffn2_norm", "final_norm", "conv_b", "conv_ln_g", "conv_ln_b"):
            put(f"{name}{l}", a[f"{name}_2"][l])
        put(f"conv_w{l}", a["conv_w_2"][l].reshape(TAPS, 3, P).transpose(1, 0, 2))
        for name in ("swa_q_norm", "swa_k_norm", "mem_q_norm", "mem_k_norm"):
            put(f"{name}{l}", np.concatenate([a[f"{name}_2"][l]] * 2))
        put(f"sinks{l}", np.repeat(np.asarray(a["swa_sinks_2"][l])[:, None], P, 1))
    return v


CONST_PARTS = (("ident", P), ("head_ones", P), ("rotate", P), ("gram_mask", 2 * 2 * C),
               ("level", LEVELS * C), ("level_t", LEVELS * C), ("ident2", C), ("pool_edge", 2 * 15), ("inv_freq", 1))
CONST_AT = {}
NCONST = 0
for _name, _cols in CONST_PARTS:
    CONST_AT[_name] = NCONST
    NCONST += _cols


def pack_constants():
    v = np.zeros((P, NCONST), np.float32)

    def put(name, x):
        x = np.asarray(x, np.float32).reshape(x.shape[0], -1)
        v[:, CONST_AT[name]:CONST_AT[name] + x.shape[1]] = x

    p = np.arange(P)
    put("ident", np.eye(P))
    put("head_ones", p[:, None] // C == p[None, :] // C)
    same = p[:, None] // C == p[None, :] // C
    half = C // 2
    first = p[None, :] % C < half
    put("rotate", np.where(same & first & (p[:, None] == p[None, :] + half), -1.0, 0.0)
        + np.where(same & ~first & (p[:, None] == p[None, :] - half), 1.0, 0.0))
    s, t = (p % C)[:, None], np.arange(C)[None, :]
    put("gram_mask", np.concatenate([s < t, s <= t, s > t, s >= t], 1))
    levels = []
    for j in range(LEVELS):
        m = 1 << j
        levels.append((s // m % 2 == 1) & (t // m == s // m - 1))
    put("level", np.concatenate(levels, 1))
    put("level_t", np.concatenate([(t // (1 << j) % 2 == 1) & (s // (1 << j) == t // (1 << j) - 1) for j in range(LEVELS)], 1))
    put("ident2", s == t)
    edge = []
    for w in POOL_WINDOWS:
        edge.append([w / (i + w // 2) for i in range(w // 2)] + [w / (w - i) for i in range(w // 2)])
    put("pool_edge", np.repeat(np.concatenate(edge)[None, :], P, 0))
    put("inv_freq", (10000.0 ** (-(2 * (p % half)).astype(np.float32) / C)).astype(np.float32)[:, None])
    return v


def pack_window():
    rel = (np.arange(P)[:, None] + P) - np.arange(2 * P)[None, :]
    return np.where((rel >= 0) & (rel < P), np.float32(0.0), np.float32(NEG)).astype(np.float32)


def pack_bias(rpb):
    heads = rpb.shape[0]
    col = np.arange(64)
    start = np.clip(col - 8, 0, 48)
    ok = (col[None, :] >= start[:, None]) & (col[None, :] < start[:, None] + 16)
    dc = np.clip(col[None, :] - col[:, None], -15, 15) + 15
    t = np.where(ok[None, None], rpb[:, :, dc], np.float32(NEG)).transpose(0, 2, 1, 3)
    out = np.full((heads, 2, 64, 16, 64), np.float32(NEG), np.float32)
    out[:, 0, :, 0:15] = t
    out[:, 1, :, 1:16] = t
    return out.reshape(heads, P, 16 * 64)



def build_program(nc, panels, vecs, consts, x_in, c_in, mem_in, pool_w, bias, pos, window_in, out, x_save):
    npanels = panels.shape[0]
    with ExitStack() as ctx:
        def sb(name, shape, dt=F32):
            return ctx.enter_context(nc.sbuf_tensor(name, shape, dt))

        sems = {}

        def sem(name):
            if name not in sems:
                sems[name] = ctx.enter_context(nc.semaphore(name))
            return sems[name]

        arena = sb("arena", [P, 5 * UNIT + RING * PANEL])
        vec = sb("vec", [P, NVEC])
        const = sb("const", [P, NCONST])
        ones = sb("ones", [P, P])
        square = sb("square", [P, 2, TOK])
        rstd = sb("rstd", [P, TOK])
        mod_sb = sb("mod", [P, 2, 2, 6 * KD])
        gain = sb("gain", [P, 2, 4, 2, KD])
        silu_c = sb("silu_c", [P, KD, 2])
        raw_c = sb("raw_c", [P, KD, 2])
        stat = sb("stat", [P, 16])
        reset = sb("reset", [P, TOK])
        ps = ctx.enter_context(nc.psum_tensor("ps", [P, 8, 512], F32))

        def area(at, *shape):
            n = int(np.prod(shape))
            flat = arena[:, at:at + n]
            if len(shape) == 1:
                return flat
            names = " ".join("abcd"[:len(shape)])
            return flat.rearrange(f"p ({names}) -> p {names}", **{"abcd"[i]: s for i, s in enumerate(shape)})

        X0, H0, Y0, W0 = 0, UNIT, 2 * UNIT, 3 * UNIT
        RING0 = 5 * UNIT
        X, H, Y = (area(o, KD, TOK) for o in (X0, H0, Y0))
        ring = [area(RING0 + s * PANEL, KD, COLS) for s in range(RING)]
        hidden1 = [area(W0 + s * UNIT, KD, TOK) for s in range(2)]
        hidden2 = [area(W0 + s * KD * LAT, KD, LAT) for s in range(2)]
        Z = area(W0, KD, TOK)
        qT = area(W0, 4, TOK)
        kT = area(W0 + 4 * TOK, 4, TOK)
        vN = area(W0 + 8 * TOK, TOK // P, 512)
        pool_buf = [area(W0 + 12 * TOK + i * 792, 792) for i in range(3)]
        pool_wb = area(W0 + 12 * TOK + 3 * 792, 4, P)
        probs = area(H0, 3, TOK)
        probsT = area(H0 + 3 * TOK, 2, TOK)
        bias_sb = area(H0 + 5 * TOK, 2, 1024)
        B0 = W0
        q2 = area(B0, 6, LAT)
        mk2 = area(B0 + 6 * LAT, 2, CTX)
        v2 = area(B0 + 7 * LAT, 4, P)
        mv2 = area(B0 + 8 * LAT, 2, 256)
        conv_in = area(B0 + 9 * LAT, 3, TAPS - 1 + LAT)
        conv_y = area(B0 + 9 * LAT + 3 * (TAPS - 1 + LAT), 3, LAT)
        rope = area(W0 + 2 * KD * LAT, 2, LAT)
        rope_tmp = area(W0 + 2 * KD * LAT + 2 * LAT, 2, LAT)
        pos_i = area(W0 + 2 * KD * LAT + 4 * LAT, LAT)
        window = area(W0 + 2 * KD * LAT + 5 * LAT, 2 * P)
        sig = square[:, :, 0:LAT]

        def vcol(name, c=0, n=1):
            return vec[:, VEC_AT[name] + c:VEC_AT[name] + c + n]

        def ccol(name, c=0, n=1):
            return const[:, CONST_AT[name] + c:CONST_AT[name] + c + n]

        ident = ccol("ident", 0, P)
        head_ones = ccol("head_ones", 0, P)
        rotate = ccol("rotate", 0, P)

        SEG2 = ((0, 384), (384, TOK))
        SEG1 = ((0, LAT),)
        SEGM = ((LAT, TOK),)

        def norm_banks(lo, hi):
            return [(a, b, bank) for a, b, bank in ((lo, min(hi, LAT), 4), (max(lo, LAT), hi, 5)) if b > a]

        def norm_psum(lo, hi):
            flat = ps[:, 4:6, :].rearrange("p a b -> p (a b)")
            return flat[:, lo:hi]

        def even_units():
            units = []
            for h in range(8):
                base, ch = C * (h % 2), h // 2
                for qt in range(TOK // P):
                    lat = qt < LAT // P
                    lo = 0 if lat else LAT
                    units.append(dict(
                        q=qT[base:base + C, ch, qt * P:(qt + 1) * P],
                        keys=[kT[base:base + C, ch, a:b] for a, b in ([(0, LAT)] if lat else []) + [(LAT, TOK)]],
                        bias=bias_sb[:, h % 2, (7 - 2 * qt) * 64:(7 - 2 * qt) * 64 + LAT] if lat else None,
                        bias_head=h, width=TOK - lo, sink=None,
                        values=[vN[:, t, h * C:(h + 1) * C] for t in range(lo // P, TOK // P)],
                        base=base, dest=Y[base:base + C, 4 + ch, qt * P:(qt + 1) * P]))
            return units

        def conformer_units(l):
            units = []
            for i in range(6):
                base, ch = C * (i % 2), i // 2
                for qb in range(LAT // P):
                    lo = max(0, qb - 1)
                    n = (qb + 1 - lo) * P
                    units.append(dict(
                        q=q2[base:base + C, ch, qb * P:(qb + 1) * P],
                        keys=[q2[base:base + C, 3, lo * P:(qb + 1) * P]],
                        bias=window[:, 2 * P - n:2 * P], bias_head=None, width=n,
                        sink=vcol(f"sinks{l}", Q_ORDER[i]),
                        values=[v2[:, t, (i % 2) * C:(i % 2 + 1) * C] for t in range(lo, qb + 1)],
                        base=base, dest=Y[base:base + C, 3 + ch, qb * P:(qb + 1) * P]))
            for h in range(4):
                base, ch = C * (h % 2), h // 2
                for qb in range(LAT // P):
                    units.append(dict(
                        q=q2[base:base + C, 4 + ch, qb * P:(qb + 1) * P],
                        keys=[mk2[base:base + C, ch, :]], bias=None, bias_head=None, width=CTX, sink=None,
                        values=[mv2[:, t, h * C:(h + 1) * C] for t in range(2)],
                        base=base, dest=Y[base:base + C, 6 + ch, qb * P:(qb + 1) * P]))
            return units

        def scores_ps(u, width):
            return ps[:, 2 * (u % 2):2 * (u % 2) + 2, :].rearrange("p a b -> p (a b)")[:, 0:width]

        def turned_ps(width):
            return ps[:, 4:6, :].rearrange("p a b -> p (a b)")[:, 0:width]

        XX, MIX = Y, area(W0, KD, TOK)
        K = area(W0 + UNIT, KD, TOK)
        V = area(X0, CHUNKS, PAIRS, C)
        R = area(H0, KD, LAT)
        decay_in, a_in = area(H0 + KD * LAT, TOK), area(H0 + KD * LAT + TOK, TOK)
        gate_in = area(H0 + KD * LAT + 2 * TOK, LAT)
        LORA_SLOT = 3
        lora2 = area(RING0 + LORA_SLOT * PANEL, 3, D)
        k_sum = area(RING0 + LORA_SLOT * PANEL + 3 * D, LAT)
        y_pair = area(RING0 + LORA_SLOT * PANEL + 3 * D + LAT, LAT)
        state = sb("state", [P, 2, C])
        omka = sb("omka", [P, KD])
        w0_neg = sb("w0_neg", [P, 2, C])
        state_dec = sb("state_dec", [P, 2, C])
        chunk_decay = sb("chunk_decay", [P, 2, CHUNKS])
        WORK = ((Y0, 2 * UNIT), (RING0, 3 * PANEL))
        BLOCK = CHUNKS * C
        SET = 8 * BLOCK + 2 * LAT
        sets = []
        for o, _ in WORK:
            sets.append(dict(
                kr=area(o, CHUNKS, 2, C), bkn=area(o + 2 * BLOCK, CHUNKS, 2 * C),
                uv=area(o + 4 * BLOCK, CHUNKS, 2, C),
                bv=area(o + 6 * BLOCK, CHUNKS, C), xt=area(o + 7 * BLOCK, CHUNKS, C),
                gram=area(o + 8 * BLOCK, LAT // C, 2, C)))
        bk = area(Y0 + SET, CHUNKS, 2, C)
        couple = area(RING0 + SET, 2, CHUNKS, C)
        spare = [area(o + SET + 2 * BLOCK + k * TOK, TOK) for o, _ in WORK for k in range(4)]
        f_kk, f_a, f_inc, f_inv, f_kd = spare[0:5]
        chunked = lambda f: f.rearrange("p (c t) -> p c t", t=C)
        f_x, f_am, f_y1 = (chunked(f) for f in spare[5:8])
        v_turned = area(RING0 + SET + 2 * BLOCK + 4 * TOK, LAT)
        assert all(SET + 2 * BLOCK + 4 * TOK + LAT <= n for _, n in WORK)
        f_cs = square[:, 1, :]
        HALF = CHUNKS // 2
        E_HALF = float(np.exp(-0.5))
        JOBS = 2 * PAIRS
        GRAMS = CHUNKS // 2
        INVERSE = GRAMS + 2
        FEATURE_SLOTS = ((9, "norm"), (12, "decay"), (15, "rate"))
        EXPONENT_SLOT = 18
        KEY_SLOT = 21

        def chunk_order(d):
            ctx_first = list(range(LAT // C, CHUNKS))
            lat = list(range(LAT // C))
            return ctx_first + lat if d == 0 else ctx_first[::-1] + lat[::-1]

        def two_banks(b, n=TOK):
            return ps[:, b:b + 2, :].rearrange("p a b -> p (a b)")[:, 0:n]

        def job_steps(e):
            for t in range(JOBS + 2):
                for slot in range(3 * CHUNKS):
                    if t < JOBS:
                        e["features"](t, slot)
                    if 0 <= t - 2:
                        e[("state_in", "solve", "state_out")[slot % 3]](t - 2, slot // 3)
                    if 0 <= t - 1 < JOBS:
                        e["prepare"](t - 1, slot)
                if t >= 3 and t % 2 == 1:
                    e["readout"]((t - 3) // 2)

        def model(e):
            e["load"]()
            e["mod"](0, 0, 4)
            e["gains"](0, 0)
            e["norm_mod"](0, 0)
            e["even_in"]()
            e["gains"](0, 1)
            e["attention"](even_units(), None)
            e["project"](2, SEG2, Y, Z, "attn")
            e["post"](Z, 0, 1)
            e["norm_mod"](0, 2)
            e["mlp"](SEG2, True)
            e["post"](Y, 0, 3)
            e["gains"](1, 0)
            e["gains"](1, 1)
            e["norm_mod"](1, 0)
            e["odd_in"]()
            job_steps(e)
            e["odd_out"]()
            e["project"](2, SEG1, R, Z, "odd")
            e["post"](Z, 1, 1)
            e["norm_mod"](1, 2)
            e["mlp"](SEG1, False)
            e["post"](Y, 1, 3)
            e["tables"]()
            for l in range(2):
                e["norm_vec"](0, LAT, "ffn1_norm", l, X)
                e["swiglu"]()
                e["half_step"]()
                e["norm_vec"](LAT, TOK, "mem_norm", l, X)
                e["norm_vec"](0, LAT, "mix_norm", l, X)
                e["mix_in"](l)
                e["attention"](conformer_units(l), l)
                e["conv"](l)
                e["project"](2, SEG1, Y, None, "attn")
                e["norm_vec"](0, LAT, "ffn2_norm", l, X)
                e["swiglu"]()
                e["half_step"]()
                e["norm_vec"](0, LAT, "final_norm", l, X)
            e["store"]()

        block = ctx.enter_context(nc.Block())

        def counting():
            n = defaultdict(int)

            def more(name, k=1):
                n[name] += k
                return n[name]

            def one(name):
                n[name] += 1
                return 1

            return n, more, one

        @block.sync
        def _(sp):
            n, more, one = counting()
            ends = []

            def load_panel(tiles, width=PANEL):
                p = len(ends)
                if p >= RING:
                    if ends[p - RING] > 0:
                        sp.wait_ge(sem("tile_done"), ends[p - RING])
                sp.dma_start(arena[:, RING0 + (p % RING) * PANEL:RING0 + (p % RING) * PANEL + width],
                             panels[p, :, 0:width]).then_inc(sem(f"panel{p % RING}"), 16)
                n["tile"] += tiles
                ends.append(n["tile"])

            def load():
                sp.dma_start(raw_c[:, :, :], c_in).then_inc(sem("small_in"), 16)
                sp.dma_start(vec[:, :], vecs).then_inc(sem("small_in"), 16)
                load_panel(1)
                load_panel(1)
                sp.dma_start(const[:, :], consts).then_inc(sem("small_in"), 16)
                sp.dma_start(X, x_in).then_inc(sem("x_in"), 16)
                n["mod_skip"] = 2

            def mod(i, lo, hi):
                for _ in range(lo + n["mod_skip"], hi):
                    load_panel(1)
                n["mod_skip"] = 0

            def even_in():
                for j, tiles in enumerate((8, 8, 8, TOK // P)):
                    load_panel(tiles)
                    mod(0, 4 + 2 * j, 6 + 2 * j)
                n["tile"] += 8

            def project(count, segs, src, dest, ready):
                for _ in range(count):
                    load_panel(4 * len(segs))

            def mlp(segs, beside):
                for step, _ in enumerate(mlp_steps(len(FF1_GROUPS))):
                    if beside and step in MOD_STEPS:
                        mod(1, 2 * (step - MOD_STEPS[0]), 2 * (step - MOD_STEPS[0]) + 2)
                    for _ in range(2):
                        load_panel(4 * len(segs))

            def swiglu():
                for kind, g in mlp_steps(len(FF2_GROUPS)):
                    if kind == "up":
                        for _ in range(FF2_GROUPS[g] // 2):
                            load_panel(4)
                    else:
                        for _ in range(2):
                            load_panel(4, FF2_GROUPS[g] * COLS)

            def odd_in():
                load_panel(5)
                for _ in range(2):
                    load_panel(8)
                for _ in range(2):
                    load_panel(CHUNKS)
                load_panel(0, 3 * D)
                for _ in range(2):
                    load_panel(4)

            def odd_out():
                if PAIRS > 0:
                    sp.wait_ge(sem("r_out"), PAIRS)

            def mix_in(l):
                for tiles in (4, 4, 4, 4, LAT // P):
                    load_panel(tiles)

            def store():
                if 10 * KD > 0:
                    sp.wait_ge(sem("x_chunk"), 10 * KD)
                sp.dma_start(out, X[:, :, 0:LAT]).then_inc(sem("stored"), 16)
                sp.wait_ge(sem("stored"), 16)

            skip = lambda *a: None
            model(dict(load=load, mod=mod, gains=skip, norm_mod=skip, even_in=even_in, attention=skip, project=project,
                       post=skip, mlp=mlp, odd_in=odd_in, features=skip, prepare=skip, state_in=skip, solve=skip, state_out=skip,
                       readout=skip, odd_out=odd_out, tables=skip, norm_vec=skip, swiglu=swiglu, half_step=skip,
                       mix_in=mix_in, conv=skip, store=store))
            assert len(ends) == npanels

        @block.gpsimd
        def _(pool):
            n, more, one = counting()

            def load():
                pool.dma_start(pool_wb, pool_w).then_inc(sem("pool_w"), 16)
                pool.memset(ones[:, :], 1.0).then_inc(sem("ones"), one("ones"))

            def attention(units, l):
                heads = []
                for u, unit in enumerate(units):
                    h = unit["bias_head"]
                    if h is not None and h not in heads:
                        heads.append(h)
                        if len(heads) == 1:
                            if n["tile"] > 0:
                                pool.wait_ge(sem("tile_free"), n["tile"])
                        if len(heads) > 2:
                            if u - TOK // P > 0:
                                pool.wait_ge(sem("scored"), u - TOK // P)
                        pool.dma_start(bias_sb[:, h % 2, :], bias[h]).then_inc(sem(f"bias{h % 2}"), 16)

            def even_in():
                n["tile"] += 24 + TOK // P + 8 + 8

            def mod(i, lo, hi):
                n["tile"] += hi - lo

            def odd_in():
                if 2 * KD > 0:
                    pool.wait_ge(sem("x_chunk"), 2 * KD)
                pool.dma_start(x_save, X[:, :, 0:LAT]).then_inc(sem("x_saved"), 16)

            def half(h):
                return slice(C * h, C * h + C)

            def mask_couplings(j, level):
                upper = "level_t" if j % 2 == 0 else "level"
                for h in range(2):
                    m = ccol(upper, C * level, C)[half(h), :].unsqueeze(1).broadcast_to([C, CHUNKS, C])
                    ins = pool.tensor_tensor(f_am[half(h)], couple[half(h), h, :, :], m, ALU.mult)
                ins.then_inc(sem("masked"), one("masked"))

            def prepare(j, i):
                p, d = divmod(j, 2)
                if i == 0:
                    uv = sets[d]["uv"]
                    pool.wait_ge(sem("decayed"), more("decayed"))
                    for h, lo in ((0, C), (1, 0)):
                        ins = pool.tensor_copy(uv[lo:lo + C, :, h, :], V[lo:lo + C, :, p, :])
                    ins.then_inc(sem("values"), one("values"))
                elif i == INVERSE:
                    pool.wait_ge(sem("gram_read"), more("gram_read", GRAMS))
                    mask_couplings(j, 0)
                    pool.wait_ge(sem("started"), more("started"))
                    mask_couplings(j, 1)
                elif INVERSE < i <= INVERSE + 3 * (LEVELS - 2):
                    level, q = divmod(i - INVERSE - 1, 3)
                    if q == 1:
                        pool.wait_ge(sem("first_product"), 2 * ((LEVELS - 1) * j + level + 1))
                        mask_couplings(j, level + 2)

            def odd_out():
                if PAIRS > 0:
                    pool.wait_ge(sem("r_out"), PAIRS)
                pool.dma_start(X[:, :, 0:LAT], x_save).then_inc(sem("x_back"), 16)
                pool.dma_start(X[:, :, LAT:TOK], mem_in).then_inc(sem("mem_in"), 16)

            def tables():
                if 4 * KD > 0:
                    pool.wait_ge(sem("x_chunk"), 4 * KD)
                pool.dma_start(pos_i.bitcast(I32), pos).then_inc(sem("pos"), 16)
                pool.dma_start(window, window_in).then_inc(sem("pos"), 16)

            skip = lambda *a: None
            model(dict(load=load, mod=mod, gains=skip, norm_mod=skip, even_in=even_in, attention=attention, project=skip,
                       post=skip, mlp=skip, odd_in=odd_in, features=skip, prepare=prepare, state_in=skip, solve=skip, state_out=skip,
                       readout=skip, odd_out=odd_out, tables=tables, norm_vec=skip, swiglu=skip, half_step=skip,
                       mix_in=skip, conv=skip, store=skip))

        @block.tensor
        def _(pe):
            n, more, one = counting()

            def panel():
                p = n["panel"]
                n["panel"] += 1
                pe.wait_ge(sem(f"panel{p % RING}"), 16 * (p // RING + 1))
                return ring[p % RING]

            def tile():
                if n["tile"] - 3 > 0:
                    pe.wait_ge(sem("tile_free"), n["tile"] - 3)
                n["tile"] += 1
                return ps[:, (n["tile"] - 1) % 4, :]

            def accumulate(dest, left, right, nk=KD, ready=None):
                for k in range(nk):
                    if ready:
                        pe.wait_ge(sem(ready), more(ready))
                    ins = pe.matmul(dest, left(k), right(k), start=(k == 0), stop=(k == nk - 1))
                ins.then_inc(sem("tile_done"), one("tile_done"))

            def columns(w, ms, src, segs, nk=KD, ready=None):
                for m in ms:
                    for a, b in segs:
                        accumulate(tile()[:, 0:b - a], lambda k: w[:, k, m * P:(m + 1) * P],
                                   lambda k: src[:, k, a:b], nk, ready)
                        ready = None

            def rows(w, lo, width, src, tok, cols, ready=None):
                for t in tok:
                    accumulate(tile()[:, 0:width], lambda k: src[:, k, t * P:(t + 1) * P],
                               lambda k: w[:, k, cols:cols + width], KD, ready)
                    ready = None

            def sums(lhs, count, lo, hi, src="square"):
                if n["norm"] > 0:
                    pe.wait_ge(sem("var"), n["norm"])
                n["norm"] += 1
                for c in range(count):
                    if src == "square":
                        pe.wait_ge(sem("square"), more("square"))
                    for a, b, bank in norm_banks(lo, hi):
                        right = square[:, n["sq"] % 2, a - lo:b - lo] if src == "square" else conv_y[:, c, :]
                        ins = pe.matmul(ps[:, bank, 0:b - a], lhs, right, start=(c == 0), stop=(c == count - 1))
                    n["sq"] += src == "square"
                    ins.then_inc(sem("summed"), one("summed"))

            def load():
                pe.wait_ge(sem("small_in"), 48)
                pe.wait_ge(sem("ones"), more("ones"))
                pe.wait_ge(sem("silu"), more("silu"))

            def mod(i, lo, hi):
                for _ in range(lo, hi):
                    w = panel()
                    bank = tile()
                    for m in range(4):
                        for k in range(KD):
                            ins = pe.matmul(bank[:, 2 * m:2 * m + 2], w[:, k, m * P:(m + 1) * P], silu_c[:, k, :],
                                            start=(k == 0), stop=(k == KD - 1))
                    ins.then_inc(sem("tile_done"), one("tile_done"))

            def norm_mod(i, which):
                sums(ones[:, :], KD, 0, TOK if (i, which) != (1, 2) else LAT)
                n["source"] = "h_act"

            def norm_vec(lo, hi, name, l, src):
                sums(ones[:, :], KD, lo, hi)
                n["source"] = "h_dve"

            def post(src, i, which):
                sums(ones[:, :], KD, 0, TOK if i == 0 else LAT)

            def even_in():
                columns(panel(), range(4), H, ((0, LAT), (LAT, TOK)), ready="h_act")
                mod(0, 4, 6)
                columns(panel(), range(4), H, SEG2)
                mod(0, 6, 8)
                columns(panel(), range(4), H, SEG2)
                mod(0, 8, 10)
                rows(panel(), 0, 512, H, range(TOK // P), 0)
                mod(0, 10, 12)
                pe.wait_ge(sem("pool_w"), 16)
                for g in range(4):
                    pe.wait_ge(sem("pooled"), more("pooled"))
                    for a, b in SEG2:
                        accumulate(tile()[:, 0:b - a], lambda k: pool_wb[:, g, :], lambda k: Y[:, 4 + g, a:b], 1)

            def attention(units, l):
                if n["tile"] > 0:
                    pe.wait_ge(sem("tile_free"), n["tile"])
                if n["norm"] > 0:
                    pe.wait_ge(sem("var"), n["norm"])
                if n["unit"] > 0:
                    pe.wait_ge(sem("roped"), more("roped"))
                base = n["unit"]
                for i in range(len(units) + 3):
                    if i < len(units):
                        unit, u = units[i], base + i
                        if u - 1 > 0:
                            pe.wait_ge(sem("scored"), u - 1)
                        col = 0
                        for key in unit["keys"]:
                            w = key.shape[1]
                            ins = pe.matmul(scores_ps(u, TOK)[:, col:col + w], unit["q"], key, start=True, stop=True)
                            col += w
                        ins.then_inc(sem("scores"), one("scores"))
                    if 2 <= i <= len(units) + 1:
                        unit, u = units[i - 2], base + i - 2
                        pe.wait_ge(sem("probs"), more("probs"))
                        if u > 0:
                            pe.wait_ge(sem("turned_copy"), u)
                        for t in range(unit["width"] // P):
                            ins = pe.transpose(turned_ps(TOK)[:, t * P:(t + 1) * P], probs[:, u % 3, t * P:(t + 1) * P],
                                               ident)
                        ins.then_inc(sem("turned"), one("turned"))
                    if i >= 3:
                        unit, u = units[i - 3], base + i - 3
                        if u + 1 > 0:
                            pe.wait_ge(sem("turned_copy"), u + 1)
                        if u - 1 > 0:
                            pe.wait_ge(sem("attended"), u - 1)
                        nt = unit["width"] // P
                        for t in range(nt):
                            ins = pe.matmul(ps[unit["base"]:unit["base"] + C, 6 + u % 2, 0:P], unit["values"][t],
                                            probsT[:, u % 2, t * P:(t + 1) * P], start=(t == 0), stop=(t == nt - 1))
                        ins.then_inc(sem("output"), one("output"))
                n["unit"] += len(units)

            def project(count, segs, src, dest, ready):
                if ready == "attn":
                    if n["unit"] > 0:
                        pe.wait_ge(sem("attended"), n["unit"])
                    if dest is None:
                        pe.wait_ge(sem("convolved"), more("convolved"))
                for _ in range(count):
                    columns(panel(), range(4), src, segs)

            def mlp(segs, beside):
                ready = "h_act"
                ends = {}
                for step, (kind, g) in enumerate(mlp_steps(len(FF1_GROUPS))):
                    if beside and step in MOD_STEPS:
                        mod(1, 2 * (step - MOD_STEPS[0]), 2 * (step - MOD_STEPS[0]) + 2)
                    if kind == "down":
                        if ends[g] > 0:
                            pe.wait_ge(sem("tile_free"), ends[g])
                    for _ in range(2):
                        columns(panel(), range(4), H if kind == "up" else hidden1[g % 2], segs, KD, ready)
                        ready = None
                    ends[g] = n["tile"]

            def swiglu():
                ready = "h_dve"
                ends = {}
                for kind, g in mlp_steps(len(FF2_GROUPS)):
                    if kind == "up":
                        for _ in range(FF2_GROUPS[g] // 2):
                            columns(panel(), range(4), H, SEG1, KD, ready)
                            ready = None
                        ends[g] = n["tile"]
                    else:
                        if ends[g] > 0:
                            pe.wait_ge(sem("tile_free"), ends[g])
                        for _ in range(2):
                            columns(panel(), range(4), hidden2[g % 2], SEG1, FF2_GROUPS[g])

            def odd_in():
                n["h_act"] += KD
                w = panel()
                columns(w, [0], K, SEG2, ready="mix")
                columns(w, [1], MIX, SEG2, ready="mix")
                columns(w, [2], K, SEG1, ready="mix")
                ready = "mix"
                for _ in range(2):
                    columns(panel(), range(4), MIX, SEG2, ready=ready)
                    ready = None
                ready = "mix"
                for h in range(2):
                    w = panel()
                    lo = C if h == 0 else 0
                    for c in range(CHUNKS):
                        accumulate(tile()[lo:lo + C, :], lambda k: MIX[:, k, c * C:(c + 1) * C], lambda k: w[:, k, :],
                                   KD, ready)
                        ready = None
                panel()
                ready = "mix"
                for _ in range(2):
                    columns(panel(), range(4), XX, SEG1, ready=ready)
                    ready = None
                if n["tile"] > 0:
                    pe.wait_ge(sem("tile_free"), n["tile"])
                pe.wait_ge(sem("lora"), more("lora", 3))
                if n["norm"] > 0:
                    pe.wait_ge(sem("var"), n["norm"])

            def half(h):
                return slice(C * h, C * h + C)

            def features(j, i):
                p, d = divmod(j, 2)
                for at_slot, what in FEATURE_SLOTS:
                    if at_slot != i or (what == "norm" and d == 1):
                        continue
                    for a, b in SEG2:
                        if n["feature_pe"] > 0:
                            pe.wait_ge(sem("feature_read"), n["feature_pe"])
                        if what == "norm":
                            pe.wait_ge(sem("key_square"), more("key_square"))
                            left, right = head_ones, square[:, 0, a:b]
                        elif what == "decay":
                            left, right = lora2[half(d), 0, p * P:(p + 1) * P], decay_in[half(d), a:b]
                        else:
                            left, right = lora2[half(d), 1, p * P:(p + 1) * P], a_in[half(d), a:b]
                        pe.matmul(ps[:, 5, 0:b - a], left, right, start=True, stop=True).then_inc(
                            sem("feature_pe"), one("feature_pe"))

            def prepare(j, i):
                p, d = divmod(j, 2)
                S = sets[d]
                if 1 <= i <= GRAMS:
                    g = i - 1
                    if g == 0:
                        pe.wait_ge(sem("keys"), more("keys"))
                        pe.wait_ge(sem("decayed"), more("decayed"))
                    if GRAMS * j + g - 1 > 0:
                        pe.wait_ge(sem("gram_read"), GRAMS * j + g - 1)
                    if GRAMS * j + g > 0:
                        pe.wait_ge(sem("gram_copied"), GRAMS * j + g)
                    bank = 2 * (g % 2)
                    pair = (2 * g, 2 * g + 1)
                    for n_c, c in enumerate(pair):
                        for h in range(2):
                            right = S["kr"][half(h), c, :, :] if c < LAT // C else S["kr"][half(h), c, 0:1, :]
                            wd = 2 * C if c < LAT // C else C
                            o = n_c * 2 * C
                            pe.matmul(ps[:, bank + h, o:o + wd], bk[half(h), c, :, :].rearrange("p a b -> p (a b)"),
                                      right.rearrange("p a b -> p (a b)"), start=True, stop=True)
                    for n_c, c in enumerate(pair):
                        for h in range(2):
                            pe.matmul(ps[half(h), 4, n_c * C:(n_c + 1) * C], S["kr"][half(h), c, 0, :], bk[half(h), c, h, :],
                                      start=True, stop=True)
                    for n_c, c in enumerate(pair):
                        o = (1 + n_c) * P
                        ins = pe.transpose(ps[:, 4, o:o + P], bk[:, c, :, :].rearrange("p a b -> p (a b)"), ident)
                    ins.then_inc(sem("gram"), one("gram"))
                elif i == INVERSE - 1:
                    pe.wait_ge(sem("values"), more("values"))
                    pe.wait_ge(sem("gram_read"), GRAMS * (j + 1))
                    pe.wait_ge(sem("gram_copied"), GRAMS * (j + 1))
                    for b in range(2):
                        batch(b, b, lambda c, h: couple[half(1 - h), h, c, :], lambda c, h: S["uv"][half(1 - h), c, h, :]
                              ).then_inc(sem("value_product"), one("value_product"))
                elif INVERSE < i <= INVERSE + 3 * (LEVELS - 1):
                    level, q = divmod(i - INVERSE - 1, 3)
                    for b in range(2):
                        if q == 0:
                            if b == 0:
                                pe.wait_ge(sem("masked"), (LEVELS) * j + level + 2)
                            pe.wait_ge(sem("inverse"), 2 * (LEVELS * j + level) + b + 1)
                            pe.wait_ge(sem("values_read"), 2 * j + b + 1)
                            batch(b, b, lambda c, h: f_am[half(h), c, :], lambda c, h: f_x[half(h), c, :]).then_inc(
                                sem("first_product"), one("first_product"))
                        elif q == 1:
                            pe.wait_ge(sem("first_copied"), more("first_copied"))
                            if level < LEVELS - 2:
                                batch(2 + b, b, lambda c, h: S["xt"][half(h), c, :], lambda c, h: f_y1[half(h), c, :]
                                      ).then_inc(sem("second_product"), one("second_product"))
                        else:
                            batch(b, b, lambda c, h: f_y1[half(h), c, :], lambda c, h: S["xt"][half(h), c, :]).then_inc(
                                sem("third_product"), one("third_product"))

            def batch(bank, b, left, right):
                for k in range(HALF):
                    for h in range(2):
                        ins = pe.matmul(ps[half(h), bank, k * C:(k + 1) * C], left(b * HALF + k, h), right(b * HALF + k, h),
                                        start=True, stop=True)
                return ins

            def state_in(j, s):
                d = j % 2
                S, c = sets[d], chunk_order(d)[s]
                if s == 0:
                    pe.wait_ge(sem("inverse"), 2 * LEVELS * (j + 1))
                pe.wait_ge(sem("state"), more("state"))
                for h in range(2):
                    ins = pe.matmul(ps[half(h), 6, 0:C], S["kr"][half(h), c, 0, :], state[half(h), d, :],
                                    start=True, stop=True)
                ins.then_inc(sem("from_state"), one("from_state"))

            def solve(j, s):
                d = j % 2
                S, c = sets[d], chunk_order(d)[s]
                pe.wait_ge(sem("residual"), more("residual"))
                for h in range(2):
                    ins = pe.matmul(ps[half(h), 6, C:2 * C], S["xt"][half(h), c, :], w0_neg[half(h), d, :],
                                    start=True, stop=True)
                ins.then_inc(sem("solved"), one("solved"))
                if c < LAT // C:
                    if n["y"] > 0:
                        pe.wait_ge(sem("y_read"), n["y"])
                    for h in range(2):
                        pe.matmul(ps[half(h), 7, 0:C], state[half(h), d, :], S["kr"][half(h), c, 1, :],
                                  start=True, stop=False)

            def state_out(j, s):
                d = j % 2
                S, c = sets[d], chunk_order(d)[s]
                pe.wait_ge(sem("update"), more("update"))
                if s < CHUNKS - 1:
                    for h in range(2):
                        ins = pe.matmul(ps[half(h), 6, 2 * C:3 * C], S["bkn"][:, c, half(h)], S["uv"][:, c, h, :],
                                        start=True, stop=True)
                    ins.then_inc(sem("to_state"), one("to_state"))
                if c < LAT // C:
                    for h in range(2):
                        ins = pe.matmul(ps[half(h), 7, 0:C], S["uv"][:, c, h, :], S["gram"][:, c, h, :],
                                        start=False, stop=True)
                    ins.then_inc(sem("y"), one("y"))

            def readout(p):
                pe.wait_ge(sem("read_dve"), more("read_dve"))
                n["read_dve"] += 2
                pe.matmul(ps[:, 0, :], head_ones, y_pair, start=True, stop=True).then_inc(sem("read_pe"), one("read_pe"))
                pe.matmul(ps[:, 1, :], head_ones, R[:, p, :], start=True, stop=True)
                for c in range(LAT // C):
                    for h in range(2):
                        pe.matmul(ps[half(h), 2, c * C:(c + 1) * C], V[half(1 - h), c, p, :],
                                  ccol("ident2", 0, C)[half(1 - h), :], start=True, stop=True)
                pe.matmul(ps[:, 3, :], lora2[:, 2, p * P:(p + 1) * P], gate_in, start=True, stop=True).then_inc(sem("read_pe"), one("read_pe"))
                pe.wait_ge(sem("read_act"), more("read_act"))
                pe.matmul(ps[:, 4, :], head_ones, square[:, 0, 0:LAT], start=True, stop=True).then_inc(sem("read_pe"), one("read_pe"))
                pe.wait_ge(sem("r_out"), more("r_out"))

            def mix_in(l):
                w = panel()
                columns(w, range(2), H, SEGM, ready="h_dve")
                for t in range(2):
                    accumulate(tile()[:, 0:CTX], lambda k: H[:, k, LAT + t * P:LAT + (t + 1) * P],
                               lambda k: w[:, k, CTX:2 * CTX])
                ready = "h_dve"
                for _ in range(3):
                    columns(panel(), range(4), H, SEG1, ready=ready)
                    ready = None
                rows(panel(), 0, P, H, range(LAT // P), 0)
                for i in range(8):
                    sums(head_ones, 1, 0, LAT if i < 6 else CTX)
                    if i < 4:
                        pe.wait_ge(sem("normed"), more("normed"))
                        pe.matmul(ps[:, 5, :], rotate, q2[:, i, :], start=True, stop=True).then_inc(sem("rotated"), one("rotated"))

            def conv(l):
                pe.wait_ge(sem("tapped"), more("tapped"))
                sums(ones[:, :], 3, 0, LAT, "conv")
                sums(ones[:, :], 3, 0, LAT)

            skip = lambda *a: None
            model(dict(load=load, mod=mod, gains=skip, norm_mod=norm_mod, even_in=even_in, attention=attention,
                       project=project, post=post, mlp=mlp, odd_in=odd_in, features=features, prepare=prepare, state_in=state_in,
                       solve=solve, state_out=state_out, readout=readout, odd_out=skip, tables=skip,
                       norm_vec=norm_vec, swiglu=swiglu, half_step=skip, mix_in=mix_in, conv=conv, store=skip))

        @block.scalar
        def _(act):
            n, more, one = counting()
            sigmoid_used = [0, 0]

            def load():
                act.wait_ge(sem("small_in"), 48)
                act.activation(silu_c[:, :, :], raw_c[:, :, :], ACT.Sigmoid).then_inc(sem("sigmoid_c"), one("sigmoid_c"))
                n["source"] = "load"

            def squares(src, count, lo, hi, ready):
                if sigmoid_used[-1] > 0:
                    act.wait_ge(sem("tile_free"), sigmoid_used[-1])
                for c in range(count):
                    ready(c)
                    if n["sq"] - 1 + n["plain_sums"] > 0:
                        act.wait_ge(sem("summed"), n["sq"] - 1 + n["plain_sums"])
                    act.activation(square[:, n["sq"] % 2, 0:hi - lo], src(c), ACT.Square).then_inc(sem("square"), one("square"))
                    n["sq"] += 1
                act.wait_ge(sem("var"), more("var"))
                act.activation(rstd[:, 0:hi - lo], rstd[:, 0:hi - lo], ACT.Sqrt).then_inc(sem("std"), one("std"))

            def source():
                kind = n["source"]
                if kind == "load":
                    act.wait_ge(sem("x_in"), 16)
                    return lambda c: None
                if kind == "x_chunk":
                    base = n["x_chunk"] - KD
                    return lambda c: act.wait_ge(sem("x_chunk"), base + c + 1)
                base = n["tile"] - KD
                return lambda c: act.wait_ge(sem("tile_free"), base + c + 1)

            def mod(i, lo, hi):
                n["tile"] += hi - lo

            def norm_mod(i, which):
                hi = TOK if (i, which) != (1, 2) else LAT
                squares(lambda c: X[:, c, 0:hi], KD, 0, hi, source())
                act.wait_ge(sem("gains"), more("gains")) if which == 0 and i == 0 else None
                if (i, which) != (0, 0):
                    if 1 + 1 if i == 0 else 4 > 0:
                        act.wait_ge(sem("gains"), 1 + 1 if i == 0 else 4)
                for c in range(KD):
                    act.wait_ge(sem("scaled"), more("scaled"))
                    for v, (a, b) in enumerate(((0, LAT), (LAT, TOK))):
                        if b <= hi:
                            ins = act.activation(H[:, c, a:b], H[:, c, a:b], ACT.Identity,
                                                 bias=mod_col(i, 3 * (which // 2), v, c), scale=gain[:, i, which, v, c:c + 1])
                    ins.then_inc(sem("h_act"), one("h_act"))

            def mod_col(i, part, v, c):
                return mod_sb[:, i, v, part * KD + c:part * KD + c + 1]

            def norm_vec(lo, hi, name, l, src):
                if lo == LAT:
                    act.wait_ge(sem("mem_in"), 16)
                    ready = lambda c: None
                else:
                    ready = source()
                squares(lambda c: X[:, c, lo:hi], KD, lo, hi, ready)
                if name == "final_norm":
                    n["x_chunk"] += KD
                    n["source"] = "x_chunk"

            def even_in():
                n["tile"] += 24 + TOK // P + 8 + 8

            def attention(units, l):
                base = n["unit"]
                for i in range(len(units) + 2):
                    if i < len(units):
                        unit, u = units[i], base + i
                        w = unit["width"]
                        act.wait_ge(sem("row_max"), more("row_max"))
                        act.activation(probs[:, u % 3, 0:w], probs[:, u % 3, 0:w], ACT.Exp,
                                           bias=stat[:, 4 * (u % 3) + 1:4 * (u % 3) + 2],
                                           accum_out=stat[:, 4 * (u % 3) + 2:4 * (u % 3) + 3]).then_inc(sem("exped"), one("exped"))
                        if unit["sink"] is not None:
                            act.activation(stat[:, 4 * (u % 3) + 3:4 * (u % 3) + 4], unit["sink"], ACT.Exp,
                                               bias=stat[:, 4 * (u % 3) + 1:4 * (u % 3) + 2]).then_inc(sem("exped_sink"), one("exped_sink"))
                    if i >= 2:
                        unit, u = units[i - 2], base + i - 2
                        w = unit["width"]
                        act.wait_ge(sem("turned"), more("turned"))
                        if u - 1 > 0:
                            act.wait_ge(sem("output"), u - 1)
                        act.copy(probsT[:, u % 2, 0:w], turned_ps(w)).then_inc(sem("turned_copy"), one("turned_copy"))
                n["unit"] += len(units)

            def project(count, segs, src, dest, ready):
                n["tile"] += 4 * count * len(segs)
                n["source"] = "tile"
                n["last"] = len(segs)

            def post(src, i, which):
                hi = TOK if i == 0 else LAT
                nseg = n["last"]
                base = n["tile"] - KD * nseg
                squares(lambda c: src[:, c, 0:hi], KD, 0, hi, lambda c: act.wait_ge(sem("tile_free"), base + nseg * (c + 1)))
                n["x_chunk"] += KD
                n["source"] = "x_chunk"

            def mlp(segs, beside):
                for step, (kind, g) in enumerate(mlp_steps(len(FF1_GROUPS))):
                    if beside and step in MOD_STEPS:
                        mod(1, 2 * (step - MOD_STEPS[0]), 2 * (step - MOD_STEPS[0]) + 2)
                    for c in range(8):
                        for a, b in segs:
                            if kind == "up":
                                if n["tile"] + 1 > 0:
                                    act.wait_ge(sem("tile_done"), n["tile"] + 1)
                                act.activation(hidden1[g % 2][:, c, a:b], ps[:, n["tile"] % 4, 0:b - a], ACT.Relu).then_inc(sem("relu"), one("relu"))
                            n["tile"] += 1
                n["last"] = len(segs)

            def swiglu():
                for kind, g in mlp_steps(len(FF2_GROUPS)):
                    if kind == "down":
                        n["tile"] += 8
                        continue
                    for c in range(FF2_GROUPS[g]):
                        if sigmoid_used[-2] > 0:
                            act.wait_ge(sem("tile_free"), sigmoid_used[-2])
                        if n["tile"] + 1 > 0:
                            act.wait_ge(sem("tile_done"), n["tile"] + 1)
                        sigmoid_used.append(n["tile"] + 1)
                        act.activation(sig[:, n["sig"] % 2, :], ps[:, n["tile"] % 4, :], ACT.Sigmoid).then_inc(sem("sigmoid"), one("sigmoid"))
                        n["sig"] += 1
                        n["tile"] += 2

            def half_step():
                n["x_chunk"] += KD
                n["source"] = "x_chunk"

            def odd_in():
                base = n["tile"]
                n["tile"] += 5 + 16 + 2 * CHUNKS + 8
                if 6 * KD > 0:
                    act.wait_ge(sem("mix"), 6 * KD)
                if base + 5 > 0:
                    act.wait_ge(sem("tile_free"), base + 5)
                act.activation(decay_in, square[:, 0, :], ACT.Tanh).then_inc(sem("lora"), one("lora"))
                act.copy(a_in, square[:, 1, :]).then_inc(sem("lora"), one("lora"))
                act.activation(gate_in, rstd[:, 0:LAT], ACT.Sigmoid).then_inc(sem("lora"), one("lora"))
                if 3 > 0:
                    act.wait_ge(sem("lora"), 3)

            def half(h):
                return slice(C * h, C * h + C)

            def features(j, i):
                p, d = divmod(j, 2)
                for at_slot, what in FEATURE_SLOTS:
                    if at_slot != i or (what == "norm" and d == 1):
                        continue
                    if what == "norm":
                        act.wait_ge(sem("feature_dve"), more("feature_dve"))
                        for a, b in SEG2:
                            act.activation(square[:, 0, a:b], f_kk[:, a:b], ACT.Square).then_inc(
                                sem("key_square"), one("key_square"))
                            act.wait_ge(sem("feature_pe"), more("feature_pe"))
                            act.copy(rstd[:, a:b], ps[:, 5, 0:b - a]).then_inc(sem("feature_read"), one("feature_read"))
                        act.wait_ge(sem("feature_dve"), more("feature_dve"))
                        act.activation(rstd[:, :], rstd[:, :], ACT.Sqrt).then_inc(sem("key_root"), one("key_root"))
                        continue
                    if what == "decay":
                        act.wait_ge(sem("exponents"), 2 * j) if j > 0 else None
                        dest, bias = f_cs, vcol(f"w0{d}", p)
                    else:
                        act.wait_ge(sem("keys"), j) if j > 0 else None
                        dest, bias = f_a, vcol(f"a0{d}", p)
                    for a, b in SEG2:
                        act.wait_ge(sem("feature_pe"), more("feature_pe"))
                        act.activation(dest[:, a:b], ps[:, 5, 0:b - a], ACT.Sigmoid, bias=bias).then_inc(
                            sem("feature_read"), one("feature_read"))
                if i == EXPONENT_SLOT:
                    act.wait_ge(sem("running"), more("running"))
                    act.wait_ge(sem("decayed"), j) if j > 0 else None
                    act.wait_ge(sem("keys"), j) if j > 0 else None
                    act.activation(f_inc, f_cs, ACT.Exp, scale=-E_HALF).then_inc(sem("exponents"), one("exponents"))
                    act.activation(f_inv, f_cs, ACT.Exp, scale=E_HALF).then_inc(sem("exponents"), one("exponents"))

            def prepare(j, i):
                p, d = divmod(j, 2)
                S = sets[d]
                if 1 <= i <= GRAMS:
                    c = 2 * (i - 1)
                    act.wait_ge(sem("gram"), more("gram"))
                    bank = ps[:, 4, :]
                    act.copy(S["bkn"][:, c:c + 2, :], bank[:, P:3 * P].rearrange("p (a b) -> p a b", a=2))
                    act.copy(f_x[:, c:c + 2, :], bank[:, 0:P].rearrange("p (a b) -> p a b", a=2)).then_inc(
                        sem("gram_copied"), one("gram_copied"))
                elif i == INVERSE - 1:
                    for b in range(2):
                        act.wait_ge(sem("value_product"), more("value_product"))
                        act.mul(S["bv"][:, b * HALF:(b + 1) * HALF, :], chunked(ps[:, b, 0:HALF * C]), -1.0).then_inc(
                            sem("values_read"), one("values_read"))
                elif INVERSE < i <= INVERSE + 3 * (LEVELS - 1):
                    level, q = divmod(i - INVERSE - 1, 3)
                    if q == 0:
                        for b in range(2):
                            act.wait_ge(sem("first_product"), more("first_product"))
                            act.copy(f_y1[:, b * HALF:(b + 1) * HALF, :], chunked(ps[:, b, 0:HALF * C])).then_inc(
                                sem("first_copied"), one("first_copied"))

            def solve(j, s):
                d = j % 2
                S, c = sets[d], chunk_order(d)[s]
                act.wait_ge(sem("solved"), more("solved"))
                for h in range(2):
                    ins = act.copy(S["uv"][half(h), c, h, :], ps[half(h), 6, C:2 * C])
                ins.then_inc(sem("update"), one("update"))

            def readout(p):
                act.wait_ge(sem("read_pe"), more("read_pe", 2))
                act.copy(v_turned, ps[:, 2, :]).then_inc(sem("read_act_v"), one("read_act_v"))
                act.wait_ge(sem("read_dve"), more("read_dve", 2))
                act.activation(square[:, 0, 0:LAT], y_pair, ACT.Square).then_inc(sem("read_act"), one("read_act"))
                n["read_pe"] += 1
                act.wait_ge(sem("read_dve"), more("read_dve"))
                act.activation(rstd[:, 0:LAT], rstd[:, 0:LAT], ACT.Sqrt).then_inc(sem("read_act_root"), one("read_act_root"))

            def tables():
                act.wait_ge(sem("angle"), more("angle"))
                act.activation(rope[:, 1, :], rope_tmp[:, 0, :], ACT.Sin).then_inc(sem("sine"), one("sine"))
                act.activation(rope[:, 0, :], rope_tmp[:, 0, :], ACT.Sin, scale=0.5).then_inc(sem("sine"), one("sine"))

            def mix_in(l):
                n["tile"] += 4
                base = n["tile"]
                for m in (1, 3, 5):
                    if sigmoid_used[-2] > 0:
                        act.wait_ge(sem("tile_free"), sigmoid_used[-2])
                    if base + m + 1 > 0:
                        act.wait_ge(sem("tile_done"), base + m + 1)
                    sigmoid_used.append(base + m + 1)
                    act.activation(sig[:, n["sig"] % 2, :], ps[:, (base + m) % 4, :], ACT.Sigmoid).then_inc(sem("sigmoid"), one("sigmoid"))
                    n["sig"] += 1
                n["tile"] += 12 + LAT // P
                for i in range(8):
                    src = q2[:, i, :] if i < 6 else mk2[:, i - 6, :]
                    squares(lambda c: src, 1, 0, LAT if i < 6 else CTX, lambda c: act.wait_ge(sem("tile_free"), n["tile"]))

            def conv(l):
                act.wait_ge(sem("tapped"), more("tapped"))
                n["plain_sums"] += 3
                n["var"] += 1
                squares(lambda c: conv_y[:, c, :], 3, 0, LAT, lambda c: act.wait_ge(sem("centred"), more("centred")))
                for c in range(3):
                    act.wait_ge(sem("conv_z"), more("conv_z"))
                    act.activation(sig[:, c % 2, :] if c < 2 else rstd[:, 0:LAT], conv_y[:, c, :], ACT.Sigmoid).then_inc(sem("conv_sigmoid"), one("conv_sigmoid"))

            skip = lambda *a: None
            model(dict(load=load, mod=mod, gains=skip, norm_mod=norm_mod, even_in=even_in, attention=attention,
                       project=project, post=post, mlp=mlp, odd_in=odd_in, features=features, prepare=prepare, state_in=skip, solve=solve,
                       state_out=skip, readout=readout, odd_out=skip, tables=tables, norm_vec=norm_vec, swiglu=swiglu,
                       half_step=half_step, mix_in=mix_in, conv=conv, store=skip))

        @block.vector
        def _(dve):
            n, more, one = counting()

            def settle(ins):
                ins.then_inc(sem("own"), one("own"))
                dve.wait_ge(sem("own"), n["own"])

            def tile():
                dve.wait_ge(sem("tile_done"), more("tile_done"))
                n["tile"] += 1
                return ps[:, (n["tile"] - 1) % 4, :]

            def load():
                dve.wait_ge(sem("small_in"), 48)
                settle(dve.tensor_scalar(omka[:, :], vcol("ka", 0, KD), -1.0, 1.0, ALU.mult, ALU.add))
                dve.wait_ge(sem("sigmoid_c"), more("sigmoid_c"))
                dve.tensor_tensor(silu_c[:, :, :], silu_c[:, :, :], raw_c[:, :, :], ALU.mult).then_inc(sem("silu"), one("silu"))

            def mod(i, lo, hi):
                for j in range(lo, hi):
                    bank = tile()
                    b = vcol(f"ada_b{i}", 4 * j, 4)
                    for v in range(2):
                        ins = dve.tensor_tensor(mod_sb[:, i, v, 4 * j:4 * j + 4], bank[:, v:8:2], b, ALU.add)
                    ins.then_inc(sem("tile_free"), one("tile_free"))

            def gains(i, part):
                if n["tile"] > 0:
                    dve.wait_ge(sem("tile_free"), n["tile"])
                for which in ((0,), (1, 2, 3))[part]:
                    for v in range(2):
                        g = vcol(f"norm_g{i}{which}", 0, KD)
                        chunk = (1, 2, 4, 5)[which]
                        m = mod_sb[:, i, v, chunk * KD:(chunk + 1) * KD]
                        ins = dve.scalar_tensor_tensor(gain[:, i, which, v, :], m, 0.0 if which % 2 else 1.0, g, ALU.add,
                                                       ALU.mult)
                ins.then_inc(sem("gains"), one("gains"))
                dve.wait_ge(sem("gains"), n["gains"])

            def inverse_root(count, lo, hi, mean, eps, op=ALU.add):
                dve.wait_ge(sem("summed"), more("summed", count))
                r = rstd[:, 0:hi - lo]
                dve.tensor_scalar(r, norm_psum(lo, hi), mean, eps, ALU.mult, op).then_inc(sem("var"), one("var"))
                dve.wait_ge(sem("std"), more("std"))
                settle(dve.reciprocal(r, r))
                return r

            def norm_mod(i, which):
                hi = TOK if (i, which) != (1, 2) else LAT
                r = inverse_root(KD, 0, hi, 1.0 / D, 1e-6)
                for c in range(KD):
                    dve.tensor_tensor(H[:, c, 0:hi], X[:, c, 0:hi], r, ALU.mult).then_inc(sem("scaled"), one("scaled"))
                n["h_act"] += KD

            def norm_vec(lo, hi, name, l, src):
                r = inverse_root(KD, lo, hi, 1.0 / D, 1e-6)
                dest, signal = (X, "x_chunk") if name == "final_norm" else (H, "h_dve")
                for c in range(KD):
                    dve.scalar_tensor_tensor(dest[:, c, lo:hi], X[:, c, lo:hi], vcol(f"{name}{l}", c), r, ALU.mult,
                                                 ALU.mult).then_inc(sem(signal), one(signal))
                dve.wait_ge(sem(signal), n[signal])

            def copies(dest, ms, segs):
                for m in ms:
                    for a, b in segs:
                        dve.tensor_copy(dest[:, m, a:b], tile()[:, 0:b - a]).then_inc(sem("tile_free"), one("tile_free"))

            def even_in():
                u, s0, s1 = pool_buf
                GAP = 8
                parts = ((0, LAT, GAP), (LAT, TOK, GAP + LAT + GAP))
                settle(dve.memset(u, 0.0))
                for g, w in enumerate(POOL_WINDOWS):
                    for a, b, o in parts:
                        dve.tensor_copy(u[:, o:o + b - a], tile()[:, 0:b - a]).then_inc(sem("tile_free"), one("tile_free"))
                    dve.wait_ge(sem("tile_free"), n["tile_free"])
                    src, width = u, 1
                    while width < w:
                        dest = s0 if src is not s0 else s1
                        m = 792 - 2 * width + 1
                        settle(dve.tensor_tensor(dest[:, 0:m], src[:, 0:m], src[:, width:width + m], ALU.add))
                        src, width = dest, 2 * width
                    edge = ccol("pool_edge", 2 * (w // 2 - 1), w)
                    diff = Y[:, 4 + g, :]
                    for a, b, o in parts:
                        ins = dve.tensor_scalar(diff[:, a:b], src[:, o - w // 2:o - w // 2 + b - a], 1.0 / w, None, ALU.mult)
                    settle(ins)
                    for a, b, o in parts:
                        dve.tensor_tensor(diff[:, a:a + w // 2], diff[:, a:a + w // 2], edge[:, 0:w // 2], ALU.mult)
                        ins = dve.tensor_tensor(diff[:, b - w // 2:b], diff[:, b - w // 2:b], edge[:, w // 2:w], ALU.mult)
                    settle(ins)
                    for a, b, o in parts:
                        ins = dve.tensor_tensor(diff[:, a:b], diff[:, a:b], u[:, o:o + b - a], ALU.subtract)
                    ins.then_inc(sem("pooled"), one("pooled"))
                    dve.wait_ge(sem("pooled"), n["pooled"])
                mod(0, 4, 6)
                copies(qT, range(4), SEG2)
                mod(0, 6, 8)
                copies(kT, range(4), SEG2)
                mod(0, 8, 10)
                for t in range(TOK // P):
                    dve.tensor_copy(vN[:, t, :], tile()).then_inc(sem("tile_free"), one("tile_free"))
                mod(0, 10, 12)
                for g in range(4):
                    for a, b in SEG2:
                        dve.tensor_scalar(Y[:, g, a:b], tile()[:, 0:b - a], vcol("pool_scale", g), None, ALU.mult).then_inc(sem("tile_free"), one("tile_free"))

            def conv_tap(l, tap):
                for c in range(3):
                    w, src = vcol(f"conv_w{l}", c * TAPS + tap), conv_in[:, c, tap:tap + LAT]
                    if tap == 0:
                        ins = dve.tensor_scalar(conv_y[:, c, :], src, w, vcol(f"conv_b{l}", c), ALU.mult, ALU.add)
                    else:
                        dve.wait_ge(sem("tap"), n["tap"] - 2)
                        ins = dve.scalar_tensor_tensor(conv_y[:, c, :], src, w, conv_y[:, c, :], ALU.mult, ALU.add)
                    ins.then_inc(sem("tap"), one("tap"))

            def attention(units, l):
                base = n["unit"]
                scale = C ** -0.5
                for i in range(len(units) + 4):
                    if i < len(units):
                        unit, u = units[i], base + i
                        w, o = unit["width"], 4 * (u % 3)
                        dve.wait_ge(sem("scores"), more("scores"))
                        if u - 2 > 0:
                            dve.wait_ge(sem("turned"), u - 2)
                        S, raw = probs[:, u % 3, :], scores_ps(u, w)
                        wb = 0
                        if unit["bias"] is not None:
                            wb = min(w, LAT)
                            if unit["bias_head"] is not None:
                                h = unit["bias_head"]
                                dve.wait_ge(sem(f"bias{h % 2}"), 16 * (h // 2 + 1))
                            ins = dve.scalar_tensor_tensor(S[:, 0:wb], raw[:, 0:wb], scale, unit["bias"], ALU.mult, ALU.add)
                        if wb < w:
                            ins = dve.tensor_scalar(S[:, wb:w], raw[:, wb:w], scale, None, ALU.mult)
                        ins.then_inc(sem("scored"), one("scored"))
                        dve.wait_ge(sem("scored"), n["scored"])
                        settle(dve.tensor_reduce(stat[:, o:o + 1], S[:, 0:w], AX.X, ALU.max))
                        if unit["sink"] is not None:
                            settle(dve.tensor_tensor(stat[:, o:o + 1], stat[:, o:o + 1], unit["sink"], ALU.max))
                        dve.tensor_scalar(stat[:, o + 1:o + 2], stat[:, o:o + 1], -1.0, None, ALU.mult).then_inc(sem("row_max"), one("row_max"))
                    if 1 <= i <= len(units):
                        unit, u = units[i - 1], base + i - 1
                        w, o = unit["width"], 4 * (u % 3)
                        dve.wait_ge(sem("exped"), more("exped"))
                        if unit["sink"] is not None:
                            dve.wait_ge(sem("exped_sink"), more("exped_sink"))
                            settle(dve.tensor_tensor(stat[:, o + 2:o + 3], stat[:, o + 2:o + 3], stat[:, o + 3:o + 4], ALU.add))
                        settle(dve.reciprocal(stat[:, o + 2:o + 3], stat[:, o + 2:o + 3]))
                        dve.tensor_scalar(probs[:, u % 3, 0:w], probs[:, u % 3, 0:w], stat[:, o + 2:o + 3], None,
                                              ALU.mult).then_inc(sem("probs"), one("probs"))
                    if l is not None and i < TAPS:
                        conv_tap(l, i)
                    if i >= 4:
                        unit, u = units[i - 4], base + i - 4
                        b = unit["base"]
                        dve.wait_ge(sem("output"), more("output"))
                        dve.tensor_copy(unit["dest"], ps[b:b + C, 6 + u % 2, 0:P]).then_inc(sem("attended"), one("attended"))
                n["unit"] += len(units)

            def project(count, segs, src, dest, ready):
                for c in range(4 * count):
                    for a, b in segs:
                        bank = tile()[:, 0:b - a]
                        if dest is None:
                            ins = dve.tensor_tensor(X[:, c, a:b], bank, X[:, c, a:b], ALU.add)
                        else:
                            ins = dve.tensor_copy(dest[:, c, a:b], bank)
                        ins.then_inc(sem("tile_free"), one("tile_free"))

            def post(src, i, which):
                streams = ((0, LAT), (LAT, TOK)) if i == 0 else ((0, LAT),)
                hi = streams[-1][1]
                r = inverse_root(KD, 0, hi, 1.0 / D, 1e-6)
                if (i, which) == (1, 1):
                    dve.wait_ge(sem("x_back"), 16)
                for c in range(KD):
                    for v, (a, b) in enumerate(streams):
                        ins = dve.scalar_tensor_tensor(src[:, c, a:b], src[:, c, a:b], gain[:, i, which, v, c:c + 1],
                                                       r[:, a:b], ALU.mult, ALU.mult)
                    ins.then_inc(sem("gated"), one("gated"))
                for c in range(KD):
                    dve.wait_ge(sem("gated"), n["gated"] - KD + c + 1)
                    dve.tensor_tensor(X[:, c, 0:hi], X[:, c, 0:hi], src[:, c, 0:hi], ALU.add).then_inc(sem("x_chunk"), one("x_chunk"))

            def add_up(c, a, b, first):
                bank = tile()[:, 0:b - a]
                if first:
                    dve.tensor_copy(Y[:, c, a:b], bank).then_inc(sem("tile_free"), one("tile_free"))
                else:
                    dve.tensor_tensor(Y[:, c, a:b], bank, Y[:, c, a:b], ALU.add).then_inc(sem("tile_free"), one("tile_free"))

            def mlp(segs, beside):
                for step, (kind, g) in enumerate(mlp_steps(len(FF1_GROUPS))):
                    if beside and step in MOD_STEPS:
                        mod(1, 2 * (step - MOD_STEPS[0]), 2 * (step - MOD_STEPS[0]) + 2)
                    for c in range(8):
                        for a, b in segs:
                            if kind == "up":
                                bank = tile()[:, 0:b - a]
                                dve.wait_ge(sem("relu"), more("relu"))
                                hid = hidden1[g % 2][:, c, a:b]
                                dve.tensor_tensor(hid, hid, bank, ALU.mult).then_inc(sem("tile_free"), one("tile_free"))
                            else:
                                add_up(c, a, b, g == 0)

            def swiglu():
                for kind, g in mlp_steps(len(FF2_GROUPS)):
                    for c in range(8 if kind == "down" else FF2_GROUPS[g]):
                        if kind == "up":
                            bank = tile()
                            dve.wait_ge(sem("sigmoid"), more("sigmoid"))
                            hid = hidden2[g % 2][:, c, :]
                            dve.tensor_tensor(hid, bank, sig[:, n["sig"] % 2, :], ALU.mult).then_inc(sem("tile_free"), one("tile_free"))
                            n["sig"] += 1
                            gate = tile()
                            dve.wait_ge(sem("tile_free"), n["tile_free"])
                            dve.tensor_tensor(hid, gate, hid, ALU.mult).then_inc(sem("tile_free"), one("tile_free"))
                        else:
                            add_up(c, 0, LAT, g == 0)

            def half_step():
                if n["tile_free"] > 0:
                    dve.wait_ge(sem("tile_free"), n["tile_free"])
                for c in range(KD):
                    dve.scalar_tensor_tensor(X[:, c, 0:LAT], Y[:, c, 0:LAT], 0.5, X[:, c, 0:LAT], ALU.mult, ALU.add).then_inc(sem("x_chunk"), one("x_chunk"))

            def odd_in():
                if n["h_act"] > 0:
                    dve.wait_ge(sem("h_act"), n["h_act"])
                for a, b in ((0, LAT), (LAT, TOK)):
                    dve.tensor_tensor(XX[:, :, a + 1:b - 1], H[:, :, a:b - 2], H[:, :, a + 2:b], ALU.add)
                    dve.tensor_copy(XX[:, :, a:a + 1], H[:, :, a + 1:a + 2])
                    ins = dve.tensor_copy(XX[:, :, b - 1:b], H[:, :, b - 2:b - 1])
                settle(ins)
                settle(dve.scalar_tensor_tensor(XX, XX, 0.5, H, ALU.mult, ALU.subtract))

                def mix(mu, dest, hi):
                    for c in range(KD):
                        dve.scalar_tensor_tensor(dest[:, c, 0:hi], XX[:, c, 0:hi], vcol(f"mu{mu}", c), H[:, c, 0:hi],
                                                     ALU.mult, ALU.add).then_inc(sem("mix"), one("mix"))

                def raw(dest, segs):
                    for a, b in segs:
                        dve.tensor_copy(dest[:, a:b], tile()[:, 0:b - a]).then_inc(sem("tile_free"), one("tile_free"))

                mix(1, K, TOK)
                mix(4, MIX, TOK)
                raw(square[:, 0, :], SEG2)
                mix(5, K, LAT)
                raw(square[:, 1, :], SEG2)
                mix(2, MIX, TOK)
                raw(rstd[:, :], SEG1)
                copies(K, range(8), SEG2)
                mix(3, MIX, TOK)
                dve.wait_ge(sem("mix"), n["mix"])
                mix(0, XX, LAT)
                dve.wait_ge(sem("x_saved"), 16)
                for lo in (C, 0):
                    for c in range(CHUNKS):
                        dve.tensor_copy(V[lo:lo + C, c, :, :].rearrange("p a b -> p (a b)"), tile()[lo:lo + C, :]).then_inc(sem("tile_free"), one("tile_free"))
                dve.wait_ge(sem("mix"), n["mix"])
                copies(R, range(8), SEG1)
                dve.wait_ge(sem("tile_free"), n["tile_free"])
                settle(dve.memset(reset[:, :], 1.0))
                settle(dve.memset(chunked(reset[:, :])[:, :, 0:1], 0.0))

            def half(h):
                return slice(C * h, C * h + C)

            def each_chunk(m, count):
                return m.unsqueeze(1).broadcast_to([m.shape[0], count, m.shape[1]])

            def features(j, i):
                p, d = divmod(j, 2)
                inv, b, kd = chunked(f_inv), chunked(f_a), chunked(f_kd)
                for at_slot, what in FEATURE_SLOTS:
                    if at_slot != i:
                        continue
                    if what == "norm" and d == 0:
                        dve.tensor_scalar(f_kk, K[:, p, :], vcol("kk", p), None, ALU.mult).then_inc(
                            sem("feature_dve"), one("feature_dve"))
                        dve.wait_ge(sem("feature_read"), more("feature_read", 2))
                        dve.tensor_scalar(rstd[:, :], rstd[:, :], 1e-24, None, ALU.max).then_inc(
                            sem("feature_dve"), one("feature_dve"))
                        dve.wait_ge(sem("key_root"), more("key_root"))
                        settle(dve.reciprocal(rstd[:, :], rstd[:, :]))
                        settle(dve.tensor_tensor(f_kk, f_kk, rstd[:, :], ALU.mult))
                    elif what == "decay":
                        dve.wait_ge(sem("feature_read"), more("feature_read", 2))
                        line = f_cs if d == 0 else f_cs[:, ::-1]
                        dve.tensor_tensor_scan(line, reset[:, :], line, 0.0, ALU.mult, ALU.add).then_inc(
                            sem("running"), one("running"))
                    elif what == "rate":
                        dve.wait_ge(sem("feature_read"), more("feature_read", 2))
                        settle(dve.tensor_scalar(f_kd, f_a, vcol("ka", p), omka[:, p:p + 1], ALU.mult, ALU.add))
                        settle(dve.tensor_tensor(f_kd, f_kd, K[:, p, :], ALU.mult))
                        if d == 0:
                            settle(dve.tensor_copy(k_sum, f_kd[:, 0:LAT]))
                        else:
                            settle(dve.tensor_tensor(k_sum, k_sum, f_kd[:, 0:LAT], ALU.add))
                        settle(dve.tensor_tensor(f_a, f_kk, f_a, ALU.mult))
                if i == KEY_SLOT:
                    dve.wait_ge(sem("exponents"), more("exponents", 2))
                    for h in range(2):
                        dve.tensor_tensor(bk[half(h), :, h, :], b[half(h)], inv[half(h)], ALU.mult)
                elif i == KEY_SLOT + 1:
                    for h in range(2):
                        ins = dve.tensor_tensor(bk[half(h), :, 1 - h, :], kd[half(h)], inv[half(h)], ALU.mult)
                    ins.then_inc(sem("keys"), one("keys"))
                    dve.wait_ge(sem("keys"), n["keys"])

            def prepare(j, i):
                p, d = divmod(j, 2)
                S = sets[d]
                lat = LAT // C
                inc, kk = chunked(f_inc), chunked(f_kk)
                lower = "level" if d == 0 else "level_t"
                if i == 0:
                    to, of = (slice(1, C), slice(0, C - 1)) if d == 0 else (slice(0, C - 1), slice(1, C))
                    e = slice(0, 1) if d == 0 else slice(C - 1, C)
                    last = slice(C - 1, C) if d == 0 else slice(0, 1)
                    dve.tensor_tensor(S["kr"][:, :, 0, to], kk[:, :, to], inc[:, :, of], ALU.mult)
                    dve.tensor_copy(S["kr"][:, :, 0, e], kk[:, :, e])
                    dve.tensor_tensor(S["kr"][:, 0:lat, 1, :], chunked(R[:, p, :]), inc[:, 0:lat, :], ALU.mult)
                    dve.tensor_copy(chunk_decay[:, d, :].unsqueeze(2), inc[:, :, last]).then_inc(
                        sem("decayed"), one("decayed"))
                    dve.wait_ge(sem("decayed"), n["decayed"])
                    if d == 1:
                        settle(dve.scalar_tensor_tensor(R[:, p, :], k_sum, vcol("rk", p), R[:, p, :], ALU.mult, ALU.mult))
                elif 1 <= i <= GRAMS:
                    g = i - 1
                    c = 2 * g
                    dve.wait_ge(sem("gram"), more("gram"))
                    for h in range(2):
                        raw = ps[:, 2 * (g % 2) + h, 0:4 * C].rearrange("p (a b) -> p a b", a=2)
                        if c < lat:
                            dve.tensor_tensor(S["gram"][:, c:c + 2, h, :], raw[:, :, C:2 * C],
                                              each_chunk(ccol("gram_mask", 2 * C * d + C, C), 2), ALU.mult)
                        ins = dve.tensor_tensor(couple[:, h, c:c + 2, :], raw[:, :, 0:C],
                                                each_chunk(ccol("gram_mask", 2 * C * d, C), 2), ALU.mult)
                    ins.then_inc(sem("gram_read"), one("gram_read"))
                elif i == INVERSE:
                    dve.wait_ge(sem("gram_copied"), more("gram_copied", GRAMS))
                    settle(dve.scalar_tensor_tensor(f_x, f_x, -1.0, each_chunk(ccol(lower, 0, C), CHUNKS), ALU.mult, ALU.mult))
                    dve.tensor_tensor(f_x, f_x, each_chunk(ccol("ident2", 0, C), CHUNKS), ALU.add).then_inc(
                        sem("inverse"), one("inverse"))
                    dve.wait_ge(sem("masked"), LEVELS * j + 1)
                    dve.tensor_tensor(S["xt"], each_chunk(ccol("ident2", 0, C), CHUNKS), f_am, ALU.subtract).then_inc(
                        sem("started"), one("started"))
                    dve.wait_ge(sem("started"), n["started"])
                    dve.sem_inc(sem("inverse"), one("inverse"))
                elif INVERSE < i <= INVERSE + 3 * (LEVELS - 1):
                    level, q = divmod(i - INVERSE - 1, 3)
                    for b in range(2):
                        chunks = slice(b * HALF, (b + 1) * HALF)
                        if q == 1 and level < LEVELS - 2:
                            dve.wait_ge(sem("second_product"), more("second_product"))
                            settle(dve.tensor_tensor(f_x[:, chunks, :], f_x[:, chunks, :], chunked(ps[:, 2 + b, 0:HALF * C]),
                                                     ALU.subtract))
                        elif q == 2:
                            dve.wait_ge(sem("third_product"), more("third_product"))
                            dve.tensor_tensor(S["xt"][:, chunks, :], S["xt"][:, chunks, :], chunked(ps[:, b, 0:HALF * C]),
                                              ALU.subtract).then_inc(sem("inverse"), one("inverse"))
                            dve.wait_ge(sem("inverse"), n["inverse"])

            def state_in(j, s):
                d = j % 2
                S, c = sets[d], chunk_order(d)[s]
                if s == 0:
                    dve.memset(state[:, d, :], 0.0).then_inc(sem("state"), one("state"))
                dve.wait_ge(sem("state"), n["state"])
                dve.tensor_scalar(state_dec[:, d, :], state[:, d, :], chunk_decay[:, d, c:c + 1], None, ALU.mult)
                dve.wait_ge(sem("from_state"), more("from_state"))
                dve.scalar_tensor_tensor(w0_neg[:, d, :], ps[:, 6, 0:C], -1.0, S["bv"][:, c, :], ALU.mult,
                                             ALU.add).then_inc(sem("residual"), one("residual"))

            def state_out(j, s):
                d = j % 2
                S, c = sets[d], chunk_order(d)[s]
                if s < CHUNKS - 1:
                    dve.wait_ge(sem("to_state"), more("to_state"))
                    dve.wait_ge(sem("residual"), n["residual"])
                    dve.scalar_tensor_tensor(state[:, d, :], ps[:, 6, 2 * C:3 * C], chunk_decay[:, d, c:c + 1],
                                                 state_dec[:, d, :], ALU.mult, ALU.add).then_inc(sem("state"), one("state"))
                if c < LAT // C:
                    dve.wait_ge(sem("y"), more("y"))
                    y, raw = y_pair[:, c * C:(c + 1) * C], ps[:, 7, 0:C]
                    if d == 0:
                        dve.tensor_copy(y, raw).then_inc(sem("y_read"), one("y_read"))
                    else:
                        dve.wait_ge(sem("y_read"), n["y_read"])
                        dve.tensor_tensor(y, y, raw, ALU.add).then_inc(sem("y_read"), one("y_read"))

            def readout(p):
                dve.wait_ge(sem("y_read"), n["y_read"])
                dve.tensor_copy(stat[:, 15:16], y_pair[:, 0:1]).then_inc(sem("read_dve"), one("read_dve"))
                dve.wait_ge(sem("read_pe"), more("read_pe"))
                dve.scalar_tensor_tensor(y_pair, ps[:, 0, :], -1.0 / C, y_pair, ALU.mult, ALU.add).then_inc(sem("read_dve"), one("read_dve"))
                dve.wait_ge(sem("read_pe"), more("read_pe", 2))
                dve.tensor_scalar(rstd[:, 0:LAT], ps[:, 4, :], 1.0 / C, 64e-5, ALU.mult, ALU.add).then_inc(sem("read_dve"), one("read_dve"))
                dve.wait_ge(sem("read_act_v"), more("read_act_v"))
                settle(dve.tensor_tensor(v_turned, v_turned, ps[:, 1, :], ALU.mult))
                dve.wait_ge(sem("read_act_root"), more("read_act_root"))
                settle(dve.reciprocal(rstd[:, 0:LAT], rstd[:, 0:LAT]))
                settle(dve.scalar_tensor_tensor(y_pair, y_pair, vcol("lng", p), rstd[:, 0:LAT], ALU.mult, ALU.mult))
                settle(dve.scalar_tensor_tensor(y_pair, y_pair, vcol("lnb", p), v_turned, ALU.add, ALU.add))
                dve.tensor_tensor(R[:, p, :], y_pair, ps[:, 3, :], ALU.mult).then_inc(sem("r_out"), one("r_out"))

            def tables():
                dve.wait_ge(sem("pos"), 32)
                ang, turns = rope_tmp[:, 0, :], rope_tmp[:, 1, :]
                two_pi = 2 * np.pi
                first = 6.28125
                second = float(np.float32(np.round((two_pi - first) * 2 ** 19) / 2 ** 19))
                third = two_pi - first - second
                magic = 1.5 * 2 ** 23
                settle(dve.tensor_copy(ang, pos_i.bitcast(I32)))
                settle(dve.tensor_scalar(ang, ang, ccol("inv_freq"), None, ALU.mult))
                settle(dve.tensor_scalar(turns, ang, 1.0 / two_pi, magic, ALU.mult, ALU.add))
                settle(dve.tensor_scalar(turns, turns, magic, None, ALU.subtract))
                for part in (first, second, third):
                    settle(dve.scalar_tensor_tensor(ang, turns, -part, ang, ALU.mult, ALU.add))
                dve.tensor_scalar(ang, ang, 3.1415925, -3.1415925, ALU.min, ALU.max).then_inc(sem("angle"), one("angle"))
                dve.wait_ge(sem("sine"), more("sine", 2))
                cos = rope[:, 0, :]
                settle(dve.tensor_tensor(cos, cos, cos, ALU.mult))
                settle(dve.tensor_scalar(cos, cos, -2.0, 1.0, ALU.mult, ALU.add))

            def mix_in(l):
                settle(dve.memset(conv_in[:, :, 0:TAPS - 1], 0.0))
                for c in range(2):
                    dve.tensor_copy(mk2[:, c, :], tile()[:, 0:CTX]).then_inc(sem("tile_free"), one("tile_free"))
                for t in range(2):
                    dve.tensor_copy(mv2[:, t, :], tile()[:, 0:CTX]).then_inc(sem("tile_free"), one("tile_free"))
                for c in range(3):
                    a = conv_in[:, c, TAPS - 1:]
                    dve.tensor_copy(a, tile()).then_inc(sem("tile_free"), one("tile_free"))
                    gate = tile()
                    dve.wait_ge(sem("sigmoid"), more("sigmoid"))
                    dve.wait_ge(sem("tile_free"), n["tile_free"])
                    dve.tensor_tensor(a, a, sig[:, n["sig"] % 2, :], ALU.mult).then_inc(sem("tile_free"), one("tile_free"))
                    n["sig"] += 1
                for c in range(6):
                    dve.tensor_copy(q2[:, c, :], tile()).then_inc(sem("tile_free"), one("tile_free"))
                for t in range(LAT // P):
                    dve.tensor_copy(v2[:, t, :], tile()[:, 0:P]).then_inc(sem("tile_free"), one("tile_free"))
                gains = ["swa_q_norm"] * 3 + ["swa_k_norm"] + ["mem_q_norm"] * 2 + ["mem_k_norm"] * 2
                for i in range(8):
                    hi = LAT if i < 6 else CTX
                    t = q2[:, i, :] if i < 6 else mk2[:, i - 6, :]
                    r = inverse_root(1, 0, hi, 1.0 / C, 1e-6)
                    ins = dve.scalar_tensor_tensor(t, t, vcol(f"{gains[i]}{l}"), r, ALU.mult, ALU.mult)
                    if i >= 4:
                        settle(ins)
                        continue
                    ins.then_inc(sem("normed"), one("normed"))
                    dve.wait_ge(sem("normed"), n["normed"])
                    dve.wait_ge(sem("rotated"), more("rotated"))
                    dve.tensor_tensor(rope_tmp[:, 0, :], ps[:, 5, :], rope[:, 1, :], ALU.mult)
                    settle(dve.tensor_tensor(t, t, rope[:, 0, :], ALU.mult))
                    settle(dve.tensor_tensor(t, t, rope_tmp[:, 0, :], ALU.add))
                dve.tensor_copy(stat[:, 15:16], q2[:, 0, 0:1]).then_inc(sem("roped"), one("roped"))

            def conv(l):
                dve.wait_ge(sem("tap"), n["tap"])
                dve.tensor_copy(stat[:, 15:16], conv_y[:, 0, 0:1]).then_inc(sem("tapped"), one("tapped"))
                dve.wait_ge(sem("summed"), more("summed", 3))
                for c in range(3):
                    dve.scalar_tensor_tensor(conv_y[:, c, :], ps[:, 4, :], -1.0 / 384, conv_y[:, c, :], ALU.mult, ALU.add).then_inc(sem("centred"), one("centred"))
                dve.wait_ge(sem("centred"), n["centred"])
                dve.tensor_copy(stat[:, 14:15], conv_y[:, 0, 0:1]).then_inc(sem("var"), one("var"))
                r = inverse_root(3, 0, LAT, 1.0 / 384, 1e-6)
                for c in range(3):
                    settle(dve.scalar_tensor_tensor(conv_y[:, c, :], conv_y[:, c, :], vcol(f"conv_ln_g{l}", c), r, ALU.mult,
                                                    ALU.mult))
                for c in range(3):
                    dve.tensor_scalar(conv_y[:, c, :], conv_y[:, c, :], vcol(f"conv_ln_b{l}", c), None, ALU.add).then_inc(sem("conv_z"), one("conv_z"))
                for c in range(3):
                    dve.wait_ge(sem("conv_sigmoid"), more("conv_sigmoid"))
                    s = sig[:, c, :] if c < 2 else rstd[:, 0:LAT]
                    ins = dve.tensor_tensor(Y[:, c, 0:LAT], conv_y[:, c, :], s, ALU.mult)
                ins.then_inc(sem("convolved"), one("convolved"))

            skip = lambda *a: None
            model(dict(load=load, mod=mod, gains=gains, norm_mod=norm_mod, even_in=even_in, attention=attention,
                       project=project, post=post, mlp=mlp, odd_in=odd_in, features=features, prepare=prepare, state_in=state_in, solve=skip,
                       state_out=state_out, readout=readout, odd_out=skip, tables=tables, norm_vec=norm_vec,
                       swiglu=swiglu, half_step=half_step, mix_in=mix_in, conv=conv, store=skip))


def kernel(**inputs):
    import numpy as _np
    import concourse.bacc as _bacc
    from concourse import mybir as _mybir
    from concourse.bass_utils import run_bass_kernel_spmd as _run

    a = {k: _np.asarray(v) for k, v in inputs.items()}

    def features(x):
        return x.reshape(-1, KD, P).transpose(2, 1, 0)

    arrays = dict(
        panels=pack_panels(a), vecs=pack_vectors(a), consts=pack_constants(),
        x_in=features(_np.concatenate([a["x"][0], a["ctx"][0]], 0)),
        c_in=features(_np.stack([a["c"][0], a["c_ctx"]], 0)),
        mem_in=features(a["mem_2"][0]),
        pool_w=a["ev_pool_w"][0].transpose(1, 0, 2),
        bias=pack_bias(a["ev_rpb"][0]),
        pos=_np.repeat(a["positions_2"].astype(_np.int32).reshape(1, LAT), P, 0),
        window=pack_window(),
    )
    arrays = {f"in_{k}": _np.ascontiguousarray(v) for k, v in arrays.items()}
    nc = _bacc.Bacc("TRN2", target_bir_lowering=False, num_devices=1)
    args = [nc.dram_tensor(k, v.shape, _mybir.dt.from_np(v.dtype), kind="ExternalInput").ap() for k, v in arrays.items()]
    out = nc.dram_tensor("out_x", (P, KD, LAT), F32, kind="ExternalOutput").ap()
    x_save = nc.dram_tensor("x_save", (P, KD, LAT), F32, kind="Internal").ap()
    build_program(nc, *args, out, x_save)
    r = _run(nc, [arrays], core_ids=[0])
    return _np.ascontiguousarray(r.results[0]["out_x"].transpose(2, 1, 0)).reshape(1, LAT, D)
```

```python
from collections import defaultdict
from contextlib import ExitStack

import numpy as np

import concourse.bass as bass
from concourse import mybir

P = 128
D = 1024
KD = D // P
LAT = 512
CTX = 256
TOK = LAT + CTX
FF1 = 4096
FF2 = 2816
COLS = 512
RING = 4
C = 64
CHUNKS = TOK // C
CTX_CHUNKS = CTX // C
PAIRS = KD
NEG = -1e30
UNIT = KD * TOK
PANEL = KD * COLS
POOL_WINDOWS = (2, 4, 8, 16)
TAPS = 31
Q_ORDER = (0, 3, 1, 4, 2, 5)
LEVELS = 6

F32 = mybir.dt.float32
I32 = mybir.dt.int32
ALU = mybir.AluOpType
ACT = mybir.ActivationFunctionType
AX = mybir.AxisListType



def mlp_steps(groups):
    steps = [("up", 0)]
    for g in range(groups):
        if g + 1 < groups:
            steps.append(("up", g + 1))
        steps.append(("down", g))
    return steps


MOD_STEPS = range(1, 7)
FF1_GROUPS = [8] * (FF1 // D)
FF2_GROUPS = [8, 8, 6]


def pack_panels(a):
    panels = []

    def add(w):
        rows, cols = w.shape
        full = np.zeros((KD * P, COLS), np.float32)
        full[:rows, :cols] = w
        panels.append(full.reshape(KD, P, COLS).transpose(1, 0, 2))

    def add_cols(w, lo=0, hi=None):
        for c in range(lo, w.shape[1] if hi is None else hi, COLS):
            add(w[:, c:c + COLS])

    def add_mlp(w1, w2, beside=None):
        for step, (kind, g) in enumerate(mlp_steps(len(FF1_GROUPS))):
            if beside is not None and step in MOD_STEPS:
                lo = 2 * (step - MOD_STEPS[0])
                add_cols(beside, lo * COLS, (lo + 2) * COLS)
            if kind == "up":
                add_cols(w1, g * D, (g + 1) * D)
            else:
                add_cols(w2[g * D:(g + 1) * D])

    def add_swiglu(w1, w3, w2):
        for kind, g in mlp_steps(len(FF2_GROUPS)):
            if kind == "up":
                for j in range(FF2_GROUPS[g] // 2):
                    c = g * D + 2 * j * P
                    add(np.concatenate([w1[:, c:c + P], w3[:, c:c + P], w1[:, c + P:c + 2 * P], w3[:, c + P:c + 2 * P]], 1))
            else:
                add_cols(w2[g * D:g * D + FF2_GROUPS[g] * P])

    add_cols(a["ada_w"][0], 0, 2 * D)
    for j in range(4):
        add_cols(a["ev_w_in"][0], j * COLS, (j + 1) * COLS)
        add_cols(a["ada_w"][0], 2 * D + 2 * j * COLS, 2 * D + 2 * (j + 1) * COLS)
    add_cols(a["ev_w_out"][0])
    add_mlp(a["mlp_w1"][0], a["mlp_w2"][0], a["ada_w"][1])
    add(np.concatenate([a["rw_w1"][0, 0], a["rw_w1"][0, 1], a["rw_a1"][0, 0], a["rw_a1"][0, 1], a["rw_g1"][0]], 1))
    add_cols(a["rw_wk"][0])
    heads = a["rw_wv"][0].reshape(D, PAIRS, 2, C)
    add(heads[:, :, 0].reshape(D, COLS))
    add(heads[:, :, 1].reshape(D, COLS))
    second = np.concatenate([a["rw_w2"][0].reshape(P, D), a["rw_a2"][0].reshape(P, D), a["rw_g2"][0]], 1)
    panels.append(np.concatenate([second, np.zeros((P, PANEL - 3 * D), np.float32)], 1).reshape(P, KD, COLS))
    add_cols(a["rw_wr"][0])
    add_cols(a["rw_wo"][0])
    add_mlp(a["mlp_w1"][1], a["mlp_w2"][1])
    for l in range(2):
        add_swiglu(a["ffn1_w1_2"][l], a["ffn1_w3_2"][l], a["ffn1_w2_2"][l])
        add(a["w_mem_kv_2"][l])
        w = a["w_in_2"][l]
        conv, gate = w[:, 0:384].reshape(D, 3, P), w[:, 384:768].reshape(D, 3, P)
        q = w[:, 768:1152].reshape(D, 6, C)[:, Q_ORDER, :].reshape(D, 3, P)
        add(np.concatenate([q[:, 0], q[:, 1], q[:, 2], w[:, 1152:1280]], 1))
        add(np.concatenate([w[:, 1408:1664], conv[:, 0], gate[:, 0]], 1))
        add(np.concatenate([conv[:, 1], gate[:, 1], conv[:, 2], gate[:, 2]], 1))
        add(w[:, 1280:1408])
        wo = a["w_out_2"][l]
        wo = np.concatenate([wo[0:384], wo[384:768].reshape(6, C, D)[Q_ORDER, :, :].reshape(384, D), wo[768:]], 0)
        add_cols(wo)
        add_swiglu(a["ffn2_w1_2"][l], a["ffn2_w3_2"][l], a["ffn2_w2_2"][l])
    return np.ascontiguousarray(np.stack(panels).reshape(len(panels), P, PANEL))


VEC_AT = {}


def vector_parts():
    for i in range(2):
        for j in range(4):
            yield f"norm_g{i}{j}", KD
        yield f"ada_b{i}", 6 * KD
    yield "pool_scale", 4
    for j in range(6):
        yield f"mu{j}", KD
    for d in range(2):
        yield f"w0{d}", KD
        yield f"a0{d}", KD
    for name in ("kk", "ka", "rk", "lng", "lnb"):
        yield name, KD
    for l in range(2):
        for name in ("ffn1_norm", "mix_norm", "mem_norm", "ffn2_norm", "final_norm"):
            yield f"{name}{l}", KD
        for name in ("conv_b", "conv_ln_g", "conv_ln_b"):
            yield f"{name}{l}", 3
        yield f"conv_w{l}", 3 * TAPS
        for name in ("swa_q_norm", "swa_k_norm", "mem_q_norm", "mem_k_norm"):
            yield f"{name}{l}", 1
        yield f"sinks{l}", 6


NVEC = 0
for _name, _cols in vector_parts():
    VEC_AT[_name] = NVEC
    NVEC += _cols


def pack_vectors(a):
    v = np.zeros((P, NVEC), np.float32)

    def put(name, x):
        x = np.asarray(x).reshape(-1, P).T
        v[:, VEC_AT[name]:VEC_AT[name] + x.shape[1]] = x

    for i in range(2):
        for j in range(4):
            put(f"norm_g{i}{j}", a["norm_g"][i, j])
        put(f"ada_b{i}", a["ada_b"][i])
    put("pool_scale", a["ev_pool_scale"][0])
    for j in range(6):
        put(f"mu{j}", a["rw_mu"][0, j])
    for d in range(2):
        put(f"w0{d}", a["rw_w0"][0, d])
        put(f"a0{d}", a["rw_a0"][0, d])
    for name in ("kk", "ka", "rk", "lng", "lnb"):
        put(name, a[f"rw_{name}"][0])
    for l in range(2):
        for name in ("ffn1_norm", "mix_norm", "mem_norm", "ffn2_norm", "final_norm", "conv_b", "conv_ln_g", "conv_ln_b"):
            put(f"{name}{l}", a[f"{name}_2"][l])
        put(f"conv_w{l}", a["conv_w_2"][l].reshape(TAPS, 3, P).transpose(1, 0, 2))
        for name in ("swa_q_norm", "swa_k_norm", "mem_q_norm", "mem_k_norm"):
            put(f"{name}{l}", np.concatenate([a[f"{name}_2"][l]] * 2))
        put(f"sinks{l}", np.repeat(np.asarray(a["swa_sinks_2"][l])[:, None], P, 1))
    return v


CONST_PARTS = (("ident", P), ("head_ones", P), ("rotate", P), ("gram_mask", 2 * 2 * C),
               ("level", LEVELS * C), ("level_t", LEVELS * C), ("ident2", C), ("pool_edge", 2 * 15), ("inv_freq", 1))
CONST_AT = {}
NCONST = 0
for _name, _cols in CONST_PARTS:
    CONST_AT[_name] = NCONST
    NCONST += _cols


def pack_constants():
    v = np.zeros((P, NCONST), np.float32)

    def put(name, x):
        x = np.asarray(x, np.float32).reshape(x.shape[0], -1)
        v[:, CONST_AT[name]:CONST_AT[name] + x.shape[1]] = x

    p = np.arange(P)
    put("ident", np.eye(P))
    put("head_ones", p[:, None] // C == p[None, :] // C)
    same = p[:, None] // C == p[None, :] // C
    half = C // 2
    first = p[None, :] % C < half
    put("rotate", np.where(same & first & (p[:, None] == p[None, :] + half), -1.0, 0.0)
        + np.where(same & ~first & (p[:, None] == p[None, :] - half), 1.0, 0.0))
    s, t = (p % C)[:, None], np.arange(C)[None, :]
    put("gram_mask", np.concatenate([s < t, s <= t, s > t, s >= t], 1))
    levels = []
    for j in range(LEVELS):
        m = 1 << j
        levels.append((s // m % 2 == 1) & (t // m == s // m - 1))
    put("level", np.concatenate(levels, 1))
    put("level_t", np.concatenate([(t // (1 << j) % 2 == 1) & (s // (1 << j) == t // (1 << j) - 1) for j in range(LEVELS)], 1))
    put("ident2", s == t)
    edge = []
    for w in POOL_WINDOWS:
        edge.append([w / (i + w // 2) for i in range(w // 2)] + [w / (w - i) for i in range(w // 2)])
    put("pool_edge", np.repeat(np.concatenate(edge)[None, :], P, 0))
    put("inv_freq", (10000.0 ** (-(2 * (p % half)).astype(np.float32) / C)).astype(np.float32)[:, None])
    return v


def pack_window():
    rel = (np.arange(P)[:, None] + P) - np.arange(2 * P)[None, :]
    return np.where((rel >= 0) & (rel < P), np.float32(0.0), np.float32(NEG)).astype(np.float32)


def pack_bias(rpb):
    heads = rpb.shape[0]
    col = np.arange(64)
    start = np.clip(col - 8, 0, 48)
    ok = (col[None, :] >= start[:, None]) & (col[None, :] < start[:, None] + 16)
    dc = np.clip(col[None, :] - col[:, None], -15, 15) + 15
    t = np.where(ok[None, None], rpb[:, :, dc], np.float32(NEG)).transpose(0, 2, 1, 3)
    out = np.full((heads, 2, 64, 16, 64), np.float32(NEG), np.float32)
    out[:, 0, :, 0:15] = t
    out[:, 1, :, 1:16] = t
    return out.reshape(heads, P, 16 * 64)



def build_program(nc, panels, vecs, consts, x_in, c_in, mem_in, pool_w, bias, pos, window_in, out, x_save):
    npanels = panels.shape[0]
    with ExitStack() as ctx:
        def sb(name, shape, dt=F32):
            return ctx.enter_context(nc.sbuf_tensor(name, shape, dt))

        sems = {}

        def sem(name):
            if name not in sems:
                sems[name] = ctx.enter_context(nc.semaphore(name))
            return sems[name]

        arena = sb("arena", [P, 5 * UNIT + RING * PANEL])
        vec = sb("vec", [P, NVEC])
        const = sb("const", [P, NCONST])
        ones = sb("ones", [P, P])
        square = sb("square", [P, 2, TOK])
        rstd = sb("rstd", [P, TOK])
        mod_sb = sb("mod", [P, 2, 2, 6 * KD])
        gain = sb("gain", [P, 2, 4, 2, KD])
        silu_c = sb("silu_c", [P, KD, 2])
        raw_c = sb("raw_c", [P, KD, 2])
        stat = sb("stat", [P, 16])
        reset = sb("reset", [P, TOK])
        ps = ctx.enter_context(nc.psum_tensor("ps", [P, 8, 512], F32))

        def area(at, *shape):
            n = int(np.prod(shape))
            flat = arena[:, at:at + n]
            if len(shape) == 1:
                return flat
            names = " ".join("abcd"[:len(shape)])
            return flat.rearrange(f"p ({names}) -> p {names}", **{"abcd"[i]: s for i, s in enumerate(shape)})

        X0, H0, Y0, W0 = 0, UNIT, 2 * UNIT, 3 * UNIT
        RING0 = 5 * UNIT
        X, H, Y = (area(o, KD, TOK) for o in (X0, H0, Y0))
        ring = [area(RING0 + s * PANEL, KD, COLS) for s in range(RING)]
        hidden1 = [area(W0 + s * UNIT, KD, TOK) for s in range(2)]
        hidden2 = [area(W0 + s * KD * LAT, KD, LAT) for s in range(2)]
        Z = area(W0, KD, TOK)
        qT = area(W0, 4, TOK)
        kT = area(W0 + 4 * TOK, 4, TOK)
        vN = area(W0 + 8 * TOK, TOK // P, 512)
        pool_buf = [area(W0 + 12 * TOK + i * 792, 792) for i in range(3)]
        pool_wb = area(W0 + 12 * TOK + 3 * 792, 4, P)
        probs = area(H0, 3, TOK)
        probsT = area(H0 + 3 * TOK, 2, TOK)
        bias_sb = area(H0 + 5 * TOK, 2, 1024)
        B0 = W0
        q2 = area(B0, 6, LAT)
        mk2 = area(B0 + 6 * LAT, 2, CTX)
        v2 = area(B0 + 7 * LAT, 4, P)
        mv2 = area(B0 + 8 * LAT, 2, 256)
        conv_in = area(B0 + 9 * LAT, 3, TAPS - 1 + LAT)
        conv_y = area(B0 + 9 * LAT + 3 * (TAPS - 1 + LAT), 3, LAT)
        rope = area(W0 + 2 * KD * LAT, 2, LAT)
        rope_tmp = area(W0 + 2 * KD * LAT + 2 * LAT, 2, LAT)
        pos_i = area(W0 + 2 * KD * LAT + 4 * LAT, LAT)
        window = area(W0 + 2 * KD * LAT + 5 * LAT, 2 * P)
        tap_product = {c: area(W0 + 2 * KD * LAT + 5 * LAT + 2 * P + i * LAT, LAT) for i, c in enumerate((1, 2))}
        sig = square[:, :, 0:LAT]

        def vcol(name, c=0, n=1):
            return vec[:, VEC_AT[name] + c:VEC_AT[name] + c + n]

        def ccol(name, c=0, n=1):
            return const[:, CONST_AT[name] + c:CONST_AT[name] + c + n]

        ident = ccol("ident", 0, P)
        head_ones = ccol("head_ones", 0, P)
        rotate = ccol("rotate", 0, P)

        SEG2 = ((0, 384), (384, TOK))
        SEG1 = ((0, LAT),)
        SEGM = ((LAT, TOK),)

        def norm_banks(lo, hi):
            return [(a, b, bank) for a, b, bank in ((lo, min(hi, LAT), 4), (max(lo, LAT), hi, 5)) if b > a]

        def norm_psum(lo, hi):
            flat = ps[:, 4:6, :].rearrange("p a b -> p (a b)")
            return flat[:, lo:hi]

        def even_units():
            units = []
            for h in range(8):
                base, ch = C * (h % 2), h // 2
                for qt in range(TOK // P):
                    lat = qt < LAT // P
                    lo = 0 if lat else LAT
                    units.append(dict(
                        q=qT[base:base + C, ch, qt * P:(qt + 1) * P],
                        keys=[kT[base:base + C, ch, a:b] for a, b in ([(0, LAT)] if lat else []) + [(LAT, TOK)]],
                        bias=bias_sb[:, h % 2, (7 - 2 * qt) * 64:(7 - 2 * qt) * 64 + LAT] if lat else None,
                        bias_head=h, width=TOK - lo, sink=None,
                        values=[vN[:, t, h * C:(h + 1) * C] for t in range(lo // P, TOK // P)],
                        base=base, dest=Y[base:base + C, 4 + ch, qt * P:(qt + 1) * P]))
            return units

        def conformer_units(l):
            units = []
            for i in range(6):
                base, ch = C * (i % 2), i // 2
                for qb in range(LAT // P):
                    lo = max(0, qb - 1)
                    n = (qb + 1 - lo) * P
                    units.append(dict(
                        q=q2[base:base + C, ch, qb * P:(qb + 1) * P],
                        keys=[q2[base:base + C, 3, lo * P:(qb + 1) * P]],
                        bias=window[:, 2 * P - n:2 * P], bias_head=None, width=n,
                        sink=vcol(f"sinks{l}", Q_ORDER[i]),
                        values=[v2[:, t, (i % 2) * C:(i % 2 + 1) * C] for t in range(lo, qb + 1)],
                        base=base, dest=Y[base:base + C, 3 + ch, qb * P:(qb + 1) * P]))
            for h in range(4):
                base, ch = C * (h % 2), h // 2
                for qb in range(LAT // P):
                    units.append(dict(
                        q=q2[base:base + C, 4 + ch, qb * P:(qb + 1) * P],
                        keys=[mk2[base:base + C, ch, :]], bias=None, bias_head=None, width=CTX, sink=None,
                        values=[mv2[:, t, h * C:(h + 1) * C] for t in range(2)],
                        base=base, dest=Y[base:base + C, 6 + ch, qb * P:(qb + 1) * P]))
            return units

        DVE_CHANNELS, POOL_CHANNELS = (0,), (1, 2)

        MIX_TILES = 6 + LAT // P

        def scores_ps(u, width):
            return ps[:, 2 * (u % 2):2 * (u % 2) + 2, :].rearrange("p a b -> p (a b)")[:, 0:width]

        def turned_ps(width):
            return ps[:, 4:6, :].rearrange("p a b -> p (a b)")[:, 0:width]

        XX, MIX = Y, area(W0, KD, TOK)
        K = area(W0 + UNIT, KD, TOK)
        V = area(X0, CHUNKS, PAIRS, C)
        R = area(H0, KD, LAT)
        decay_in, a_in = area(H0 + KD * LAT, TOK), area(H0 + KD * LAT + TOK, TOK)
        gate_in = area(H0 + KD * LAT + 2 * TOK, LAT)
        LORA_SLOT = 3
        lora2 = area(RING0 + LORA_SLOT * PANEL, 3, D)
        k_sum = area(RING0 + LORA_SLOT * PANEL + 3 * D, LAT)
        y_pair = area(RING0 + LORA_SLOT * PANEL + 3 * D + LAT, LAT)
        state = sb("state", [P, 2, C])
        omka = sb("omka", [P, KD])
        w0_neg = sb("w0_neg", [P, 2, C])
        state_dec = sb("state_dec", [P, 2, C])
        chunk_decay = sb("chunk_decay", [P, 2, CHUNKS])
        WORK = ((Y0, 2 * UNIT), (RING0, 3 * PANEL))
        BLOCK = CHUNKS * C
        SET = 8 * BLOCK + 2 * LAT
        sets = []
        for o, _ in WORK:
            sets.append(dict(
                kr=area(o, CHUNKS, 2, C), bkn=area(o + 2 * BLOCK, CHUNKS, 2 * C),
                uv=area(o + 4 * BLOCK, CHUNKS, 2, C),
                bv=area(o + 6 * BLOCK, CHUNKS, C), xt=area(o + 7 * BLOCK, CHUNKS, C),
                gram=area(o + 8 * BLOCK, LAT // C, 2, C)))
        bk = area(Y0 + SET, CHUNKS, 2, C)
        couple = area(RING0 + SET, 2, CHUNKS, C)
        spare = [area(o + SET + 2 * BLOCK + k * TOK, TOK) for o, _ in WORK for k in range(4)]
        f_kk, f_a, f_inc, f_inv, f_kd = spare[0:5]
        chunked = lambda f: f.rearrange("p (c t) -> p c t", t=C)
        f_x, f_am, f_y1 = (chunked(f) for f in spare[5:8])
        v_turned = area(RING0 + SET + 2 * BLOCK + 4 * TOK, LAT)
        assert all(SET + 2 * BLOCK + 4 * TOK + LAT <= n for _, n in WORK)
        f_cs = square[:, 1, :]
        HALF = CHUNKS // 2
        E_HALF = float(np.exp(-0.5))
        JOBS = 2 * PAIRS
        GRAMS = CHUNKS // 2
        INVERSE = GRAMS + 2
        FEATURE_SLOTS = ((9, "norm"), (12, "decay"), (15, "rate"))
        SQUARE_SLOT = 8
        ROOT_SLOT = 10
        EXPONENT_SLOT = 18
        KEY_SLOT = 21
        SLOTS = [(i, b) for i in range(INVERSE + 1 + 3 * (LEVELS - 1))
                 for b in range(2 if i == INVERSE - 1 or i > INVERSE else 1)]

        def last_level(d, h):
            first, second = C // 2 * d, C // 2 * (1 - d)
            of, to = slice(first, first + C // 2), slice(second, second + C // 2)
            return slice(C * h + of.start, C * h + of.stop), slice(C * h + to.start, C * h + to.stop), of, to

        def chunk_order(d):
            ctx_first = list(range(LAT // C, CHUNKS))
            lat = list(range(LAT // C))
            return ctx_first + lat if d == 0 else ctx_first[::-1] + lat[::-1]

        def two_banks(b, n=TOK):
            return ps[:, b:b + 2, :].rearrange("p a b -> p (a b)")[:, 0:n]

        def job_steps(e):
            for t in range(JOBS + 2):
                k = 0
                for slot, b in SLOTS:
                    if t >= 4 and t % 2 == 0 and 2 <= slot <= 6:
                        e["readout_end"]((t - 4) // 2, slot - 2)
                    if t < JOBS and b == 0:
                        e["features"](t, slot)
                    if 0 <= t - 1 < JOBS:
                        e["prepare"](t - 1, slot, b)
                    if 0 <= t - 2 and slot > 2 and k < 3 * CHUNKS:
                        e[("state_in", "solve", "state_out")[k % 3]](t - 2, k // 3)
                        k += 1
                assert t < 2 or k == 3 * CHUNKS
                if t >= 3 and t % 2 == 1:
                    e["readout"]((t - 3) // 2)

        def model(e):
            e["load"]()
            e["norm_mod"](0, 0)
            e["mod"](0, 0, 4)
            e["gains"](0, 0)
            e["even_in"]()
            e["gains"](0, 1)
            e["attention"](even_units(), None)
            e["project"](2, SEG2, Y, Z, "attn")
            e["post"](Z, 0, 1)
            e["norm_mod"](0, 2)
            e["mlp"](SEG2, True)
            e["post"](Y, 0, 3)
            e["gains"](1, 0)
            e["gains"](1, 1)
            e["norm_mod"](1, 0)
            e["odd_in"]()
            job_steps(e)
            e["odd_out"]()
            for part in range(5):
                e["readout_end"](PAIRS - 1, part)
            e["project"](2, SEG1, R, Z, "odd")
            e["post"](Z, 1, 1)
            e["norm_mod"](1, 2)
            e["mlp"](SEG1, False)
            e["post"](Y, 1, 3)
            for l in range(2):
                e["norm_vec"](0, LAT, "ffn1_norm", l, X)
                if l == 0:
                    e["tables"]()
                e["swiglu"]()
                e["half_step"]()
                e["norm_vec"](LAT, TOK, "mem_norm", l, X)
                e["norm_vec"](0, LAT, "mix_norm", l, X)
                e["mix_in"](l)
                e["attention"](conformer_units(l), l)
                e["conv"](l)
                e["project"](2, SEG1, Y, None, "attn")
                e["norm_vec"](0, LAT, "ffn2_norm", l, X)
                e["swiglu"]()
                e["half_step"]()
                e["norm_vec"](0, LAT, "final_norm", l, X)
            e["store"]()

        block = ctx.enter_context(nc.Block())

        def counting():
            n = defaultdict(int)

            def more(name, k=1):
                n[name] += k
                return n[name]

            def one(name):
                n[name] += 1
                return 1

            return n, more, one

        @block.sync
        def _(sp):
            n, more, one = counting()
            ends = []

            def load_panel(tiles, width=PANEL):
                p = len(ends)
                if p >= RING:
                    if ends[p - RING] > 0:
                        sp.wait_ge(sem("tile_done"), ends[p - RING])
                sp.dma_start(arena[:, RING0 + (p % RING) * PANEL:RING0 + (p % RING) * PANEL + width],
                             panels[p, :, 0:width]).then_inc(sem(f"panel{p % RING}"), 16)
                n["tile"] += tiles
                ends.append(n["tile"])

            def load():
                sp.dma_start(raw_c[:, :, :], c_in).then_inc(sem("small_in"), 16)
                sp.dma_start(vec[:, :], vecs).then_inc(sem("small_in"), 16)
                sp.dma_start(X, x_in).then_inc(sem("x_in"), 16)
                load_panel(1)
                sp.dma_start(const[:, :], consts).then_inc(sem("const_in"), 16)
                n["mod_skip"] = 1

            def mod(i, lo, hi):
                for j in range(lo + n["mod_skip"], hi):
                    load_panel(1)
                    if j % 2 == 1:
                        n["tile"] += 2
                n["mod_skip"] = 0

            def even_in():
                for j, tiles in enumerate((8, 8, 8, TOK // P)):
                    load_panel(tiles)
                    mod(0, 4 + 2 * j, 6 + 2 * j)
                n["tile"] += 8

            def project(count, segs, src, dest, ready):
                for _ in range(count):
                    load_panel(4 * len(segs))

            def mlp(segs, beside):
                for step, _ in enumerate(mlp_steps(len(FF1_GROUPS))):
                    if beside and step in MOD_STEPS:
                        mod(1, 2 * (step - MOD_STEPS[0]), 2 * (step - MOD_STEPS[0]) + 2)
                    for _ in range(2):
                        load_panel(4 * len(segs))

            def swiglu():
                for kind, g in mlp_steps(len(FF2_GROUPS)):
                    if kind == "up":
                        for _ in range(FF2_GROUPS[g] // 2):
                            load_panel(4)
                    else:
                        for _ in range(2):
                            load_panel(4, FF2_GROUPS[g] * COLS)

            def odd_in():
                load_panel(5)
                for _ in range(2):
                    load_panel(8)
                for _ in range(2):
                    load_panel(CHUNKS)
                load_panel(0, 3 * D)
                for _ in range(2):
                    load_panel(4)

            def odd_out():
                sp.wait_ge(sem("r_out"), PAIRS)

            def mix_in(l):
                for tiles in (4, 4, 4, 4, LAT // P):
                    load_panel(tiles)

            def store():
                sp.wait_ge(sem("x_chunk"), 10 * KD)
                sp.dma_start(out, X[:, :, 0:LAT]).then_inc(sem("stored"), 16)
                sp.wait_ge(sem("stored"), 16)

            skip = lambda *a: None
            model(dict(load=load, mod=mod, gains=skip, norm_mod=skip, even_in=even_in, attention=skip, project=project,
                       post=skip, mlp=mlp, odd_in=odd_in, features=skip, prepare=skip, state_in=skip, solve=skip, state_out=skip,
                       readout=skip, readout_end=skip, odd_out=odd_out, tables=skip, norm_vec=skip, swiglu=swiglu, half_step=skip,
                       mix_in=mix_in, conv=skip, store=store))
            assert len(ends) == npanels

        @block.gpsimd
        def _(pool):
            n, more, one = counting()

            def load():
                pool.dma_start(pool_wb, pool_w).then_inc(sem("pool_w"), 16)
                pool.memset(ones[:, :], 1.0).then_inc(sem("ones"), one("ones"))

            def conv_taps(l):
                n["tap_product"] += len(POOL_CHANNELS)
                for tap in range(1, TAPS):
                    for c in POOL_CHANNELS:
                        pool.wait_ge(sem("tap_product"), more("tap_product"))
                        if n["pool_tap"] - len(POOL_CHANNELS) + 1 > 0:
                            pool.wait_ge(sem("pool_tap"), n["pool_tap"] - len(POOL_CHANNELS) + 1)
                        pool.tensor_tensor(conv_y[:, c, :], conv_y[:, c, :], tap_product[c], ALU.add).then_inc(
                            sem("pool_tap"), one("pool_tap"))

            def attention(units, l):
                if l is not None:
                    conv_taps(l)
                heads = []
                for u, unit in enumerate(units):
                    h = unit["bias_head"]
                    if h is not None and h not in heads:
                        heads.append(h)
                        if len(heads) == 1:
                            if n["tile"] > 0:
                                pool.wait_ge(sem("tile_free"), n["tile"])
                        if len(heads) > 2:
                            if u - TOK // P > 0:
                                pool.wait_ge(sem("scored"), u - TOK // P)
                        pool.dma_start(bias_sb[:, h % 2, :], bias[h]).then_inc(sem(f"bias{h % 2}"), 16)

            def even_in():
                n["tile"] += 24 + TOK // P + 8 + 2 * 8

            def mod(i, lo, hi):
                n["tile"] += 2 * (hi - lo)

            def odd_in():
                pool.wait_ge(sem("x_chunk"), 2 * KD)
                pool.dma_start(x_save, X[:, :, 0:LAT]).then_inc(sem("x_saved"), 16)

            def half(h):
                return slice(C * h, C * h + C)

            def mask_couplings(j, level, dest, chunks):
                upper = "level_t" if j % 2 == 0 else "level"
                for h in range(2):
                    d = dest[half(h), chunks]
                    m = ccol(upper, C * level, C)[half(h), :].unsqueeze(1).broadcast_to(list(d.shape))
                    ins = pool.tensor_tensor(d, couple[half(h), h, chunks, :], m, ALU.mult)
                ins.then_inc(sem("masked"), one("masked"))

            def prepare(j, i, b):
                p, d = divmod(j, 2)
                if i == 0:
                    uv = sets[d]["uv"]
                    pool.wait_ge(sem("decayed"), more("decayed", 2) - 1)
                    for h, lo in ((0, C), (1, 0)):
                        ins = pool.tensor_copy(uv[lo:lo + C, :, h, :], V[lo:lo + C, :, p, :])
                    ins.then_inc(sem("values"), one("values"))
                elif 1 <= i <= GRAMS:
                    pool.wait_ge(sem("gram_read"), more("gram_read"))
                    pair = slice(2 * (i - 1), 2 * i)
                    mask_couplings(j, 0, sets[d]["xt"], pair)
                elif i == INVERSE:
                    if (LEVELS - 1) * j > 0:
                        pool.wait_ge(sem("first_product"), 2 * (LEVELS - 1) * j)
                    mask_couplings(j, 1, f_am, slice(0, CHUNKS))
                elif INVERSE < i <= INVERSE + 3 * (LEVELS - 3):
                    level, q = divmod(i - INVERSE - 1, 3)
                    if q == 1 and b == 0:
                        pool.wait_ge(sem("first_product"), 2 * ((LEVELS - 1) * j + level + 1))
                        mask_couplings(j, level + 2, f_am, slice(0, CHUNKS))

            def odd_out():
                pool.wait_ge(sem("r_out"), PAIRS)
                pool.dma_start(X[:, :, 0:LAT], x_save).then_inc(sem("x_back"), 16)
                pool.dma_start(X[:, :, LAT:TOK], mem_in).then_inc(sem("mem_in"), 16)

            def tables():
                pool.wait_ge(sem("x_chunk"), 4 * KD)
                pool.dma_start(pos_i.bitcast(I32), pos).then_inc(sem("pos"), 16)
                pool.dma_start(window, window_in).then_inc(sem("pos"), 16)

            skip = lambda *a: None
            model(dict(load=load, mod=mod, gains=skip, norm_mod=skip, even_in=even_in, attention=attention, project=skip,
                       post=skip, mlp=skip, odd_in=odd_in, features=skip, prepare=prepare, state_in=skip, solve=skip, state_out=skip,
                       readout=skip, readout_end=skip, odd_out=odd_out, tables=tables, norm_vec=skip, swiglu=skip, half_step=skip,
                       mix_in=skip, conv=skip, store=skip))

        @block.tensor
        def _(pe):
            n, more, one = counting()

            def panel():
                p = n["panel"]
                n["panel"] += 1
                pe.wait_ge(sem(f"panel{p % RING}"), 16 * (p // RING + 1))
                return ring[p % RING]

            def tile():
                if n["tile"] - 3 > 0:
                    pe.wait_ge(sem("tile_free"), n["tile"] - 3)
                n["tile"] += 1
                return ps[:, (n["tile"] - 1) % 4, :]

            def accumulate(dest, left, right, nk=KD, ready=None):
                for k in range(nk):
                    if ready:
                        pe.wait_ge(sem(ready), more(ready))
                    ins = pe.matmul(dest, left(k), right(k), start=(k == 0), stop=(k == nk - 1))
                ins.then_inc(sem("tile_done"), one("tile_done"))

            def columns(w, ms, src, segs, nk=KD, ready=None):
                for m in ms:
                    for a, b in segs:
                        accumulate(tile()[:, 0:b - a], lambda k: w[:, k, m * P:(m + 1) * P],
                                   lambda k: src[:, k, a:b], nk, ready)
                        ready = None

            def rows(w, lo, width, src, tok, cols, ready=None):
                for t in tok:
                    accumulate(tile()[:, 0:width], lambda k: src[:, k, t * P:(t + 1) * P],
                               lambda k: w[:, k, cols:cols + width], KD, ready)
                    ready = None

            def sums(lhs, count, lo, hi, src="square"):
                if n["norm"] > 0:
                    pe.wait_ge(sem("var"), n["norm"])
                n["norm"] += 1
                for c in range(count):
                    if src == "square":
                        pe.wait_ge(sem("square"), more("square"))
                    for a, b, bank in norm_banks(lo, hi):
                        right = square[:, n["sq"] % 2, a - lo:b - lo] if src == "square" else conv_y[:, c, :]
                        ins = pe.matmul(ps[:, bank, 0:b - a], lhs, right, start=(c == 0), stop=(c == count - 1))
                    n["sq"] += src == "square"
                    ins.then_inc(sem("summed"), one("summed"))

            def load():
                pe.wait_ge(sem("small_in"), 32)
                pe.wait_ge(sem("ones"), more("ones"))
                pe.wait_ge(sem("silu"), more("silu"))

            def mod(i, lo, hi):
                for j in range(lo, hi, 2):
                    for _ in range(2):
                        w = panel()
                        accumulate(tile()[0:2, :], lambda k: silu_c[:, k, :], lambda k: w[:, k, :])
                    done = n["tile"]
                    pe.wait_ge(sem("const_in"), 16)
                    for b in range(2):
                        pe.wait_ge(sem("tile_free"), done - 1 + b)
                        bank = tile()
                        for m in range(4):
                            ins = pe.transpose(bank[:, 2 * m:2 * m + 2], square[0:2, b, m * P:(m + 1) * P], ident[0:2, 0:2])
                        ins.then_inc(sem("tile_done"), one("tile_done"))

            def norm_mod(i, which):
                sums(ones[:, :], KD, 0, TOK if (i, which) != (1, 2) else LAT)
                n["source"] = "h_act"

            def norm_vec(lo, hi, name, l, src):
                sums(ones[:, :], KD, lo, hi)
                n["source"] = "h_dve"

            def post(src, i, which):
                sums(ones[:, :], KD, 0, TOK if i == 0 else LAT)

            def even_in():
                columns(panel(), range(4), H, ((0, LAT), (LAT, TOK)), ready="h_act")
                mod(0, 4, 6)
                columns(panel(), range(4), H, SEG2)
                mod(0, 6, 8)
                columns(panel(), range(4), H, SEG2)
                mod(0, 8, 10)
                rows(panel(), 0, 512, H, range(TOK // P), 0)
                mod(0, 10, 12)
                pe.wait_ge(sem("const_in"), 16)
                pe.wait_ge(sem("pool_w"), 16)
                for g in range(4):
                    pe.wait_ge(sem("pooled"), more("pooled"))
                    for a, b in SEG2:
                        accumulate(tile()[:, 0:b - a], lambda k: pool_wb[:, g, :], lambda k: Y[:, 4 + g, a:b], 1)

            def attention(units, l):
                if n["tile"] > 0:
                    pe.wait_ge(sem("tile_free"), n["tile"])
                if n["norm"] > 0:
                    pe.wait_ge(sem("var"), n["norm"])
                if n["unit"] > 0:
                    pe.wait_ge(sem("roped"), more("roped"))
                base = n["unit"]
                for i in range(len(units) + 3):
                    if i < len(units):
                        unit, u = units[i], base + i
                        if u - 1 > 0:
                            pe.wait_ge(sem("scored"), u - 1)
                        col = 0
                        for key in unit["keys"]:
                            w = key.shape[1]
                            ins = pe.matmul(scores_ps(u, TOK)[:, col:col + w], unit["q"], key, start=True, stop=True)
                            col += w
                        ins.then_inc(sem("scores"), one("scores"))
                    if 2 <= i <= len(units) + 1:
                        unit, u = units[i - 2], base + i - 2
                        pe.wait_ge(sem("probs"), more("probs"))
                        if u > 0:
                            pe.wait_ge(sem("turned_copy"), u)
                        for t in range(unit["width"] // P):
                            ins = pe.transpose(turned_ps(TOK)[:, t * P:(t + 1) * P], probs[:, u % 3, t * P:(t + 1) * P],
                                               ident)
                        ins.then_inc(sem("turned"), one("turned"))
                    if i >= 3:
                        unit, u = units[i - 3], base + i - 3
                        if u + 1 > 0:
                            pe.wait_ge(sem("turned_copy"), u + 1)
                        if u - 1 > 0:
                            pe.wait_ge(sem("attended"), u - 1)
                        nt = unit["width"] // P
                        for t in range(nt):
                            ins = pe.matmul(ps[unit["base"]:unit["base"] + C, 6 + u % 2, 0:P], unit["values"][t],
                                            probsT[:, u % 2, t * P:(t + 1) * P], start=(t == 0), stop=(t == nt - 1))
                        ins.then_inc(sem("output"), one("output"))
                n["unit"] += len(units)

            def project(count, segs, src, dest, ready):
                if ready == "attn":
                    if n["unit"] > 0:
                        pe.wait_ge(sem("attended"), n["unit"])
                    if dest is None:
                        pe.wait_ge(sem("convolved"), more("convolved"))
                for _ in range(count):
                    columns(panel(), range(4), src, segs)

            def mlp(segs, beside):
                ready = "h_act"
                ends = {}
                for step, (kind, g) in enumerate(mlp_steps(len(FF1_GROUPS))):
                    if beside and step in MOD_STEPS:
                        mod(1, 2 * (step - MOD_STEPS[0]), 2 * (step - MOD_STEPS[0]) + 2)
                    if kind == "down":
                        if ends[g] > 0:
                            pe.wait_ge(sem("tile_free"), ends[g])
                    for _ in range(2):
                        columns(panel(), range(4), H if kind == "up" else hidden1[g % 2], segs, KD, ready)
                        ready = None
                    ends[g] = n["tile"]

            def swiglu():
                ready = "h_dve"
                ends = {}
                for kind, g in mlp_steps(len(FF2_GROUPS)):
                    if kind == "up":
                        for _ in range(FF2_GROUPS[g] // 2):
                            columns(panel(), range(4), H, SEG1, KD, ready)
                            ready = None
                        ends[g] = n["tile"]
                    else:
                        if ends[g] > 0:
                            pe.wait_ge(sem("tile_free"), ends[g])
                        for _ in range(2):
                            columns(panel(), range(4), hidden2[g % 2], SEG1, FF2_GROUPS[g])

            def odd_in():
                n["h_act"] += KD
                w = panel()
                columns(w, [0], K, SEG2, ready="mix")
                columns(w, [1], MIX, SEG2, ready="mix")
                columns(w, [2], K, SEG1, ready="mix")
                ready = "mix"
                for _ in range(2):
                    columns(panel(), range(4), MIX, SEG2, ready=ready)
                    ready = None
                ready = "mix"
                for h in range(2):
                    w = panel()
                    lo = C if h == 0 else 0
                    for c in range(CHUNKS):
                        accumulate(tile()[lo:lo + C, :], lambda k: MIX[:, k, c * C:(c + 1) * C], lambda k: w[:, k, :],
                                   KD, ready)
                        ready = None
                panel()
                ready = "mix"
                for _ in range(2):
                    columns(panel(), range(4), XX, SEG1, ready=ready)
                    ready = None
                if n["tile"] > 0:
                    pe.wait_ge(sem("tile_free"), n["tile"])
                pe.wait_ge(sem("lora"), more("lora", 3))
                if n["norm"] > 0:
                    pe.wait_ge(sem("var"), n["norm"])

            def half(h):
                return slice(C * h, C * h + C)

            def features(j, i):
                p, d = divmod(j, 2)
                for at_slot, what in FEATURE_SLOTS:
                    if at_slot != i or (what == "norm" and d == 1):
                        continue
                    for bank, (a, b) in zip((4, 5), SEG2):
                        if n["feature_pe"] - 1 > 0:
                            pe.wait_ge(sem("feature_read"), n["feature_pe"] - 1)
                        if what == "norm":
                            pe.wait_ge(sem("key_square"), more("key_square"))
                            left, right = head_ones, square[:, 0, a:b]
                        elif what == "decay":
                            left, right = lora2[half(d), 0, p * P:(p + 1) * P], decay_in[half(d), a:b]
                        else:
                            left, right = lora2[half(d), 1, p * P:(p + 1) * P], a_in[half(d), a:b]
                        pe.matmul(ps[:, bank, 0:b - a], left, right, start=True, stop=True).then_inc(
                            sem("feature_pe"), one("feature_pe"))

            def prepare(j, i, b):
                p, d = divmod(j, 2)
                S = sets[d]
                if 1 <= i <= GRAMS:
                    g = i - 1
                    if g == 0:
                        if n["feature_pe"] > 0:
                            pe.wait_ge(sem("feature_read"), n["feature_pe"])
                        pe.wait_ge(sem("keys"), more("keys"))
                        pe.wait_ge(sem("decayed"), more("decayed"))
                    elif g == 2:
                        pe.wait_ge(sem("decayed"), more("decayed"))
                    if GRAMS * j + g - 1 > 0:
                        pe.wait_ge(sem("gram_read"), GRAMS * j + g - 1)
                    if GRAMS * j + g - 1 > 0:
                        pe.wait_ge(sem("gram_copied"), GRAMS * j + g - 1)
                    bank = 2 * (g % 2)
                    pair = (2 * g, 2 * g + 1)
                    for n_c, c in enumerate(pair):
                        for h in range(2):
                            right = S["kr"][half(h), c, :, :] if c < LAT // C else S["kr"][half(h), c, 0:1, :]
                            wd = 2 * C if c < LAT // C else C
                            o = n_c * 2 * C
                            pe.matmul(ps[:, bank + h, o:o + wd], bk[half(h), c, :, :].rearrange("p a b -> p (a b)"),
                                      right.rearrange("p a b -> p (a b)"), start=True, stop=True)
                    for n_c, c in enumerate(pair):
                        for h in range(2):
                            pe.matmul(ps[half(h), 4 + g % 2, n_c * C:(n_c + 1) * C], S["kr"][half(h), c, 0, :], bk[half(h), c, h, :],
                                      start=True, stop=True)
                    for n_c, c in enumerate(pair):
                        o = (1 + n_c) * P
                        ins = pe.transpose(ps[:, 4 + g % 2, o:o + P], bk[:, c, :, :].rearrange("p a b -> p (a b)"), ident)
                    ins.then_inc(sem("gram"), one("gram"))
                elif i == INVERSE - 1:
                    pe.wait_ge(sem("values"), j + 1)
                    pe.wait_ge(sem("gram_read"), GRAMS * (j + 1))
                    pe.wait_ge(sem("gram_copied"), GRAMS * (j + 1))
                    batch(b, b, lambda c, h: couple[half(1 - h), h, c, :], lambda c, h: S["uv"][half(1 - h), c, h, :]
                          ).then_inc(sem("value_product"), one("value_product"))
                elif i > INVERSE:
                    level, q = divmod(i - INVERSE - 1, 3)
                    last = level == LEVELS - 2
                    if q == 0:
                        if b == 0 and not last:
                            pe.wait_ge(sem("masked"), (GRAMS + LEVELS - 2) * j + GRAMS + level + 1)
                        pe.wait_ge(sem("inverse"), 2 * (LEVELS * j + level) + b + 1)
                        pe.wait_ge(sem("values_read"), 2 * j + b + 1)
                        if last:
                            ins = last_batch(b, d, lambda c, h, rows, cols: couple[rows, h, c, cols],
                                             lambda c, h, rows, cols: f_x[rows, c, cols])
                        else:
                            ins = batch(b, b, lambda c, h: f_am[half(h), c, :], lambda c, h: f_x[half(h), c, :])
                        ins.then_inc(sem("first_product"), one("first_product"))
                    elif q == 1:
                        pe.wait_ge(sem("first_copied"), more("first_copied"))
                        if level < LEVELS - 2:
                            batch(2 + b, b, lambda c, h: S["xt"][half(h), c, :], lambda c, h: f_y1[half(h), c, :]
                                  ).then_inc(sem("second_product"), one("second_product"))
                    else:
                        if last:
                            ins = last_batch(b, 1 - d, lambda c, h, rows, cols: f_y1[rows, c, 0:C // 2],
                                             lambda c, h, rows, cols: S["xt"][rows, c, cols])
                        else:
                            ins = batch(b, b, lambda c, h: f_y1[half(h), c, :], lambda c, h: S["xt"][half(h), c, :])
                        ins.then_inc(sem("third_product"), one("third_product"))

            def last_batch(b, d, left, right):
                for k in range(HALF):
                    for h in range(2):
                        c = b * HALF + k
                        of_rows, to_rows, of, to = last_level(d, h)
                        ins = pe.matmul(ps[to_rows, b, k * C // 2:(k + 1) * C // 2], left(c, h, of_rows, to),
                                        right(c, h, of_rows, of), start=True, stop=True)
                return ins

            def batch(bank, b, left, right):
                for k in range(HALF):
                    for h in range(2):
                        ins = pe.matmul(ps[half(h), bank, k * C:(k + 1) * C], left(b * HALF + k, h), right(b * HALF + k, h),
                                        start=True, stop=True)
                return ins

            def state_in(j, s):
                d = j % 2
                S, c = sets[d], chunk_order(d)[s]
                if s == 0:
                    pe.wait_ge(sem("inverse"), 2 * LEVELS * (j + 1))
                pe.wait_ge(sem("state"), more("state"))
                for h in range(2):
                    ins = pe.matmul(ps[half(h), 6, 0:C], S["kr"][half(h), c, 0, :], state[half(h), d, :],
                                    start=True, stop=True)
                ins.then_inc(sem("from_state"), one("from_state"))

            def solve(j, s):
                d = j % 2
                S, c = sets[d], chunk_order(d)[s]
                pe.wait_ge(sem("residual"), more("residual"))
                for h in range(2):
                    ins = pe.matmul(ps[half(h), 6, C:2 * C], S["xt"][half(h), c, :], w0_neg[half(h), d, :],
                                    start=True, stop=True)
                ins.then_inc(sem("solved"), one("solved"))
                if c < LAT // C:
                    if n["y"] > 0:
                        pe.wait_ge(sem("y_read"), n["y"])
                    for h in range(2):
                        pe.matmul(ps[half(h), 7, 0:C], state[half(h), d, :], S["kr"][half(h), c, 1, :],
                                  start=True, stop=False)

            def state_out(j, s):
                d = j % 2
                S, c = sets[d], chunk_order(d)[s]
                pe.wait_ge(sem("update"), more("update"))
                if s < CHUNKS - 1:
                    for h in range(2):
                        ins = pe.matmul(ps[half(h), 6, 2 * C:3 * C], S["bkn"][:, c, half(h)], S["uv"][:, c, h, :],
                                        start=True, stop=True)
                    ins.then_inc(sem("to_state"), one("to_state"))
                if c < LAT // C:
                    for h in range(2):
                        ins = pe.matmul(ps[half(h), 7, 0:C], S["uv"][:, c, h, :], S["gram"][:, c, h, :],
                                        start=False, stop=True)
                    ins.then_inc(sem("y"), one("y"))

            def readout(p):
                pe.wait_ge(sem("read_dve"), more("read_dve"))
                n["read_dve"] += 2
                pe.matmul(ps[:, 0, :], head_ones, y_pair, start=True, stop=True).then_inc(sem("read_pe"), one("read_pe"))
                pe.matmul(ps[:, 1, :], head_ones, R[:, p, :], start=True, stop=True)
                for c in range(LAT // C):
                    for h in range(2):
                        pe.matmul(ps[half(h), 2, c * C:(c + 1) * C], V[half(1 - h), c, p, :],
                                  ccol("ident2", 0, C)[half(1 - h), :], start=True, stop=True)
                pe.matmul(ps[:, 3, :], lora2[:, 2, p * P:(p + 1) * P], gate_in, start=True, stop=True).then_inc(sem("read_pe"), one("read_pe"))
                pe.wait_ge(sem("read_act"), more("read_act"))
                pe.matmul(ps[:, 4, :], head_ones, square[:, 0, 0:LAT], start=True, stop=True).then_inc(sem("read_pe"), one("read_pe"))
                pe.wait_ge(sem("read_dve"), n["read_dve"])
                pe.wait_ge(sem("bonus"), more("bonus"))
                pe.wait_ge(sem("gate"), more("gate"))

            def mix_in(l):
                w = panel()
                columns(w, range(2), H, SEGM, ready="h_dve")
                for t in range(2):
                    accumulate(tile()[:, 0:CTX], lambda k: H[:, k, LAT + t * P:LAT + (t + 1) * P],
                               lambda k: w[:, k, CTX:2 * CTX])
                columns(panel(), range(4), H, SEG1, ready="h_dve")
                w = panel()
                columns(w, range(2), H, SEG1)
                for u in range(MIX_TILES):
                    if u < 6:
                        if u == 2:
                            w = panel()
                        columns(w, [(u + 2) % 4], H, SEG1)
                    else:
                        if u == 6:
                            w = panel()
                        rows(w, 0, P, H, [u - 6], 0)
                    if u < 8:
                        sums(head_ones, 1, 0, LAT if u < 6 else CTX)
                    if 1 <= u <= 4:
                        pe.wait_ge(sem("normed"), more("normed"))
                        if n["rotated"] > 0:
                            pe.wait_ge(sem("rotated_read"), n["rotated"])
                        pe.matmul(ps[:, 5, :], rotate, q2[:, u - 1, :], start=True, stop=True).then_inc(sem("rotated"), one("rotated"))

            def conv(l):
                pe.wait_ge(sem("tapped"), more("tapped"))
                sums(ones[:, :], 3, 0, LAT, "conv")
                sums(ones[:, :], 3, 0, LAT)

            skip = lambda *a: None
            model(dict(load=load, mod=mod, gains=skip, norm_mod=norm_mod, even_in=even_in, attention=attention,
                       project=project, post=post, mlp=mlp, odd_in=odd_in, features=features, prepare=prepare, state_in=state_in,
                       solve=solve, state_out=state_out, readout=readout, readout_end=skip, odd_out=skip, tables=skip,
                       norm_vec=norm_vec, swiglu=swiglu, half_step=skip, mix_in=mix_in, conv=conv, store=skip))

        @block.scalar
        def _(act):
            n, more, one = counting()
            sigmoid_used = [0, 0]

            def load():
                act.wait_ge(sem("small_in"), 32)
                act.activation(silu_c[:, :, :], raw_c[:, :, :], ACT.Sigmoid).then_inc(sem("sigmoid_c"), one("sigmoid_c"))
                n["source"] = "load"

            def squares(src, count, lo, hi, ready):
                if sigmoid_used[-1] > 0:
                    act.wait_ge(sem("tile_free"), sigmoid_used[-1])
                for c in range(count):
                    ready(c)
                    if n["sq"] - 1 + n["plain_sums"] > 0:
                        act.wait_ge(sem("summed"), n["sq"] - 1 + n["plain_sums"])
                    act.activation(square[:, n["sq"] % 2, 0:hi - lo], src(c), ACT.Square).then_inc(sem("square"), one("square"))
                    n["sq"] += 1
                act.wait_ge(sem("var"), more("var"))
                act.activation(rstd[:, 0:hi - lo], rstd[:, 0:hi - lo], ACT.Sqrt).then_inc(sem("std"), one("std"))

            def source():
                kind = n["source"]
                if kind == "load":
                    act.wait_ge(sem("x_in"), 16)
                    return lambda c: None
                if kind == "x_chunk":
                    base = n["x_chunk"] - KD
                    return lambda c: act.wait_ge(sem("x_chunk"), base + c + 1)
                base = n["tile"] - KD
                return lambda c: act.wait_ge(sem("tile_free"), base + c + 1)

            def mod(i, lo, hi):
                n["tile"] += 2 * (hi - lo)

            def norm_mod(i, which):
                hi = TOK if (i, which) != (1, 2) else LAT
                squares(lambda c: X[:, c, 0:hi], KD, 0, hi, source())
                act.wait_ge(sem("gains"), more("gains")) if which == 0 and i == 0 else None
                if (i, which) != (0, 0):
                    act.wait_ge(sem("gains"), 2 if i == 0 else 4)
                for c in range(KD):
                    act.wait_ge(sem("scaled"), more("scaled"))
                    for v, (a, b) in enumerate(((0, LAT), (LAT, TOK))):
                        if b <= hi:
                            ins = act.activation(H[:, c, a:b], H[:, c, a:b], ACT.Identity,
                                                 bias=mod_col(i, 3 * (which // 2), v, c), scale=gain[:, i, which, v, c:c + 1])
                    ins.then_inc(sem("h_act"), one("h_act"))

            def mod_col(i, part, v, c):
                return mod_sb[:, i, v, part * KD + c:part * KD + c + 1]

            def norm_vec(lo, hi, name, l, src):
                if lo == LAT:
                    act.wait_ge(sem("mem_in"), 16)
                    ready = lambda c: None
                else:
                    ready = source()
                squares(lambda c: X[:, c, lo:hi], KD, lo, hi, ready)
                if name == "final_norm":
                    n["x_chunk"] += KD
                    n["source"] = "x_chunk"

            def even_in():
                n["tile"] += 24 + TOK // P + 8 + 2 * 8

            def conv_tap(l, tap):
                for c in POOL_CHANNELS:
                    w, src = vcol(f"conv_w{l}", c * TAPS + tap), conv_in[:, c, tap:tap + LAT]
                    if tap == 0:
                        ins = act.activation(conv_y[:, c, :], src, ACT.Identity, bias=vcol(f"conv_b{l}", c), scale=w)
                    else:
                        if tap > 1:
                            act.wait_ge(sem("pool_tap"), more("pool_tap"))
                        ins = act.activation(tap_product[c], src, ACT.Identity, scale=w)
                    ins.then_inc(sem("tap_product"), one("tap_product"))
                if tap == TAPS - 1:
                    n["pool_tap"] += len(POOL_CHANNELS)

            def attention(units, l):
                base = n["unit"]
                for i in range(len(units) + 2):
                    if l is not None and 1 <= i <= TAPS:
                        conv_tap(l, i - 1)
                    if i < len(units):
                        unit, u = units[i], base + i
                        w = unit["width"]
                        act.wait_ge(sem("row_max"), more("row_max"))
                        act.activation(probs[:, u % 3, 0:w], probs[:, u % 3, 0:w], ACT.Exp,
                                           bias=stat[:, 4 * (u % 3) + 1:4 * (u % 3) + 2],
                                           accum_out=stat[:, 4 * (u % 3) + 2:4 * (u % 3) + 3]).then_inc(sem("exped"), one("exped"))
                        if unit["sink"] is not None:
                            act.activation(stat[:, 4 * (u % 3) + 3:4 * (u % 3) + 4], unit["sink"], ACT.Exp,
                                               bias=stat[:, 4 * (u % 3) + 1:4 * (u % 3) + 2]).then_inc(sem("exped_sink"), one("exped_sink"))
                    if i >= 2:
                        unit, u = units[i - 2], base + i - 2
                        w = unit["width"]
                        act.wait_ge(sem("turned"), more("turned"))
                        if u - 1 > 0:
                            act.wait_ge(sem("output"), u - 1)
                        act.copy(probsT[:, u % 2, 0:w], turned_ps(w)).then_inc(sem("turned_copy"), one("turned_copy"))
                n["unit"] += len(units)

            def project(count, segs, src, dest, ready):
                n["tile"] += 4 * count * len(segs)
                n["source"] = "tile"
                n["last"] = len(segs)

            def post(src, i, which):
                hi = TOK if i == 0 else LAT
                nseg = n["last"]
                base = n["tile"] - KD * nseg
                act.wait_ge(sem("gains"), 2 if i == 0 else 4)

                def scale_chunk(c):
                    act.wait_ge(sem("square"), n["sq"])
                    for v, (a, b) in enumerate(((0, LAT), (LAT, TOK))):
                        if b <= hi:
                            ins = act.activation(src[:, c, a:b], src[:, c, a:b], ACT.Identity,
                                                 scale=gain[:, i, which, v, c:c + 1])
                    ins.then_inc(sem("gated"), one("gated"))

                def ready(c):
                    if c > 0:
                        scale_chunk(c - 1)
                    act.wait_ge(sem("tile_free"), base + nseg * (c + 1))

                squares(lambda c: src[:, c, 0:hi], KD, 0, hi, ready)
                scale_chunk(KD - 1)
                n["x_chunk"] += KD
                n["source"] = "x_chunk"

            def mlp(segs, beside):
                for step, (kind, g) in enumerate(mlp_steps(len(FF1_GROUPS))):
                    if beside and step in MOD_STEPS:
                        mod(1, 2 * (step - MOD_STEPS[0]), 2 * (step - MOD_STEPS[0]) + 2)
                    for c in range(8):
                        for a, b in segs:
                            if kind == "up":
                                if n["tile"] + 1 > 0:
                                    act.wait_ge(sem("tile_done"), n["tile"] + 1)
                                act.activation(hidden1[g % 2][:, c, a:b], ps[:, n["tile"] % 4, 0:b - a], ACT.Relu).then_inc(sem("relu"), one("relu"))
                            n["tile"] += 1
                n["last"] = len(segs)

            def swiglu():
                for kind, g in mlp_steps(len(FF2_GROUPS)):
                    if kind == "down":
                        n["tile"] += 8
                        continue
                    for c in range(FF2_GROUPS[g]):
                        if sigmoid_used[-2] > 0:
                            act.wait_ge(sem("tile_free"), sigmoid_used[-2])
                        if n["tile"] + 1 > 0:
                            act.wait_ge(sem("tile_done"), n["tile"] + 1)
                        sigmoid_used.append(n["tile"] + 1)
                        act.activation(sig[:, n["sig"] % 2, :], ps[:, n["tile"] % 4, :], ACT.Sigmoid).then_inc(sem("sigmoid"), one("sigmoid"))
                        n["sig"] += 1
                        n["tile"] += 2

            def half_step():
                n["x_chunk"] += KD
                n["source"] = "x_chunk"

            def odd_in():
                base = n["tile"]
                n["tile"] += 5 + 16 + 2 * CHUNKS + 8
                act.wait_ge(sem("mix"), 6 * KD)
                if base + 5 > 0:
                    act.wait_ge(sem("tile_free"), base + 5)
                act.activation(decay_in, square[:, 0, :], ACT.Tanh).then_inc(sem("lora"), one("lora"))
                act.copy(a_in, square[:, 1, :]).then_inc(sem("lora"), one("lora"))
                act.activation(gate_in, rstd[:, 0:LAT], ACT.Sigmoid).then_inc(sem("lora"), one("lora"))
                act.wait_ge(sem("lora"), 3)

            def half(h):
                return slice(C * h, C * h + C)

            def features(j, i):
                p, d = divmod(j, 2)
                for at_slot, what in FEATURE_SLOTS:
                    if at_slot != i or (what == "norm" and d == 1):
                        continue
                    if what == "norm":
                        for bank, (a, b) in zip((4, 5), SEG2):
                            act.wait_ge(sem("feature_pe"), more("feature_pe"))
                            act.copy(rstd[:, a:b], ps[:, bank, 0:b - a]).then_inc(sem("feature_read"), one("feature_read"))
                        continue
                    if what == "decay":
                        act.wait_ge(sem("exponents"), 2 * j) if j > 0 else None
                        dest, bias = f_cs, vcol(f"w0{d}", p)
                    else:
                        act.wait_ge(sem("keys"), j) if j > 0 else None
                        dest, bias = f_a, vcol(f"a0{d}", p)
                    for bank, (a, b) in zip((4, 5), SEG2):
                        act.wait_ge(sem("feature_pe"), more("feature_pe"))
                        act.activation(dest[:, a:b], ps[:, bank, 0:b - a], ACT.Sigmoid, bias=bias).then_inc(
                            sem("feature_read"), one("feature_read"))
                if i == SQUARE_SLOT and d == 0:
                    act.wait_ge(sem("feature_dve"), more("feature_dve"))
                    for a, b in SEG2:
                        act.activation(square[:, 0, a:b], f_kk[:, a:b], ACT.Square).then_inc(
                            sem("key_square"), one("key_square"))
                if i == ROOT_SLOT and d == 0:
                    act.wait_ge(sem("feature_dve"), more("feature_dve"))
                    act.activation(rstd[:, :], rstd[:, :], ACT.Sqrt).then_inc(sem("key_root"), one("key_root"))
                if i == EXPONENT_SLOT:
                    act.wait_ge(sem("running"), more("running"))
                    act.wait_ge(sem("decayed"), 2 * j) if j > 0 else None
                    act.wait_ge(sem("keys"), j) if j > 0 else None
                    act.activation(f_inc, f_cs, ACT.Exp, scale=-E_HALF).then_inc(sem("exponents"), one("exponents"))
                    act.activation(f_inv, f_cs, ACT.Exp, scale=E_HALF).then_inc(sem("exponents"), one("exponents"))

            def prepare(j, i, b):
                p, d = divmod(j, 2)
                S = sets[d]
                if 1 <= i <= GRAMS:
                    c = 2 * (i - 1)
                    act.wait_ge(sem("gram"), more("gram"))
                    bank = ps[:, 4 + (i - 1) % 2, :]
                    act.copy(S["bkn"][:, c:c + 2, :], bank[:, P:3 * P].rearrange("p (a b) -> p a b", a=2))
                    act.copy(f_x[:, c:c + 2, :], bank[:, 0:P].rearrange("p (a b) -> p a b", a=2)).then_inc(
                        sem("gram_copied"), one("gram_copied"))
                elif i == INVERSE - 1:
                    act.wait_ge(sem("value_product"), more("value_product"))
                    act.mul(S["bv"][:, b * HALF:(b + 1) * HALF, :], chunked(ps[:, b, 0:HALF * C]), -1.0).then_inc(
                        sem("values_read"), one("values_read"))
                elif i > INVERSE and (i - INVERSE - 1) % 3 == 0:
                    act.wait_ge(sem("first_product"), more("first_product"))
                    if i == INVERSE + 1 + 3 * (LEVELS - 2):
                        for h in range(2):
                            _, to_rows, _, _ = last_level(d, h)
                            ins = act.copy(f_y1[to_rows, b * HALF:(b + 1) * HALF, 0:C // 2],
                                           ps[to_rows, b, 0:HALF * C // 2].rearrange("p (c t) -> p c t", t=C // 2))
                        ins.then_inc(sem("first_copied"), one("first_copied"))
                        return
                    act.copy(f_y1[:, b * HALF:(b + 1) * HALF, :], chunked(ps[:, b, 0:HALF * C])).then_inc(
                        sem("first_copied"), one("first_copied"))

            def solve(j, s):
                d = j % 2
                S, c = sets[d], chunk_order(d)[s]
                act.wait_ge(sem("solved"), more("solved"))
                for h in range(2):
                    ins = act.copy(S["uv"][half(h), c, h, :], ps[half(h), 6, C:2 * C])
                ins.then_inc(sem("update"), one("update"))

            def readout(p):
                act.wait_ge(sem("read_pe"), more("read_pe", 2))
                act.copy(v_turned, ps[:, 2, :]).then_inc(sem("read_act_v"), one("read_act_v"))
                act.wait_ge(sem("read_dve"), more("read_dve", 2))
                act.activation(square[:, 0, 0:LAT], y_pair, ACT.Square).then_inc(sem("read_act"), one("read_act"))
                act.wait_ge(sem("read_pe"), more("read_pe"))
                act.copy(square[:, 0, 0:LAT], ps[:, 3, :]).then_inc(sem("gate"), one("gate"))
                act.wait_ge(sem("read_dve"), more("read_dve"))
                act.activation(rstd[:, 0:LAT], rstd[:, 0:LAT], ACT.Sqrt).then_inc(sem("read_act_root"), one("read_act_root"))

            def tables():
                act.wait_ge(sem("angle"), more("angle"))
                act.activation(rope[:, 1, :], rope_tmp[:, 0, :], ACT.Sin).then_inc(sem("sine"), one("sine"))
                act.activation(rope[:, 0, :], rope_tmp[:, 0, :], ACT.Sin, scale=0.5).then_inc(sem("sine"), one("sine"))

            def mix_in(l):
                mem, heads = n["tile"], n["tile"] + 4
                gates = heads + 6
                for u in range(MIX_TILES):
                    if u in (1, 3, 5):
                        act.wait_ge(sem("tile_done"), gates + u + 1)
                        act.activation(conv_y[:, u // 2, :], ps[:, (gates + u) % 4, :], ACT.Sigmoid).then_inc(
                            sem("sigmoid"), one("sigmoid"))
                    if u < 8:
                        src = q2[:, u, :] if u < 6 else mk2[:, u - 6, :]
                        copied = heads + u + 1 if u < 6 else mem + u - 6 + 1
                        squares(lambda c: src, 1, 0, LAT if u < 6 else CTX, lambda c: act.wait_ge(sem("tile_free"), copied))
                n["tile"] += 4 + 12 + LAT // P

            def conv(l):
                act.wait_ge(sem("tapped"), more("tapped"))
                n["plain_sums"] += 3
                n["var"] += 1
                squares(lambda c: conv_y[:, c, :], 3, 0, LAT, lambda c: act.wait_ge(sem("centred"), more("centred")))
                for c in range(3):
                    act.wait_ge(sem("conv_z"), more("conv_z"))
                    act.activation(sig[:, c % 2, :] if c < 2 else rstd[:, 0:LAT], conv_y[:, c, :], ACT.Sigmoid).then_inc(sem("conv_sigmoid"), one("conv_sigmoid"))

            skip = lambda *a: None
            model(dict(load=load, mod=mod, gains=skip, norm_mod=norm_mod, even_in=even_in, attention=attention,
                       project=project, post=post, mlp=mlp, odd_in=odd_in, features=features, prepare=prepare, state_in=skip, solve=solve,
                       state_out=skip, readout=readout, readout_end=skip, odd_out=skip, tables=tables, norm_vec=norm_vec, swiglu=swiglu,
                       half_step=half_step, mix_in=mix_in, conv=conv, store=skip))

        @block.vector
        def _(dve):
            n, more, one = counting()

            def settle(ins):
                ins.then_inc(sem("own"), one("own"))
                dve.wait_ge(sem("own"), n["own"])

            def tile():
                dve.wait_ge(sem("tile_done"), more("tile_done"))
                n["tile"] += 1
                return ps[:, (n["tile"] - 1) % 4, :]

            def load():
                dve.wait_ge(sem("small_in"), 32)
                settle(dve.tensor_scalar(omka[:, :], vcol("ka", 0, KD), -1.0, 1.0, ALU.mult, ALU.add))
                dve.wait_ge(sem("sigmoid_c"), more("sigmoid_c"))
                dve.tensor_tensor(silu_c[:, :, :], silu_c[:, :, :], raw_c[:, :, :], ALU.mult).then_inc(sem("silu"), one("silu"))

            def mod(i, lo, hi):
                for j in range(lo, hi):
                    if j % 2 == 0:
                        for r in range(2):
                            dve.tensor_copy(square[0:2, r, 0:COLS], tile()[0:2, :]).then_inc(
                                sem("tile_free"), one("tile_free"))
                    bank = tile()
                    b = vcol(f"ada_b{i}", 4 * j, 4)
                    for v in range(2):
                        ins = dve.tensor_tensor(mod_sb[:, i, v, 4 * j:4 * j + 4], bank[:, v:8:2], b, ALU.add)
                    ins.then_inc(sem("tile_free"), one("tile_free"))

            def gains(i, part):
                if n["tile"] > 0:
                    dve.wait_ge(sem("tile_free"), n["tile"])
                for which in ((0,), (1, 2, 3))[part]:
                    for v in range(2):
                        g = vcol(f"norm_g{i}{which}", 0, KD)
                        chunk = (1, 2, 4, 5)[which]
                        m = mod_sb[:, i, v, chunk * KD:(chunk + 1) * KD]
                        ins = dve.scalar_tensor_tensor(gain[:, i, which, v, :], m, 0.0 if which % 2 else 1.0, g, ALU.add,
                                                       ALU.mult)
                ins.then_inc(sem("gains"), one("gains"))
                dve.wait_ge(sem("gains"), n["gains"])

            def inverse_root(count, lo, hi, mean, eps, op=ALU.add):
                dve.wait_ge(sem("summed"), more("summed", count))
                r = rstd[:, 0:hi - lo]
                dve.tensor_scalar(r, norm_psum(lo, hi), mean, eps, ALU.mult, op).then_inc(sem("var"), one("var"))
                dve.wait_ge(sem("std"), more("std"))
                settle(dve.reciprocal(r, r))
                return r

            def norm_mod(i, which):
                hi = TOK if (i, which) != (1, 2) else LAT
                r = inverse_root(KD, 0, hi, 1.0 / D, 1e-6)
                for c in range(KD):
                    dve.tensor_tensor(H[:, c, 0:hi], X[:, c, 0:hi], r, ALU.mult).then_inc(sem("scaled"), one("scaled"))
                n["h_act"] += KD

            def norm_vec(lo, hi, name, l, src):
                r = inverse_root(KD, lo, hi, 1.0 / D, 1e-6)
                dest, signal = (X, "x_chunk") if name == "final_norm" else (H, "h_dve")
                for c in range(KD):
                    dve.scalar_tensor_tensor(dest[:, c, lo:hi], X[:, c, lo:hi], vcol(f"{name}{l}", c), r, ALU.mult,
                                                 ALU.mult).then_inc(sem(signal), one(signal))
                dve.wait_ge(sem(signal), n[signal])

            def copies(dest, ms, segs):
                for m in ms:
                    for a, b in segs:
                        dve.tensor_copy(dest[:, m, a:b], tile()[:, 0:b - a]).then_inc(sem("tile_free"), one("tile_free"))

            def even_in():
                u, s0, s1 = pool_buf
                GAP = 8
                parts = ((0, LAT, GAP), (LAT, TOK, GAP + LAT + GAP))
                dve.wait_ge(sem("const_in"), 16)
                settle(dve.memset(u, 0.0))
                for g, w in enumerate(POOL_WINDOWS):
                    for a, b, o in parts:
                        dve.tensor_copy(u[:, o:o + b - a], tile()[:, 0:b - a]).then_inc(sem("tile_free"), one("tile_free"))
                    dve.wait_ge(sem("tile_free"), n["tile_free"])
                    src, width = u, 1
                    while width < w:
                        dest = s0 if src is not s0 else s1
                        m = 792 - 2 * width + 1
                        settle(dve.tensor_tensor(dest[:, 0:m], src[:, 0:m], src[:, width:width + m], ALU.add))
                        src, width = dest, 2 * width
                    edge = ccol("pool_edge", 2 * (w // 2 - 1), w)
                    diff = Y[:, 4 + g, :]
                    for a, b, o in parts:
                        ins = dve.tensor_scalar(diff[:, a:b], src[:, o - w // 2:o - w // 2 + b - a], 1.0 / w, None, ALU.mult)
                    settle(ins)
                    for a, b, o in parts:
                        dve.tensor_tensor(diff[:, a:a + w // 2], diff[:, a:a + w // 2], edge[:, 0:w // 2], ALU.mult)
                        ins = dve.tensor_tensor(diff[:, b - w // 2:b], diff[:, b - w // 2:b], edge[:, w // 2:w], ALU.mult)
                    settle(ins)
                    for a, b, o in parts:
                        ins = dve.tensor_tensor(diff[:, a:b], diff[:, a:b], u[:, o:o + b - a], ALU.subtract)
                    ins.then_inc(sem("pooled"), one("pooled"))
                    dve.wait_ge(sem("pooled"), n["pooled"])
                mod(0, 4, 6)
                copies(qT, range(4), SEG2)
                mod(0, 6, 8)
                copies(kT, range(4), SEG2)
                mod(0, 8, 10)
                for t in range(TOK // P):
                    dve.tensor_copy(vN[:, t, :], tile()).then_inc(sem("tile_free"), one("tile_free"))
                mod(0, 10, 12)
                for g in range(4):
                    for a, b in SEG2:
                        dve.tensor_scalar(Y[:, g, a:b], tile()[:, 0:b - a], vcol("pool_scale", g), None, ALU.mult).then_inc(sem("tile_free"), one("tile_free"))

            def conv_tap(l, tap):
                for c in DVE_CHANNELS:
                    w, src = vcol(f"conv_w{l}", c * TAPS + tap), conv_in[:, c, tap:tap + LAT]
                    if tap == 0:
                        ins = dve.tensor_scalar(conv_y[:, c, :], src, w, vcol(f"conv_b{l}", c), ALU.mult, ALU.add)
                    else:
                        dve.wait_ge(sem("tap"), n["tap"] - len(DVE_CHANNELS) + 1)
                        ins = dve.scalar_tensor_tensor(conv_y[:, c, :], src, w, conv_y[:, c, :], ALU.mult, ALU.add)
                    ins.then_inc(sem("tap"), one("tap"))

            def attention(units, l):
                base = n["unit"]
                scale = C ** -0.5
                for i in range(len(units) + 4):
                    if i < len(units):
                        unit, u = units[i], base + i
                        w, o = unit["width"], 4 * (u % 3)
                        dve.wait_ge(sem("scores"), more("scores"))
                        if u - 2 > 0:
                            dve.wait_ge(sem("turned"), u - 2)
                        S, raw = probs[:, u % 3, :], scores_ps(u, w)
                        wb = 0
                        if unit["bias"] is not None:
                            wb = min(w, LAT)
                            if unit["bias_head"] is not None:
                                h = unit["bias_head"]
                                dve.wait_ge(sem(f"bias{h % 2}"), 16 * (h // 2 + 1))
                            ins = dve.scalar_tensor_tensor(S[:, 0:wb], raw[:, 0:wb], scale, unit["bias"], ALU.mult, ALU.add)
                        if wb < w:
                            ins = dve.tensor_scalar(S[:, wb:w], raw[:, wb:w], scale, None, ALU.mult)
                        ins.then_inc(sem("scored"), one("scored"))
                        dve.wait_ge(sem("scored"), n["scored"])
                        settle(dve.tensor_reduce(stat[:, o:o + 1], S[:, 0:w], AX.X, ALU.max))
                        if unit["sink"] is not None:
                            settle(dve.tensor_tensor(stat[:, o:o + 1], stat[:, o:o + 1], unit["sink"], ALU.max))
                        dve.tensor_scalar(stat[:, o + 1:o + 2], stat[:, o:o + 1], -1.0, None, ALU.mult).then_inc(sem("row_max"), one("row_max"))
                    if 1 <= i <= len(units):
                        unit, u = units[i - 1], base + i - 1
                        w, o = unit["width"], 4 * (u % 3)
                        dve.wait_ge(sem("exped"), more("exped"))
                        if unit["sink"] is not None:
                            dve.wait_ge(sem("exped_sink"), more("exped_sink"))
                            settle(dve.tensor_tensor(stat[:, o + 2:o + 3], stat[:, o + 2:o + 3], stat[:, o + 3:o + 4], ALU.add))
                        settle(dve.reciprocal(stat[:, o + 2:o + 3], stat[:, o + 2:o + 3]))
                        dve.tensor_scalar(probs[:, u % 3, 0:w], probs[:, u % 3, 0:w], stat[:, o + 2:o + 3], None,
                                              ALU.mult).then_inc(sem("probs"), one("probs"))
                    if l is not None and i < TAPS:
                        conv_tap(l, i)
                    if i >= 4:
                        unit, u = units[i - 4], base + i - 4
                        b = unit["base"]
                        dve.wait_ge(sem("output"), more("output"))
                        dve.tensor_copy(unit["dest"], ps[b:b + C, 6 + u % 2, 0:P]).then_inc(sem("attended"), one("attended"))
                n["unit"] += len(units)

            def project(count, segs, src, dest, ready):
                for c in range(4 * count):
                    for a, b in segs:
                        bank = tile()[:, 0:b - a]
                        if dest is None:
                            ins = dve.tensor_tensor(X[:, c, a:b], bank, X[:, c, a:b], ALU.add)
                        else:
                            ins = dve.tensor_copy(dest[:, c, a:b], bank)
                        ins.then_inc(sem("tile_free"), one("tile_free"))

            def post(src, i, which):
                hi = TOK if i == 0 else LAT
                r = inverse_root(KD, 0, hi, 1.0 / D, 1e-6)
                if (i, which) == (1, 1):
                    dve.wait_ge(sem("x_back"), 16)
                for c in range(KD):
                    dve.wait_ge(sem("gated"), more("gated"))
                    dve.tensor_tensor(src[:, c, 0:hi], src[:, c, 0:hi], r, ALU.mult).then_inc(sem("normalised"), one("normalised"))
                    if c > 0:
                        add_chunk(src, c - 1, hi, n["normalised"] - 1)
                add_chunk(src, KD - 1, hi, n["normalised"])

            def add_chunk(src, c, hi, count):
                dve.wait_ge(sem("normalised"), count)
                dve.tensor_tensor(X[:, c, 0:hi], X[:, c, 0:hi], src[:, c, 0:hi], ALU.add).then_inc(sem("x_chunk"), one("x_chunk"))

            def add_up(c, a, b, first):
                bank = tile()[:, 0:b - a]
                if first:
                    dve.tensor_copy(Y[:, c, a:b], bank).then_inc(sem("tile_free"), one("tile_free"))
                else:
                    dve.tensor_tensor(Y[:, c, a:b], bank, Y[:, c, a:b], ALU.add).then_inc(sem("tile_free"), one("tile_free"))

            def mlp(segs, beside):
                for step, (kind, g) in enumerate(mlp_steps(len(FF1_GROUPS))):
                    if beside and step in MOD_STEPS:
                        mod(1, 2 * (step - MOD_STEPS[0]), 2 * (step - MOD_STEPS[0]) + 2)
                    for c in range(8):
                        for a, b in segs:
                            if kind == "up":
                                bank = tile()[:, 0:b - a]
                                dve.wait_ge(sem("relu"), more("relu"))
                                hid = hidden1[g % 2][:, c, a:b]
                                dve.tensor_tensor(hid, hid, bank, ALU.mult).then_inc(sem("tile_free"), one("tile_free"))
                            else:
                                add_up(c, a, b, g == 0)

            def swiglu():
                for kind, g in mlp_steps(len(FF2_GROUPS)):
                    for c in range(8 if kind == "down" else FF2_GROUPS[g]):
                        if kind == "up":
                            bank = tile()
                            dve.wait_ge(sem("sigmoid"), more("sigmoid"))
                            hid = hidden2[g % 2][:, c, :]
                            dve.tensor_tensor(hid, bank, sig[:, n["sig"] % 2, :], ALU.mult).then_inc(sem("tile_free"), one("tile_free"))
                            n["sig"] += 1
                            gate = tile()
                            dve.wait_ge(sem("tile_free"), n["tile_free"])
                            dve.tensor_tensor(hid, gate, hid, ALU.mult).then_inc(sem("tile_free"), one("tile_free"))
                        else:
                            add_up(c, 0, LAT, g == 0)

            def half_step():
                if n["tile_free"] > 0:
                    dve.wait_ge(sem("tile_free"), n["tile_free"])
                for c in range(KD):
                    dve.scalar_tensor_tensor(X[:, c, 0:LAT], Y[:, c, 0:LAT], 0.5, X[:, c, 0:LAT], ALU.mult, ALU.add).then_inc(sem("x_chunk"), one("x_chunk"))

            def odd_in():
                def mix_chunk(mu, dest, hi, c):
                    dve.scalar_tensor_tensor(dest[:, c, 0:hi], XX[:, c, 0:hi], vcol(f"mu{mu}", c), H[:, c, 0:hi],
                                             ALU.mult, ALU.add).then_inc(sem("mix"), one("mix"))

                for c in range(KD):
                    dve.wait_ge(sem("h_act"), n["h_act"] - KD + c + 1)
                    for a, b in ((0, LAT), (LAT, TOK)):
                        dve.tensor_tensor(XX[:, c, a + 1:b - 1], H[:, c, a:b - 2], H[:, c, a + 2:b], ALU.add)
                        dve.tensor_copy(XX[:, c, a:a + 1], H[:, c, a + 1:a + 2])
                        ins = dve.tensor_copy(XX[:, c, b - 1:b], H[:, c, b - 2:b - 1])
                    settle(ins)
                    settle(dve.scalar_tensor_tensor(XX[:, c, :], XX[:, c, :], 0.5, H[:, c, :], ALU.mult, ALU.subtract))
                    mix_chunk(1, K, TOK, c)

                def mix(mu, dest, hi):
                    for c in range(KD):
                        mix_chunk(mu, dest, hi, c)

                def raw(dest, segs):
                    for a, b in segs:
                        dve.tensor_copy(dest[:, a:b], tile()[:, 0:b - a]).then_inc(sem("tile_free"), one("tile_free"))

                mix(4, MIX, TOK)
                raw(square[:, 0, :], SEG2)
                mix(5, K, LAT)
                raw(square[:, 1, :], SEG2)
                mix(2, MIX, TOK)
                raw(rstd[:, :], SEG1)
                copies(K, range(8), SEG2)
                mix(3, MIX, TOK)
                dve.wait_ge(sem("mix"), n["mix"])
                mix(0, XX, LAT)
                dve.wait_ge(sem("x_saved"), 16)
                for lo in (C, 0):
                    for c in range(CHUNKS):
                        dve.tensor_copy(V[lo:lo + C, c, :, :].rearrange("p a b -> p (a b)"), tile()[lo:lo + C, :]).then_inc(sem("tile_free"), one("tile_free"))
                dve.wait_ge(sem("mix"), n["mix"])
                copies(R, range(8), SEG1)
                dve.wait_ge(sem("tile_free"), n["tile_free"])
                settle(dve.memset(reset[:, :], 1.0))
                settle(dve.memset(chunked(reset[:, :])[:, :, 0:1], 0.0))

            def half(h):
                return slice(C * h, C * h + C)

            def each_chunk(m, count):
                return m.unsqueeze(1).broadcast_to([m.shape[0], count, m.shape[1]])

            def features(j, i):
                p, d = divmod(j, 2)
                inv, b, kd = chunked(f_inv), chunked(f_a), chunked(f_kd)
                for at_slot, what in FEATURE_SLOTS:
                    if at_slot != i:
                        continue
                    if what == "decay":
                        dve.wait_ge(sem("feature_read"), more("feature_read", 2))
                        line = f_cs if d == 0 else f_cs[:, ::-1]
                        dve.tensor_tensor_scan(line, reset[:, :], line, 0.0, ALU.mult, ALU.add).then_inc(
                            sem("running"), one("running"))
                    elif what == "rate":
                        dve.wait_ge(sem("feature_read"), more("feature_read", 2))
                        settle(dve.tensor_scalar(f_kd, f_a, vcol("ka", p), omka[:, p:p + 1], ALU.mult, ALU.add))
                        settle(dve.tensor_tensor(f_kd, f_kd, K[:, p, :], ALU.mult))
                        if d == 0:
                            settle(dve.tensor_copy(k_sum, f_kd[:, 0:LAT]))
                        else:
                            settle(dve.tensor_tensor(k_sum, k_sum, f_kd[:, 0:LAT], ALU.add))
                        settle(dve.tensor_tensor(f_a, f_kk, f_a, ALU.mult))
                if i == SQUARE_SLOT and d == 0:
                    dve.tensor_scalar(f_kk, K[:, p, :], vcol("kk", p), None, ALU.mult).then_inc(
                        sem("feature_dve"), one("feature_dve"))
                elif i == ROOT_SLOT and d == 0:
                    dve.wait_ge(sem("feature_read"), more("feature_read", 2))
                    dve.tensor_scalar(rstd[:, :], rstd[:, :], 1e-24, None, ALU.max).then_inc(
                        sem("feature_dve"), one("feature_dve"))
                elif i in (ROOT_SLOT + 1, ROOT_SLOT + 2) and d == 0:
                    if i == ROOT_SLOT + 1:
                        dve.wait_ge(sem("key_root"), more("key_root"))
                    a, z = SEG2[i - ROOT_SLOT - 1]
                    settle(dve.reciprocal(rstd[:, a:z], rstd[:, a:z]))
                    settle(dve.tensor_tensor(f_kk[:, a:z], f_kk[:, a:z], rstd[:, a:z], ALU.mult))
                if i == KEY_SLOT:
                    dve.wait_ge(sem("exponents"), more("exponents", 2))
                    for h in range(2):
                        dve.tensor_tensor(bk[half(h), :, h, :], b[half(h)], inv[half(h)], ALU.mult)
                elif i == KEY_SLOT + 1:
                    for h in range(2):
                        ins = dve.tensor_tensor(bk[half(h), :, 1 - h, :], kd[half(h)], inv[half(h)], ALU.mult)
                    ins.then_inc(sem("keys"), one("keys"))
                    dve.wait_ge(sem("keys"), n["keys"])

            def prepare(j, i, b):
                p, d = divmod(j, 2)
                S = sets[d]
                lat = LAT // C
                inc, kk = chunked(f_inc), chunked(f_kk)
                lower = "level" if d == 0 else "level_t"
                if i == 0:
                    to, of = (slice(1, C), slice(0, C - 1)) if d == 0 else (slice(0, C - 1), slice(1, C))
                    e = slice(0, 1) if d == 0 else slice(C - 1, C)
                    last = slice(C - 1, C) if d == 0 else slice(0, 1)
                    for lo, hi in ((0, 4), (4, CHUNKS)):
                        end = min(hi, lat)
                        dve.tensor_tensor(S["kr"][:, lo:hi, 0, to], kk[:, lo:hi, to], inc[:, lo:hi, of], ALU.mult)
                        dve.tensor_copy(S["kr"][:, lo:hi, 0, e], kk[:, lo:hi, e])
                        ins = dve.tensor_tensor(S["kr"][:, lo:end, 1, :], chunked(R[:, p, :])[:, lo:end, :], inc[:, lo:end, :],
                                                ALU.mult)
                        if lo == 0:
                            ins.then_inc(sem("decayed"), one("decayed"))
                    dve.tensor_copy(chunk_decay[:, d, :].unsqueeze(2), inc[:, :, last]).then_inc(
                        sem("decayed"), one("decayed"))
                    dve.wait_ge(sem("decayed"), n["decayed"])
                    if d == 1:
                        settle(dve.scalar_tensor_tensor(R[:, p, :], k_sum, vcol("rk", p), R[:, p, :], ALU.mult, ALU.mult))
                elif 1 <= i <= GRAMS:
                    g = i - 1
                    c = 2 * g
                    dve.wait_ge(sem("gram"), more("gram"))
                    for h in range(2):
                        raw = ps[:, 2 * (g % 2) + h, 0:4 * C].rearrange("p (a b) -> p a b", a=2)
                        if c < lat:
                            dve.tensor_tensor(S["gram"][:, c:c + 2, h, :], raw[:, :, C:2 * C],
                                              each_chunk(ccol("gram_mask", 2 * C * d + C, C), 2), ALU.mult)
                        ins = dve.tensor_tensor(couple[:, h, c:c + 2, :], raw[:, :, 0:C],
                                                each_chunk(ccol("gram_mask", 2 * C * d, C), 2), ALU.mult)
                    ins.then_inc(sem("gram_read"), one("gram_read"))
                elif i == INVERSE - 1 and b == 0:
                    dve.wait_ge(sem("gram_copied"), more("gram_copied", GRAMS))
                    settle(dve.scalar_tensor_tensor(f_x, f_x, -1.0, each_chunk(ccol(lower, 0, C), CHUNKS), ALU.mult, ALU.mult))
                    dve.tensor_tensor(f_x, f_x, each_chunk(ccol("ident2", 0, C), CHUNKS), ALU.add).then_inc(
                        sem("inverse"), one("inverse"))
                    dve.wait_ge(sem("masked"), (GRAMS + LEVELS - 2) * j + GRAMS)
                    dve.tensor_tensor(S["xt"], each_chunk(ccol("ident2", 0, C), CHUNKS), S["xt"], ALU.subtract).then_inc(
                        sem("inverse"), one("inverse"))
                    dve.wait_ge(sem("inverse"), n["inverse"])
                elif i > INVERSE:
                    level, q = divmod(i - INVERSE - 1, 3)
                    chunks = slice(b * HALF, (b + 1) * HALF)
                    if q == 1 and level < LEVELS - 2:
                        dve.wait_ge(sem("second_product"), more("second_product"))
                        settle(dve.tensor_tensor(f_x[:, chunks, :], f_x[:, chunks, :], chunked(ps[:, 2 + b, 0:HALF * C]),
                                                 ALU.subtract))
                    elif q == 2:
                        dve.wait_ge(sem("third_product"), more("third_product"))
                        if level == LEVELS - 2:
                            for h in range(2):
                                of_rows, _, _, to = last_level(d, h)
                                xt = S["xt"][of_rows, chunks, to]
                                raw = ps[of_rows, b, 0:HALF * C // 2].rearrange("p (c t) -> p c t", t=C // 2)
                                ins = dve.tensor_tensor(xt, xt, raw, ALU.subtract)
                            ins.then_inc(sem("inverse"), one("inverse"))
                            dve.wait_ge(sem("inverse"), n["inverse"])
                            return
                        dve.tensor_tensor(S["xt"][:, chunks, :], S["xt"][:, chunks, :], chunked(ps[:, b, 0:HALF * C]),
                                          ALU.subtract).then_inc(sem("inverse"), one("inverse"))
                        dve.wait_ge(sem("inverse"), n["inverse"])

            def state_in(j, s):
                d = j % 2
                S, c = sets[d], chunk_order(d)[s]
                if s == 0:
                    dve.memset(state[:, d, :], 0.0).then_inc(sem("state"), one("state"))
                dve.wait_ge(sem("state"), n["state"])
                dve.tensor_scalar(state_dec[:, d, :], state[:, d, :], chunk_decay[:, d, c:c + 1], None, ALU.mult)
                dve.wait_ge(sem("from_state"), more("from_state"))
                dve.scalar_tensor_tensor(w0_neg[:, d, :], ps[:, 6, 0:C], -1.0, S["bv"][:, c, :], ALU.mult,
                                             ALU.add).then_inc(sem("residual"), one("residual"))

            def state_out(j, s):
                d = j % 2
                S, c = sets[d], chunk_order(d)[s]
                if s < CHUNKS - 1:
                    dve.wait_ge(sem("to_state"), more("to_state"))
                    dve.wait_ge(sem("residual"), n["residual"])
                    dve.scalar_tensor_tensor(state[:, d, :], ps[:, 6, 2 * C:3 * C], chunk_decay[:, d, c:c + 1],
                                                 state_dec[:, d, :], ALU.mult, ALU.add).then_inc(sem("state"), one("state"))
                if c < LAT // C:
                    dve.wait_ge(sem("y"), more("y"))
                    y, raw = y_pair[:, c * C:(c + 1) * C], ps[:, 7, 0:C]
                    if d == 0:
                        dve.tensor_copy(y, raw).then_inc(sem("y_read"), one("y_read"))
                    else:
                        dve.wait_ge(sem("y_read"), n["y_read"])
                        dve.tensor_tensor(y, y, raw, ALU.add).then_inc(sem("y_read"), one("y_read"))

            def readout(p):
                dve.wait_ge(sem("y_read"), n["y_read"])
                dve.tensor_copy(stat[:, 15:16], y_pair[:, 0:1]).then_inc(sem("read_dve"), one("read_dve"))
                dve.wait_ge(sem("read_pe"), more("read_pe"))
                dve.scalar_tensor_tensor(y_pair, ps[:, 0, :], -1.0 / C, y_pair, ALU.mult, ALU.add).then_inc(sem("read_dve"), one("read_dve"))
                n["read_pe"] += 1
                dve.wait_ge(sem("read_act_v"), more("read_act_v"))
                dve.tensor_tensor(v_turned, v_turned, ps[:, 1, :], ALU.mult).then_inc(sem("bonus"), one("bonus"))
                dve.wait_ge(sem("read_pe"), more("read_pe"))
                dve.tensor_scalar(rstd[:, 0:LAT], ps[:, 4, :], 1.0 / C, 64e-5, ALU.mult, ALU.add).then_inc(sem("read_dve"), one("read_dve"))

            def readout_end(p, part):
                if part < 2:
                    if part == 0:
                        dve.wait_ge(sem("read_act_root"), more("read_act_root"))
                    r = rstd[:, part * LAT // 2:(part + 1) * LAT // 2]
                    settle(dve.reciprocal(r, r))
                elif part == 2:
                    settle(dve.scalar_tensor_tensor(y_pair, y_pair, vcol("lng", p), rstd[:, 0:LAT], ALU.mult, ALU.mult))
                elif part == 3:
                    dve.wait_ge(sem("bonus"), n["bonus"])
                    settle(dve.scalar_tensor_tensor(y_pair, y_pair, vcol("lnb", p), v_turned, ALU.add, ALU.add))
                else:
                    dve.wait_ge(sem("gate"), more("gate"))
                    dve.tensor_tensor(R[:, p, :], y_pair, square[:, 0, 0:LAT], ALU.mult).then_inc(sem("r_out"), one("r_out"))

            def tables():
                dve.wait_ge(sem("pos"), 32)
                ang, turns = rope_tmp[:, 0, :], rope_tmp[:, 1, :]
                two_pi = 2 * np.pi
                first = 6.28125
                second = float(np.float32(np.round((two_pi - first) * 2 ** 19) / 2 ** 19))
                third = two_pi - first - second
                magic = 1.5 * 2 ** 23
                settle(dve.tensor_copy(ang, pos_i.bitcast(I32)))
                settle(dve.tensor_scalar(ang, ang, ccol("inv_freq"), None, ALU.mult))
                settle(dve.tensor_scalar(turns, ang, 1.0 / two_pi, magic, ALU.mult, ALU.add))
                settle(dve.tensor_scalar(turns, turns, magic, None, ALU.subtract))
                for part in (first, second, third):
                    settle(dve.scalar_tensor_tensor(ang, turns, -part, ang, ALU.mult, ALU.add))
                dve.tensor_scalar(ang, ang, 3.1415925, -3.1415925, ALU.min, ALU.max).then_inc(sem("angle"), one("angle"))
                dve.wait_ge(sem("sine"), more("sine", 2))
                cos = rope[:, 0, :]
                settle(dve.tensor_tensor(cos, cos, cos, ALU.mult))
                settle(dve.tensor_scalar(cos, cos, -2.0, 1.0, ALU.mult, ALU.add))

            def mix_in(l):
                settle(dve.memset(conv_in[:, :, 0:TAPS - 1], 0.0))
                for c in range(2):
                    dve.tensor_copy(mk2[:, c, :], tile()[:, 0:CTX]).then_inc(sem("tile_free"), one("tile_free"))
                for t in range(2):
                    dve.tensor_copy(mv2[:, t, :], tile()[:, 0:CTX]).then_inc(sem("tile_free"), one("tile_free"))
                for c in range(6):
                    dve.tensor_copy(q2[:, c, :], tile()).then_inc(sem("tile_free"), one("tile_free"))
                gains = ["swa_q_norm"] * 3 + ["swa_k_norm"] + ["mem_q_norm"] * 2 + ["mem_k_norm"] * 2
                for u in range(MIX_TILES):
                    a = conv_in[:, min(u // 2, 2), TAPS - 1:]
                    if u >= 6:
                        dve.tensor_copy(v2[:, u - 6, :], tile()[:, 0:P]).then_inc(sem("tile_free"), one("tile_free"))
                    elif u % 2 == 0:
                        dve.tensor_copy(a, tile()).then_inc(sem("tile_free"), one("tile_free"))
                    else:
                        gate = tile()
                        dve.wait_ge(sem("sigmoid"), more("sigmoid"))
                        dve.wait_ge(sem("tile_free"), n["tile_free"])
                        dve.tensor_tensor(a, a, conv_y[:, u // 2, :], ALU.mult).then_inc(sem("tile_free"), one("tile_free"))
                    if u < 8:
                        hi = LAT if u < 6 else CTX
                        t = q2[:, u, :] if u < 6 else mk2[:, u - 6, :]
                        r = inverse_root(1, 0, hi, 1.0 / C, 1e-6)
                        ins = dve.scalar_tensor_tensor(t, t, vcol(f"{gains[u]}{l}"), r, ALU.mult, ALU.mult)
                        if u < 4:
                            ins.then_inc(sem("normed"), one("normed"))
                            dve.wait_ge(sem("normed"), n["normed"])
                        else:
                            settle(ins)
                    if 1 <= u <= 4:
                        t = q2[:, u - 1, :]
                        dve.wait_ge(sem("rotated"), more("rotated"))
                        dve.tensor_tensor(rope_tmp[:, 0, :], ps[:, 5, :], rope[:, 1, :], ALU.mult).then_inc(
                            sem("rotated_read"), one("rotated_read"))
                        settle(dve.tensor_tensor(t, t, rope[:, 0, :], ALU.mult))
                        settle(dve.tensor_tensor(t, t, rope_tmp[:, 0, :], ALU.add))
                dve.tensor_copy(stat[:, 15:16], q2[:, 0, 0:1]).then_inc(sem("roped"), one("roped"))

            def conv(l):
                dve.wait_ge(sem("tap"), n["tap"])
                dve.wait_ge(sem("pool_tap"), more("pool_tap", (TAPS - 1) * len(POOL_CHANNELS)))
                dve.tensor_copy(stat[:, 15:16], conv_y[:, 0, 0:1]).then_inc(sem("tapped"), one("tapped"))
                dve.wait_ge(sem("summed"), more("summed", 3))
                for c in range(3):
                    dve.scalar_tensor_tensor(conv_y[:, c, :], ps[:, 4, :], -1.0 / 384, conv_y[:, c, :], ALU.mult, ALU.add).then_inc(sem("centred"), one("centred"))
                dve.wait_ge(sem("centred"), n["centred"])
                dve.tensor_copy(stat[:, 14:15], conv_y[:, 0, 0:1]).then_inc(sem("var"), one("var"))
                r = inverse_root(3, 0, LAT, 1.0 / 384, 1e-6)
                for c in range(3):
                    settle(dve.scalar_tensor_tensor(conv_y[:, c, :], conv_y[:, c, :], vcol(f"conv_ln_g{l}", c), r, ALU.mult,
                                                    ALU.mult))
                for c in range(3):
                    dve.tensor_scalar(conv_y[:, c, :], conv_y[:, c, :], vcol(f"conv_ln_b{l}", c), None, ALU.add).then_inc(sem("conv_z"), one("conv_z"))
                for c in range(3):
                    dve.wait_ge(sem("conv_sigmoid"), more("conv_sigmoid"))
                    s = sig[:, c, :] if c < 2 else rstd[:, 0:LAT]
                    ins = dve.tensor_tensor(Y[:, c, 0:LAT], conv_y[:, c, :], s, ALU.mult)
                ins.then_inc(sem("convolved"), one("convolved"))

            skip = lambda *a: None
            model(dict(load=load, mod=mod, gains=gains, norm_mod=norm_mod, even_in=even_in, attention=attention,
                       project=project, post=post, mlp=mlp, odd_in=odd_in, features=features, prepare=prepare, state_in=state_in, solve=skip,
                       state_out=state_out, readout=readout, readout_end=readout_end, odd_out=skip, tables=tables, norm_vec=norm_vec,
                       swiglu=swiglu, half_step=half_step, mix_in=mix_in, conv=conv, store=skip))


def kernel(**inputs):
    import numpy as _np
    import concourse.bacc as _bacc
    from concourse import mybir as _mybir
    from concourse.bass_utils import run_bass_kernel_spmd as _run

    a = {k: _np.asarray(v) for k, v in inputs.items()}

    def features(x):
        return x.reshape(-1, KD, P).transpose(2, 1, 0)

    arrays = dict(
        panels=pack_panels(a), vecs=pack_vectors(a), consts=pack_constants(),
        x_in=features(_np.concatenate([a["x"][0], a["ctx"][0]], 0)),
        c_in=features(_np.stack([a["c"][0], a["c_ctx"]], 0)),
        mem_in=features(a["mem_2"][0]),
        pool_w=a["ev_pool_w"][0].transpose(1, 0, 2),
        bias=pack_bias(a["ev_rpb"][0]),
        pos=_np.repeat(a["positions_2"].astype(_np.int32).reshape(1, LAT), P, 0),
        window=pack_window(),
    )
    arrays = {f"in_{k}": _np.ascontiguousarray(v) for k, v in arrays.items()}
    nc = _bacc.Bacc("TRN2", target_bir_lowering=False, num_devices=1)
    args = [nc.dram_tensor(k, v.shape, _mybir.dt.from_np(v.dtype), kind="ExternalInput").ap() for k, v in arrays.items()]
    out = nc.dram_tensor("out_x", (P, KD, LAT), F32, kind="ExternalOutput").ap()
    x_save = nc.dram_tensor("x_save", (P, KD, LAT), F32, kind="Internal").ap()
    build_program(nc, *args, out, x_save)
    r = _run(nc, [arrays], core_ids=[0])
    return _np.ascontiguousarray(r.results[0]["out_x"].transpose(2, 1, 0)).reshape(1, LAT, D)
```
